# Optimizing a Trainium2 kernel written in Bass

```python
import math
import jax
import jax.numpy as jnp
from jax import lax
import numpy as np
import jax, jax.numpy as jnp

D_MODEL = 1024
BATCH = 1
SEQ = 256
DEPTH = 2

GRID_W = 64
CTX_LEN = 256

N_MIXERS = 2
D_FF = 4 * D_MODEL
N_MOD = 6
NORM_EPS = 1e-6

MLA_HEADS = 8
MLA_NOPE = 128
MLA_ROPE = 64
MLA_V = 128
MLA_Q_RANK = 384
MLA_KV_RANK = 256
ROPE_BASE = 10000.0
Q_BLOCK = 128

GLA_HEADS = 4
GLA_DK = D_MODEL // 2 // GLA_HEADS
GLA_DV = D_MODEL // GLA_HEADS
GLA_GATE_RANK = 16
GLA_TAU = 16.0
GLA_CHUNK = 64


def rms_norm(x, g):
    xf = x.astype(jnp.float32)
    y = xf * lax.rsqrt(jnp.mean(xf * xf, axis=-1, keepdims=True) + NORM_EPS)
    return (y * g.astype(jnp.float32)).astype(x.dtype)

def modulate(h, shift, scale):
    return h * (1.0 + scale) + shift

def sqrelu_mlp(h, w1, w2):
    return jnp.square(jax.nn.relu(h @ w1)) @ w2

def axial_rope_tables(n_tokens):
    rows = n_tokens // GRID_W
    row = jnp.repeat(jnp.arange(rows, dtype=jnp.float32), GRID_W)
    col = jnp.tile(jnp.arange(GRID_W, dtype=jnp.float32), rows)
    half = MLA_ROPE // 2
    inv_freq = ROPE_BASE ** (-jnp.arange(0, half, 2, dtype=jnp.float32) / half)
    ang_r = row[:, None] * inv_freq
    ang_c = col[:, None] * inv_freq
    return (jnp.cos(ang_r), jnp.sin(ang_r), jnp.cos(ang_c), jnp.sin(ang_c))

def _rotate_half(x, cos, sin):
    x1, x2 = jnp.split(x, 2, axis=-1)
    return jnp.concatenate([x1 * cos - x2 * sin, x1 * sin + x2 * cos], axis=-1)

def apply_axial_rope(x, rope):
    cos_r, sin_r, cos_c, sin_c = rope
    if x.ndim == 4:
        cos_r, sin_r, cos_c, sin_c = (t[:, None, :] for t in rope)
    x_r, x_c = jnp.split(x, 2, axis=-1)
    out = jnp.concatenate([_rotate_half(x_r, cos_r, sin_r), _rotate_half(x_c, cos_c, sin_c)], axis=-1)
    return out.astype(x.dtype)

def mla_attend(q_nope, q_rope, k_nope, k_rope, v):
    scale = (MLA_NOPE + MLA_ROPE) ** -0.5
    s = (jnp.einsum('bqhd,bkhd->bhqk', q_nope, k_nope, preferred_element_type=jnp.float32)
         + jnp.einsum('bqhr,bkr->bhqk', q_rope, k_rope, preferred_element_type=jnp.float32))
    p = jax.nn.softmax(s * scale, axis=-1)
    return jnp.einsum('bhqk,bkhd->bqhd', p.astype(v.dtype), v)

def mla_mixer(h_ctx, h_lat, rope, need_ctx, w_dq, g_q, w_uq, w_dkv, g_kv, w_ukv, w_o):
    B, C, _ = h_ctx.shape
    S = h_lat.shape[1]
    T = C + S
    h_all = jnp.concatenate([h_ctx, h_lat], axis=1)
    cq = rms_norm(h_all @ w_dq, g_q)
    q = (cq @ w_uq).reshape(B, T, MLA_HEADS, MLA_NOPE + MLA_ROPE)
    ckv = h_all @ w_dkv
    c_kv = rms_norm(ckv[..., :MLA_KV_RANK], g_kv)
    kv = (c_kv @ w_ukv).reshape(B, T, MLA_HEADS, MLA_NOPE + MLA_V)
    q_nope, q_rope = q[..., :MLA_NOPE], q[..., MLA_NOPE:]
    k_nope, v = kv[..., :MLA_NOPE], kv[..., MLA_NOPE:]
    k_rope = ckv[..., MLA_KV_RANK:]
    q_rope = jnp.concatenate([q_rope[:, :C], apply_axial_rope(q_rope[:, C:], rope)], axis=1)
    k_rope = jnp.concatenate([k_rope[:, :C], apply_axial_rope(k_rope[:, C:], rope)], axis=1)

    nb = S // Q_BLOCK
    def to_blocks(a):
        return jnp.moveaxis(a.reshape(B, nb, Q_BLOCK, *a.shape[2:]), 1, 0)
    qn_blk = to_blocks(q_nope[:, C:])
    qr_blk = to_blocks(q_rope[:, C:])
    o_lat = lax.map(lambda qb: mla_attend(qb[0], qb[1], k_nope, k_rope, v), (qn_blk, qr_blk))
    o_lat = jnp.moveaxis(o_lat, 0, 1).reshape(B, S, MLA_HEADS * MLA_V)
    y_lat = o_lat @ w_o

    y_ctx = None
    if need_ctx:
        o_ctx = mla_attend(q_nope[:, :C], q_rope[:, :C], k_nope[:, :C], k_rope[:, :C], v[:, :C])
        y_ctx = o_ctx.reshape(B, C, MLA_HEADS * MLA_V) @ w_o
    return y_ctx, y_lat

def gla_log_gate(h, w1, w2, b):
    return jax.nn.log_sigmoid(((h @ w1) @ w2 + b).astype(jnp.float32)) / GLA_TAU

def gla_chunk_scan(q, k, v, g, s0):
    B, T, H, _ = q.shape
    n = T // GLA_CHUNK
    def to_chunks(a):
        return a.reshape(B, n, GLA_CHUNK, H, a.shape[-1]).transpose(1, 0, 3, 2, 4).astype(jnp.float32)
    mask = jnp.tril(jnp.ones((GLA_CHUNK, GLA_CHUNK), dtype=bool))
    def step(s, inp):
        qc, kc, vc, gc = inp
        G = jnp.cumsum(gc, axis=2)
        G_last = G[:, :, -1:, :]
        q_t = qc * jnp.exp(G)
        k_t = kc * jnp.exp(-G)
        a = jnp.where(mask, jnp.einsum('bhid,bhjd->bhij', q_t, k_t), 0.0)
        o = jnp.einsum('bhij,bhjv->bhiv', a, vc) + jnp.einsum('bhid,bhdv->bhiv', q_t, s)
        k_end = kc * jnp.exp(G_last - G)
        s_new = jnp.exp(G_last[:, :, 0, :])[..., None] * s + jnp.einsum('bhjd,bhjv->bhdv', k_end, vc)
        return s_new, o
    s_fin, o = lax.scan(step, s0, (to_chunks(q), to_chunks(k), to_chunks(v), to_chunks(g)))
    o = o.transpose(1, 0, 3, 2, 4).reshape(B, T, H, v.shape[-1])
    return o, s_fin

def gla_mixer(h_ctx, h_lat, need_ctx, w_q, w_k, w_v, w_r, w_gate1, w_gate2, b_gate, g_o, w_o):
    B, C, _ = h_ctx.shape
    S = h_lat.shape[1]
    T = C + S
    h_all = jnp.concatenate([h_ctx, h_lat], axis=1)
    def heads(a, d):
        return a.reshape(B, T, GLA_HEADS, d)
    q = heads(h_all @ w_q, GLA_DK) * (GLA_DK ** -0.5)
    k = heads(h_all @ w_k, GLA_DK)
    v = heads(h_all @ w_v, GLA_DV)
    g_fwd = heads(gla_log_gate(h_all, w_gate1[0], w_gate2[0], b_gate[0]), GLA_DK)
    g_bwd = heads(gla_log_gate(h_all, w_gate1[1], w_gate2[1], b_gate[1]), GLA_DK)
    flip = lambda a: jnp.flip(a, axis=1)
    zeros = jnp.zeros((B, GLA_HEADS, GLA_DK, GLA_DV), jnp.float32)
    qc, kc, vc = q[:, :C], k[:, :C], v[:, :C]
    ql, kl, vl = q[:, C:], k[:, C:], v[:, C:]
    o_cf, s_cf = gla_chunk_scan(qc, kc, vc, g_fwd[:, :C], zeros)
    o_cb, s_cb = gla_chunk_scan(flip(qc), flip(kc), flip(vc), flip(g_bwd[:, :C]), zeros)
    o_lf, _ = gla_chunk_scan(ql, kl, vl, g_fwd[:, C:], s_cf)
    o_lb, _ = gla_chunk_scan(flip(ql), flip(kl), flip(vl), flip(g_bwd[:, C:]), s_cb)
    def out(o, h):
        y = rms_norm(o, g_o).astype(h.dtype).reshape(B, -1, GLA_HEADS * GLA_DV)
        return (y * jax.nn.silu(h @ w_r)) @ w_o
    y_lat = out(o_lf + flip(o_lb), h_lat)
    y_ctx = out(o_cf + flip(o_cb), h_ctx) if need_ctx else None
    return y_ctx, y_lat

def first_inputs(seed: int = 0) -> dict:
    key = jax.random.key(seed)
    ks = jax.random.split(key, 32)
    D = D_MODEL
    n_a = (DEPTH + N_MIXERS - 1) // N_MIXERS
    n_b = DEPTH // N_MIXERS
    def nrm(k, shape, scale):
        return jax.random.normal(k, shape, jnp.float32) * scale
    return {
        'x': nrm(ks[0], (BATCH, SEQ, D), 1.0),
        'c': nrm(ks[1], (BATCH, D), 1.0),
        'ctx': nrm(ks[2], (BATCH, CTX_LEN, D), 1.0),
        'c_ctx': nrm(ks[3], (D,), 1.0),
        'ada_w': nrm(ks[4], (DEPTH, D, N_MOD * D), 0.5 * D ** -0.5),
        'ada_b': nrm(ks[5], (DEPTH, N_MOD * D), 0.02),
        'norm_g': 1.0 + nrm(ks[6], (DEPTH, 4, D), 0.02),
        'mlp_w1': nrm(ks[7], (DEPTH, D, D_FF), D ** -0.5),
        'mlp_w2': nrm(ks[8], (DEPTH, D_FF, D), D_FF ** -0.5),
        'mla_w_dq': nrm(ks[9], (n_a, D, MLA_Q_RANK), D ** -0.5),
        'mla_g_q': 1.0 + nrm(ks[10], (n_a, MLA_Q_RANK), 0.02),
        'mla_w_uq': nrm(ks[11], (n_a, MLA_Q_RANK, MLA_HEADS * (MLA_NOPE + MLA_ROPE)), MLA_Q_RANK ** -0.5),
        'mla_w_dkv': nrm(ks[12], (n_a, D, MLA_KV_RANK + MLA_ROPE), D ** -0.5),
        'mla_g_kv': 1.0 + nrm(ks[13], (n_a, MLA_KV_RANK), 0.02),
        'mla_w_ukv': nrm(ks[14], (n_a, MLA_KV_RANK, MLA_HEADS * (MLA_NOPE + MLA_V)), MLA_KV_RANK ** -0.5),
        'mla_w_o': nrm(ks[15], (n_a, MLA_HEADS * MLA_V, D), (MLA_HEADS * MLA_V) ** -0.5),
        'gla_w_q': nrm(ks[16], (n_b, D, GLA_HEADS * GLA_DK), D ** -0.5),
        'gla_w_k': nrm(ks[17], (n_b, D, GLA_HEADS * GLA_DK), D ** -0.5),
        'gla_w_v': nrm(ks[18], (n_b, D, GLA_HEADS * GLA_DV), D ** -0.5),
        'gla_w_r': nrm(ks[19], (n_b, D, GLA_HEADS * GLA_DV), D ** -0.5),
        'gla_w_gate1': nrm(ks[20], (n_b, 2, D, GLA_GATE_RANK), D ** -0.5),
        'gla_w_gate2': nrm(ks[21], (n_b, 2, GLA_GATE_RANK, GLA_HEADS * GLA_DK), GLA_GATE_RANK ** -0.5),
        'gla_b_gate': nrm(ks[22], (n_b, 2, GLA_HEADS * GLA_DK), 0.1),
        'gla_g_o': 1.0 + nrm(ks[23], (n_b, GLA_DV), 0.02),
        'gla_w_o': nrm(ks[24], (n_b, GLA_HEADS * GLA_DV, D), (GLA_HEADS * GLA_DV) ** -0.5),
    }

def first_block(x, c, ctx, c_ctx, ada_w, ada_b, norm_g, mlp_w1, mlp_w2,
              mla_w_dq, mla_g_q, mla_w_uq, mla_w_dkv, mla_g_kv, mla_w_ukv, mla_w_o,
              gla_w_q, gla_w_k, gla_w_v, gla_w_r, gla_w_gate1, gla_w_gate2, gla_b_gate,
              gla_g_o, gla_w_o):
    B, S, D = x.shape
    rope = axial_rope_tables(S)
    silu_c = jax.nn.silu(c)
    silu_cc = jax.nn.silu(c_ctx)
    x_lat, x_ctx = x, ctx
    for i in range(DEPTH):
        need_ctx = i < DEPTH - 1
        j = i // N_MIXERS
        m_lat = (silu_c @ ada_w[i] + ada_b[i]).reshape(B, N_MOD, 1, D)
        m_ctx = (silu_cc @ ada_w[i] + ada_b[i]).reshape(N_MOD, D)
        h_lat = modulate(rms_norm(x_lat, norm_g[i, 0]), m_lat[:, 0], m_lat[:, 1])
        h_ctx = modulate(rms_norm(x_ctx, norm_g[i, 0]), m_ctx[0], m_ctx[1])
        if i % N_MIXERS == 0:
            y_ctx, y_lat = mla_mixer(h_ctx, h_lat, rope, need_ctx, mla_w_dq[j], mla_g_q[j], mla_w_uq[j],
                                     mla_w_dkv[j], mla_g_kv[j], mla_w_ukv[j], mla_w_o[j])
        else:
            y_ctx, y_lat = gla_mixer(h_ctx, h_lat, need_ctx, gla_w_q[j], gla_w_k[j], gla_w_v[j], gla_w_r[j],
                                     gla_w_gate1[j], gla_w_gate2[j], gla_b_gate[j], gla_g_o[j], gla_w_o[j])
        x_lat = x_lat + m_lat[:, 2] * rms_norm(y_lat, norm_g[i, 1])
        h = modulate(rms_norm(x_lat, norm_g[i, 2]), m_lat[:, 3], m_lat[:, 4])
        x_lat = x_lat + m_lat[:, 5] * rms_norm(sqrelu_mlp(h, mlp_w1[i], mlp_w2[i]), norm_g[i, 3])
        if need_ctx:
            x_ctx = x_ctx + m_ctx[2] * rms_norm(y_ctx, norm_g[i, 1])
            h = modulate(rms_norm(x_ctx, norm_g[i, 2]), m_ctx[3], m_ctx[4])
            x_ctx = x_ctx + m_ctx[5] * rms_norm(sqrelu_mlp(h, mlp_w1[i], mlp_w2[i]), norm_g[i, 3])
    return x_lat


D_FF_2 = 4 * D_MODEL
CONV_W = 3
ML_HEADS = 8
ML_DV = D_MODEL // ML_HEADS
ML_DQK = ML_DV // 2
ML_QK_COLS = 2 * ML_HEADS * ML_DQK
ML_QKV_COLS = ML_QK_COLS + ML_HEADS * ML_DV
ML_PROJ_COLS = ML_QKV_COLS + ML_HEADS * ML_DV
ML_CHUNK = 128
EPS = 1e-6
N_CONV_LAYERS = (DEPTH + N_MIXERS - 1) // N_MIXERS
N_MLSTM_LAYERS = DEPTH // N_MIXERS


def _rmsnorm(x, w):
    x32 = x.astype(jnp.float32)
    y = x32 * lax.rsqrt(jnp.mean(x32 * x32, axis=-1, keepdims=True) + EPS)
    return y.astype(x.dtype) * w

def _modulate(h, shift, scale):
    return h * (1 + scale) + shift

def _dwconv_centred(u, w, axis):
    n = u.shape[axis]
    half = CONV_W // 2
    pad = [(0, 0)] * u.ndim
    pad[axis] = (half, CONV_W - 1 - half)
    up = jnp.pad(u, pad)
    out = w[0] * lax.slice_in_dim(up, 0, n, axis=axis)
    for j in range(1, CONV_W):
        out = out + w[j] * lax.slice_in_dim(up, j, j + n, axis=axis)
    return out

def _short_conv_mixer(h, w_in, conv_w, w_out, rows):
    bsz, t_len, d = h.shape
    b_gate, c_gate, u = jnp.split(h @ w_in, 3, axis=-1)
    u = c_gate * u
    if rows is None:
        y = _dwconv_centred(u, conv_w, axis=1)
    else:
        y = _dwconv_centred(u.reshape(bsz, rows, GRID_W, d), conv_w, axis=2).reshape(bsz, t_len, d)
    return (b_gate * y) @ w_out

def _sqrelu_mlp(h, w1, w2):
    return jnp.square(jax.nn.relu(h @ w1)) @ w2

def _mlstm_inputs(h, w_qkvo, w_if, b_if, with_o):
    bsz, t_len, _ = h.shape
    p = h @ (w_qkvo if with_o else w_qkvo[:, :ML_QKV_COLS])
    q = p[..., :ML_HEADS * ML_DQK]
    k = p[..., ML_HEADS * ML_DQK:ML_QK_COLS]
    v = p[..., ML_QK_COLS:ML_QKV_COLS]
    o = p[..., ML_QKV_COLS:] if with_o else None

    def heads(a, dh):
        return a.reshape(bsz, t_len, ML_HEADS, dh).transpose(0, 2, 1, 3).astype(jnp.float32)

    q = heads(q, ML_DQK) * (ML_DQK ** -0.5)
    k = heads(k, ML_DQK)
    v = heads(v, ML_DV)
    g = (jnp.einsum('btd,rdg->rbgt', h, w_if) + b_if[:, None, :, None]).astype(jnp.float32)
    ig = g[:, :, :ML_HEADS]
    lf = jax.nn.log_sigmoid(g[:, :, ML_HEADS:])
    return q, k, v, o, ig, lf

def _mlstm_scan(q, k, v, ig, lf, state, with_output):
    bsz, nh, t_len, _ = q.shape
    dv = v.shape[-1]
    nc = t_len // ML_CHUNK

    def chunks(a):
        a = a.reshape(a.shape[:2] + (nc, ML_CHUNK) + a.shape[3:])
        return jnp.moveaxis(a, 2, 0)

    xs = (chunks(q), chunks(k), chunks(v), chunks(ig), chunks(lf))
    tri = jnp.tril(jnp.ones((ML_CHUNK, ML_CHUNK), dtype=bool))

    def body(carry, inp):
        c_mat, n_vec, m = carry
        qc, kc, vc, ic, fc = inp
        b = jnp.cumsum(fc, axis=-1)
        out = None
        if with_output:
            logd = b[..., :, None] - b[..., None, :] + ic[..., None, :]
            logd = jnp.where(tri, logd, -jnp.inf)
            inter = b + m[..., None]
            m_t = jnp.maximum(inter, jnp.max(logd, axis=-1))
            s = jnp.einsum('bhtd,bhsd->bhts', qc, kc) * jnp.exp(logd - m_t[..., None])
            w_inter = jnp.exp(inter - m_t)
            num = jnp.einsum('bhts,bhsv->bhtv', s, vc) + w_inter[..., None] * jnp.einsum('bhtd,bhdv->bhtv', qc, c_mat)
            den = jnp.sum(s, axis=-1) + w_inter * jnp.einsum('bhtd,bhd->bht', qc, n_vec)
            out = num / jnp.maximum(jnp.abs(den), jnp.exp(-m_t))[..., None]
        b_last = b[..., -1]
        dec = b_last[..., None] - b + ic
        m_new = jnp.maximum(b_last + m, jnp.max(dec, axis=-1))
        wk = jnp.exp(dec - m_new[..., None])
        a = jnp.exp(b_last + m - m_new)
        c_new = a[..., None, None] * c_mat + jnp.einsum('bhsd,bhsv->bhdv', kc * wk[..., None], vc)
        n_new = a[..., None] * n_vec + jnp.einsum('bhs,bhsd->bhd', wk, kc)
        return (c_new, n_new, m_new), out

    state, hs = lax.scan(body, state, xs)
    if with_output:
        hs = jnp.moveaxis(hs, 0, 2).reshape(bsz, nh, t_len, dv)
    return hs, state

def _mlstm_readout(h, o, norm_w, w_out):
    bsz, nh, t_len, dv = h.shape
    h = h.transpose(0, 2, 1, 3)
    h = h * lax.rsqrt(jnp.mean(h * h, axis=-1, keepdims=True) + EPS)
    h = h.reshape(bsz, t_len, nh * dv).astype(o.dtype) * norm_w
    return (jax.nn.sigmoid(o) * h) @ w_out

def _mlstm_mixer(hx, hc, w_qkvo, w_if, b_if, norm_w, w_out, ctx_out):
    qx, kx, vx, ox, igx, lfx = _mlstm_inputs(hx, w_qkvo, w_if, b_if, True)
    qc, kc, vc, oc, igc, lfc = _mlstm_inputs(hc, w_qkvo, w_if, b_if, ctx_out)
    bsz = hx.shape[0]
    zero = (jnp.zeros((bsz, ML_HEADS, ML_DQK, ML_DV), jnp.float32),
            jnp.zeros((bsz, ML_HEADS, ML_DQK), jnp.float32),
            jnp.zeros((bsz, ML_HEADS), jnp.float32))
    hx_sum = 0.0
    hc_sum = 0.0
    for r in range(2):
        if r == 0:
            flip = lambda a: a
        else:
            flip = lambda a: jnp.flip(a, axis=2)
        hc_r, st = _mlstm_scan(flip(qc), flip(kc), flip(vc), flip(igc[r]), flip(lfc[r]), zero, ctx_out)
        hx_r, _ = _mlstm_scan(flip(qx), flip(kx), flip(vx), flip(igx[r]), flip(lfx[r]), st, True)
        hx_sum = hx_sum + flip(hx_r)
        if ctx_out:
            hc_sum = hc_sum + flip(hc_r)
    yx = _mlstm_readout(hx_sum, ox, norm_w, w_out)
    yc = _mlstm_readout(hc_sum, oc, norm_w, w_out) if ctx_out else None
    return yx, yc

def second_inputs(seed: int = 0) -> dict:
    key = jax.random.key(seed)
    ks = jax.random.split(key, 20)
    f32 = jnp.float32

    def nrm(k, shape, fan_in):
        return jax.random.normal(k, shape, f32) * (fan_in ** -0.5)

    x = jax.random.normal(ks[0], (BATCH, SEQ, D_MODEL), f32)
    c = jax.random.normal(ks[1], (BATCH, D_MODEL), f32)
    ctx = jax.random.normal(ks[2], (BATCH, CTX_LEN, D_MODEL), f32)
    c_ctx = jax.random.normal(ks[3], (D_MODEL,), f32)
    norm_w = 1.0 + 0.02 * jax.random.normal(ks[4], (DEPTH, 4, D_MODEL), f32)
    mod_w = nrm(ks[5], (DEPTH, D_MODEL, 6 * D_MODEL), D_MODEL)
    mod_b = 0.01 * jax.random.normal(ks[6], (DEPTH, 6 * D_MODEL), f32)
    mlp_w1 = nrm(ks[7], (DEPTH, D_MODEL, D_FF_2), D_MODEL)
    mlp_w2 = nrm(ks[8], (DEPTH, D_FF_2, D_MODEL), D_FF_2)
    conv_w_in = nrm(ks[9], (N_CONV_LAYERS, D_MODEL, 3 * D_MODEL), D_MODEL)
    conv_w = nrm(ks[10], (N_CONV_LAYERS, CONV_W, D_MODEL), CONV_W)
    conv_w_out = nrm(ks[11], (N_CONV_LAYERS, D_MODEL, D_MODEL), D_MODEL)
    ml_w_qkvo = nrm(ks[12], (N_MLSTM_LAYERS, D_MODEL, ML_PROJ_COLS), D_MODEL)
    ml_w_if = nrm(ks[13], (N_MLSTM_LAYERS, 2, D_MODEL, 2 * ML_HEADS), D_MODEL)
    ig_b = 0.1 * jax.random.normal(ks[14], (N_MLSTM_LAYERS, 2, ML_HEADS), f32)
    fg_b = jnp.linspace(3.0, 6.0, ML_HEADS, dtype=f32) + 0.1 * jax.random.normal(ks[15], (N_MLSTM_LAYERS, 2, ML_HEADS), f32)
    ml_b_if = jnp.concatenate([ig_b, fg_b], axis=-1)
    ml_norm_w = 1.0 + 0.02 * jax.random.normal(ks[16], (N_MLSTM_LAYERS, ML_HEADS * ML_DV), f32)
    ml_w_out = nrm(ks[17], (N_MLSTM_LAYERS, ML_HEADS * ML_DV, D_MODEL), ML_HEADS * ML_DV)
    return {'x': x, 'c': c, 'ctx': ctx, 'c_ctx': c_ctx, 'norm_w': norm_w, 'mod_w': mod_w, 'mod_b': mod_b,
            'mlp_w1': mlp_w1, 'mlp_w2': mlp_w2, 'conv_w_in': conv_w_in, 'conv_w': conv_w,
            'conv_w_out': conv_w_out, 'ml_w_qkvo': ml_w_qkvo, 'ml_w_if': ml_w_if, 'ml_b_if': ml_b_if,
            'ml_norm_w': ml_norm_w, 'ml_w_out': ml_w_out}

def second_block(x, c, ctx, c_ctx, norm_w, mod_w, mod_b, mlp_w1, mlp_w2, conv_w_in, conv_w, conv_w_out,
              ml_w_qkvo, ml_w_if, ml_b_if, ml_norm_w, ml_w_out):
    rows = x.shape[1] // GRID_W
    silu_c = jax.nn.silu(c)[:, None, :]
    silu_cc = jax.nn.silu(c_ctx)
    cx = ctx
    for i in range(DEPTH):
        last = i == DEPTH - 1
        kind = i % N_MIXERS
        j = i // N_MIXERS
        nw = norm_w[i]
        mx = jnp.split(silu_c @ mod_w[i] + mod_b[i], 6, axis=-1)
        hx = _modulate(_rmsnorm(x, nw[0]), mx[0], mx[1])
        need_ctx = (not last) or kind == 1
        if need_ctx:
            mc = jnp.split(silu_cc @ mod_w[i] + mod_b[i], 6, axis=-1)
            hc = _modulate(_rmsnorm(cx, nw[0]), mc[0], mc[1])
        if kind == 0:
            yx = _short_conv_mixer(hx, conv_w_in[j], conv_w[j], conv_w_out[j], rows)
            yc = _short_conv_mixer(hc, conv_w_in[j], conv_w[j], conv_w_out[j], None) if not last else None
        else:
            yx, yc = _mlstm_mixer(hx, hc, ml_w_qkvo[j], ml_w_if[j], ml_b_if[j], ml_norm_w[j], ml_w_out[j],
                                  not last)
        x = x + mx[2] * _rmsnorm(yx, nw[1])
        x = x + mx[5] * _rmsnorm(_sqrelu_mlp(_modulate(_rmsnorm(x, nw[2]), mx[3], mx[4]), mlp_w1[i], mlp_w2[i]), nw[3])
        if not last:
            cx = cx + mc[2] * _rmsnorm(yc, nw[1])
            cx = cx + mc[5] * _rmsnorm(_sqrelu_mlp(_modulate(_rmsnorm(cx, nw[2]), mc[3], mc[4]), mlp_w1[i], mlp_w2[i]), nw[3])
    return x


def setup_inputs(seed=0):
    out = dict(first_inputs(seed))
    for name, value in second_inputs(seed + 1).items():
        if name != "x":
            out[name + "_2"] = value
    return out


def reference(
    x, c, ctx, c_ctx, ada_w, ada_b, norm_g, mlp_w1, mlp_w2, mla_w_dq, mla_g_q, mla_w_uq,
    mla_w_dkv, mla_g_kv, mla_w_ukv, mla_w_o, gla_w_q, gla_w_k, gla_w_v, gla_w_r, gla_w_gate1,
    gla_w_gate2, gla_b_gate, gla_g_o, gla_w_o, c_2, ctx_2, c_ctx_2, norm_w_2, mod_w_2, mod_b_2,
    mlp_w1_2, mlp_w2_2, conv_w_in_2, conv_w_2, conv_w_out_2, ml_w_qkvo_2, ml_w_if_2, ml_b_if_2,
    ml_norm_w_2, ml_w_out_2,
):
    x = first_block(
        x, c, ctx, c_ctx, ada_w, ada_b, norm_g, mlp_w1, mlp_w2, mla_w_dq, mla_g_q, mla_w_uq,
        mla_w_dkv, mla_g_kv, mla_w_ukv, mla_w_o, gla_w_q, gla_w_k, gla_w_v, gla_w_r,
        gla_w_gate1, gla_w_gate2, gla_b_gate, gla_g_o, gla_w_o,
    )
    return second_block(
        x, c_2, ctx_2, c_ctx_2, norm_w_2, mod_w_2, mod_b_2, mlp_w1_2, mlp_w2_2, conv_w_in_2,
        conv_w_2, conv_w_out_2, ml_w_qkvo_2, ml_w_if_2, ml_b_if_2, ml_norm_w_2, ml_w_out_2,
    )


_drawn_inputs = setup_inputs


def setup_inputs(seed=0):
    import zlib

    import numpy as np

    out = dict(_drawn_inputs(seed))
    spreads = {}
    factors = {'mla_g_q': 8.0,
     'mla_g_kv': 3.829,
     'gla_g_o': 46.477,
     'ml_norm_w_2': 50.682,
     'gla_b_gate': 3.088}
    for name, (base, spread) in spreads.items():
        noise = np.random.default_rng([zlib.crc32(name.encode()), seed]).standard_normal(out[name].shape)
        drawn = base * np.exp(spread * noise) if base else spread * noise
        out[name] = jnp.asarray(drawn.astype(out[name].dtype))
    for name, factor in factors.items():
        out[name] = (out[name] * factor).astype(out[name].dtype)
    return out
```

```python
from contextlib import ExitStack

import numpy as np

import concourse.bass as bass
from concourse import mybir

F32 = mybir.dt.float32
F32R = mybir.dt.float32r
I32 = mybir.dt.int32
ALU = mybir.AluOpType
ACT = mybir.ActivationFunctionType
AX = mybir.AxisListType

D = 1024
FF = 4096
EPS = 1e-6
NRAW = 3
NSPL = 4
NADA = 3
NTMP = 3

CONST_SLICES = {}


def const_table():
    parts = []
    at = [0]

    def add(name, a):
        full = np.zeros((128, a.shape[1]), np.float32)
        full[:a.shape[0]] = a
        CONST_SLICES[name] = (at[0], a.shape[1])
        at[0] += a.shape[1]
        parts.append(full)

    j = np.arange(128)[:, None]
    i = np.arange(128)[None, :]
    same = (j // 64) == (i // 64)
    add("ident", np.eye(128, dtype=np.float32))
    add("ones", np.ones((128, 128), np.float32))
    s = 1.0 / 16.0
    add("cum", np.concatenate([(same & (j <= i)) * s, (same & (j >= i)) * s], 1).astype(np.float32))
    add("end", np.concatenate([(same & (j > i)) * s, (same & (j < i)) * s], 1).astype(np.float32))
    add("endc", np.concatenate([(j > i) * s, (j < i) * s], 1).astype(np.float32))
    add("sum", np.full((128, 128), s, np.float32))
    add("gmask", np.concatenate([same & (j <= i), same & (j >= i)], 1).astype(np.float32))
    t = np.arange(256)[None, :]
    p = np.arange(128)[:, None]
    neg = np.float32(-1e30)
    mf = [np.where(p + 128 * q <= t, np.float32(0), neg) for q in range(2)]
    mb = [np.where(p + 128 * q >= t, np.float32(0), neg) for q in range(2)]
    add("mmask", np.concatenate(mf + mb, 1).astype(np.float32))
    sel = np.zeros((8, 8, 128), np.float32)
    for h in range(8):
        sel[h, h, :] = 1.0
    add("sel", sel.reshape(8, 1024))
    rot = np.zeros((64, 64), np.float32)
    for base in (0, 32):
        for q in range(16):
            rot[base + q + 16, base + q] = -1.0
            rot[base + q, base + q + 16] = 1.0
    add("rot", rot)
    half = 32
    inv = (np.float32(10000.0) ** (-np.arange(0, half, 2, dtype=np.float32) / np.float32(half))).astype(np.float32)
    row = np.repeat(np.arange(4, dtype=np.float32), 64)
    col = np.tile(np.arange(64, dtype=np.float32), 4)
    ar = (row[None, :] * inv[:, None]).astype(np.float32)
    ac = (col[None, :] * inv[:, None]).astype(np.float32)
    ang = np.concatenate([ar, ar, ac, ac], 0)
    add("cos", np.cos(ang).astype(np.float32))
    add("sin", np.sin(ang).astype(np.float32))
    return np.ascontiguousarray(np.concatenate(parts, 1))


CONSTS = const_table()


class Queue:

    def __init__(self, sem):
        self.sem = sem
        self.n = 0
        self.ops = []
        self.seen = {}

    def wait(self, *marks):
        for m in marks:
            if m is None or len(m) == 0:
                continue
            if isinstance(m, list) or not isinstance(m[0], int):
                self.wait(*m)
                continue
            key, sem, v = m
            if self.seen.get(key, 0) >= v:
                continue
            self.seen[key] = v
            self.ops.append(lambda e, sem=sem, v=v: e.wait_ge(sem, v))

    def do(self, fn, *marks, inc=True):
        self.wait(*marks)
        if inc:
            self.n += 1
            self.ops.append(lambda e: fn(e).then_inc(self.sem, 1))
            return (id(self), self.sem, self.n)
        self.ops.append(fn)
        return None

    def last(self):
        return (id(self), self.sem, self.n) if self.n else None

    def play(self, e):
        for op in self.ops:
            op(e)


class Slot:

    def __init__(self, ap, sem):
        self.ap = ap
        self.sem = sem
        self.n = 0
        self.free = []

    def load(self, q, dst, src, *marks):
        q.wait(self.free, *marks)
        self.n += 16
        sem = self.sem
        q.ops.append(lambda e: e.dma_start(dst, src).then_inc(sem, 16))
        return (id(self), sem, self.n)


def build(nc, A, out):
    ctx = ExitStack()
    with ctx:
        def sb(name, shape, dt=F32, stack=ctx):
            return stack.enter_context(nc.sbuf_tensor(name, shape, dt))

        def semf(name):
            return ctx.enter_context(nc.semaphore(name))

        banks = [ctx.enter_context(nc.psum_tensor(f"bank{i}", [128, 512], F32)) for i in range(8)]
        PE, AC, DV, PO, SP = (Queue(semf(n)) for n in ("s_pe", "s_act", "s_dve", "s_pool", "s_sp"))

        free_banks = [(b, []) for b in banks]

        def bank():
            b, marks = free_banks.pop(0)
            return b, list(marks)

        def release(b, *marks):
            free_banks.append((b, [m for m in marks]))

        X = sb("X", [128, 4, D])
        HH = sb("HH", [128, 8, 512], F32R)
        HL = sb("HL", [128, 8, 512], F32R)
        Y = sb("Y", [128, 4224])
        Y4 = Y[:, 0:4096].rearrange("p (t n) -> p t n", t=4)
        G = sb("G", [128, 2, D])
        raws = [Slot(sb(f"raw{i}", [128, 1024]), semf(f"s_raw{i}")) for i in range(NRAW)]
        spl = [(sb(f"wh{i}", [128, 1024], F32R), sb(f"wl{i}", [128, 1024], F32R)) for i in range(NSPL)]
        spl_free = [None] * NSPL
        adas = [Slot(sb(f"ada{i}", [128, 2, 512]), semf(f"s_ada{i}")) for i in range(NADA)]
        acc = sb("acc", [128, 2, 2, 512])
        gb = Slot(sb("gb", [128, 2, 512]), semf("s_gb"))
        ident = sb("ident", [128, 128])
        ones = sb("ones", [128, 128])
        tmps = [sb(f"tmp{i}", [128, 512]) for i in range(NTMP)]
        tmp_free = [[] for _ in range(NTMP)]
        tmp_n = [0]
        sc = sb("sc", [128, 4, 8])
        cw = sb("cw", [128, 2, 32])
        bgc = sb("bgc", [128, 2, 80])
        mod = sb("mod", [128, 2, 4, 2, 8])

        def tmp():
            i = tmp_n[0] % NTMP
            tmp_n[0] += 1
            return tmps[i], list(tmp_free[i]), i

        def fence():
            return [q.last() for q in (PE, AC, DV, PO)]

        def cap(name):
            a, n = CONST_SLICES[name]
            return A["consts"][:, a:a + n]

        def mload(dst, src, *marks, q=PO):
            return misc_load(q, dst, src, marks)

        misc_slots = {id(q): [Slot(None, semf(f"s_m{j}_{i}")) for i in range(10)] for j, q in enumerate((SP, PO))}
        misc_n = {id(SP): 0, id(PO): 0}

        def misc_load(q, dst, src, marks):
            sl = misc_slots[id(q)][misc_n[id(q)] % 10]
            misc_n[id(q)] += 1
            if sl.n:
                q.wait((id(sl), sl.sem, sl.n))
            return sl.load(q, dst, src, *marks)

        def tr(o, i, idn, *marks, inc=True):
            return PE.do(lambda e: e.transpose(o, i, idn), *marks, inc=inc)

        def cp(o, i, *marks):
            return DV.do(lambda e: e.tensor_copy(o, i), *marks)

        def rcp(o, i, *marks):
            return DV.do(lambda e: e.reciprocal(o, i), *marks)

        def rmax(o, i, ax, *marks):
            return DV.do(lambda e: e.reduce_max(o, i, ax), *marks)

        def rsum(o, i, ax, *marks):
            return DV.do(lambda e: e.reduce_sum(o, i, ax), *marks)

        def mset(o, v, *marks):
            return DV.do(lambda e: e.memset(o, v), *marks)

        def scan(o, a, b_, init, op0, op1, *marks):
            return DV.do(lambda e: e.tensor_tensor_scan(o, a, b_, init, op0, op1), *marks)

        def cpred(o, m, i, *marks):
            return DV.do(lambda e: e.copy_predicated(o, m, i), *marks)

        def act(o, i, f, *marks, **kw):
            return AC.do(lambda e: e.activation(o, i, f, **kw), *marks)

        def tt(o, a, b_, op, *marks, q=DV):
            return q.do(lambda e: e.tensor_tensor(o, a, b_, op), *marks)

        def ts(o, a, s1, s2, op0, op1, *marks, q=DV):
            if op1 is None:
                return q.do(lambda e: e.tensor_scalar(o, a, s1, None, op0), *marks)
            return q.do(lambda e: e.tensor_scalar(o, a, s1, s2, op0, op1), *marks)

        def stt(o, a, s, b_, op0, op1, *marks):
            return DV.do(lambda e: e.scalar_tensor_tensor(out=o, in0=a, scalar=s, in1=b_, op0=op0, op1=op1), *marks)

        d_id = mload(ident[:], cap("ident"))
        d_on = mload(ones[:], cap("ones"))
        crow = sb("crow", [8, 4, 128])
        d_c = [mload(crow[:, i, :], A[n], q=SP) for i, n in enumerate(("c_ctx", "c", "c_ctx_2", "c_2"))]
        d_x = [None] * 4
        for t in range(4):
            src = A["ctx"] if t < 2 else A["x"]
            d_x[t] = mload(X[:, t, :], src[(t % 2) * 128:(t % 2) * 128 + 128, :], q=SP)

        b, fr = bank()
        for i in range(4):
            pt = tr(b[:, 8 * i:8 * i + 8], crow[:, i, :], ident[0:8, 0:8],
                       fr, d_id, d_c[i])
        t1, tf, ti = tmp()
        a1 = act(t1[:, 0:32], b[:, 0:32], ACT.Exp, pt, tf, scale=-1.0)
        v1 = ts(t1[:, 32:64], t1[:, 0:32], 1.0, None, ALU.add, None, a1)
        v2 = rcp(t1[:, 64:96], t1[:, 32:64], v1)
        scd = tt(sc[:].rearrange("p a k -> p (a k)"), b[:, 0:32], t1[:, 64:96], ALU.mult, v2)
        tmp_free[ti] = [scd]
        release(b, scd)

        LAYERS = [
            dict(w=A["ada_w"][0], bia=A["ada_b"][0], g=A["norm_g"][0], c=0, both=True, w1=A["mlp_w1"][0], w2=A["mlp_w2"][0]),
            dict(w=A["ada_w"][1], bia=A["ada_b"][1], g=A["norm_g"][1], c=0, both=False, w1=A["mlp_w1"][1], w2=A["mlp_w2"][1]),
            dict(w=A["mod_w_2"][0], bia=A["mod_b_2"][0], g=A["norm_w_2"][0], c=2, both=True, w1=A["mlp_w1_2"][0], w2=A["mlp_w2_2"][0]),
            dict(w=A["mod_w_2"][1], bia=A["mod_b_2"][1], g=A["norm_w_2"][1], c=2, both=False, w1=A["mlp_w1_2"][1], w2=A["mlp_w2_2"][1]),
        ]

        def feat(W, c0, ncols, rows=D):
            for cb in range(c0, c0 + ncols, 256):
                for kk in range(0, rows, 512):
                    yield W[kk:kk + 512, cb:cb + 256].rearrange("(k p) n -> p k n", p=128)

        def tokw(W, r0, rows, c0, ncols):
            for cb in range(c0, c0 + ncols, 512):
                for kk in range(r0, r0 + rows, 256):
                    yield W[kk:kk + 256, cb:cb + 512].rearrange("(k p) n -> p k n", p=128)

        def mlp_stream(L):
            for q in range(4):
                yield from feat(L["w1"], q * 1024, 1024)
                yield from tokw(L["w2"], q * 1024, 1024, 0, 1024)

        def stream():
            for k in range(0, D, 256):
                yield A["mla_w_dq"][0][k:k + 256, :].rearrange("(k p) n -> p k n", p=128)
            for k in range(0, D, 256):
                yield A["mla_w_dkv"][0][k:k + 256, :].rearrange("(k p) n -> p k n", p=128)
            for h in range(8):
                yield A["mla_w_uq"][0][:, h * 192:(h + 1) * 192].rearrange("(k p) n -> p k n", p=128)
                yield A["mla_w_ukv"][0][:, h * 256:(h + 1) * 256].rearrange("(k p) n -> p k n", p=128)
            yield from tokw(A["mla_w_o"][0], 0, D, 0, D)
            yield from mlp_stream(LAYERS[0])
            for r in range(2):
                yield A["gla_w_gate1"][0, r].rearrange("(k p) n -> p k n", p=128)
            yield from tokw(A["gla_w_k"][0], 0, D, 0, 512)
            yield from tokw(A["gla_w_v"][0], 0, D, 0, 1024)
            yield from feat(A["gla_w_q"][0], 0, 512)
            yield from feat(A["gla_w_r"][0], 0, 1024)
            yield from tokw(A["gla_w_o"][0], 0, D, 0, D)
            yield from mlp_stream(LAYERS[1])
            W = A["conv_w_in_2"][0]
            for c in range(0, D, 256):
                yield from feat(W, D + c, 256)
                yield from feat(W, 2 * D + c, 256)
                yield from feat(W, c, 256)
            yield from tokw(A["conv_w_out_2"][0], 0, D, 0, D)
            yield from mlp_stream(LAYERS[2])
            W = A["ml_w_qkvo_2"][0]
            for r in range(2):
                yield A["ml_w_if_2"][0, r].rearrange("(k p) n -> p k n", p=128)
            yield from tokw(W, 0, D, 512, 512)
            yield from tokw(W, 0, D, 1024, 1024)
            yield from feat(W, 0, 512)
            yield from feat(W, 512, 512)
            yield from feat(W, 2048, 1024)
            yield from tokw(A["ml_w_out_2"][0], 0, D, 0, D)
            yield from mlp_stream(LAYERS[3])

        WL = list(stream())
        w_at = [0]
        w_split = [0]
        w_dma = [0]
        w_mark = {}
        w_done = {}
        w_raw = {}

        def shape2(ap):
            return ap.shape[1], ap.shape[2]

        def issue_dma():
            k = w_dma[0]
            if k >= len(WL):
                return
            sl = raws[k % NRAW]
            a, n = shape2(WL[k])
            w_raw[k] = sl.load(SP, sl.ap[:, 0:a * n].rearrange("p (a n) -> p a n", a=a), WL[k])
            w_dma[0] += 1

        def issue_split():
            k = w_split[0]
            if k >= len(WL):
                return
            while w_dma[0] <= k:
                issue_dma()
            sl = raws[k % NRAW]
            hi, lo = spl[k % NSPL]
            a, n = shape2(WL[k])
            m = a * n
            done = w_done[k - NSPL] if k >= NSPL else None
            r = sl.ap
            t1 = AC.do(lambda e: e.activation(hi[:, 0:m], r[:, 0:m], ACT.Copy), w_raw[k], done)
            t2 = DV.do(lambda e: e.tensor_tensor(lo[:, 0:m], r[:, 0:m], hi[:, 0:m].bitcast(F32), ALU.subtract),
                       w_raw[k], t1, done)
            sl.free = [t1, t2]
            w_mark[k] = [t1, t2]
            w_split[0] += 1
            issue_dma()

        bg = []
        bg_done = set()
        allow = set()

        def pump(n):
            while n > 0 and bg and bg[0][0] in allow:
                key, fn, last = bg.pop(0)
                fn()
                if last:
                    bg_done.add(key)
                n -= 1

        def ensure(key):
            allow.add(key)
            while key not in bg_done:
                assert bg[0][0] in allow, (bg[0][0], key)
                pump(1)

        PUMP = [1]

        def take():
            k = w_at[0]
            while w_split[0] < min(k + NSPL, len(WL)):
                issue_split()
            w_at[0] += 1
            pump(PUMP[0])
            hi, lo = spl[k % NSPL]
            a, n = shape2(WL[k])
            v = [x[:, 0:a * n].rearrange("p (a n) -> p a n", a=a) for x in (hi, lo)]
            return k, v[0], v[1], w_mark[k]

        def gave(k, mark):
            w_done[k] = mark

        def mm3(o, s, m, start, stop, marks=(), inc=False):
            PE.wait(*marks)
            sh, sl_ = s
            mh, ml = m
            PE.do(lambda e: e.matmul(o, sh, mh, start=start, stop=False, skip_group_check=True), inc=False)
            PE.do(lambda e: e.matmul(o, sh, ml, start=False, stop=False, skip_group_check=True), inc=False)
            return PE.do(lambda e: e.matmul(o, sl_, mh, start=False, stop=stop, skip_group_check=True), inc=inc)

        def mm(o, s, m, start, stop, marks=(), inc=False):
            PE.wait(*marks)
            return PE.do(lambda e: e.matmul(o, s, m, start=start, stop=stop, skip_group_check=True), inc=inc)

        ada_n = [0]
        acc_free = [[], []]
        acc_n = [0]
        G_free = [None]
        mod_mark = {}
        G_mark = {}

        def ada_prepare(li):
            L = LAYERS[li]
            t1, tf, ti = tmp()
            m1 = mload(t1[0:48, 0:128], L["bia"].rearrange("(r p) -> r p", p=128), tf)
            m2 = mload(t1[0:32, 128:256], L["g"].rearrange("a (r p) -> (a r) p", p=128), tf)
            b, fr = bank()
            tr(b[:, 0:48], t1[0:48, 0:128], ident[0:48, 0:48], fr, m1, d_id, inc=False)
            p = tr(b[:, 48:80], t1[0:32, 128:256], ident[0:32, 0:32], m2)
            v = cp(bgc[:, li % 2, :], b[:, 0:80], p)
            tmp_free[ti] = [p]
            release(b, v)
            mod_mark[(li, "bg")] = v

        def ada_units(li):
            L = LAYERS[li]
            W = L["w"]
            order = [0, 1, 3, 4, 2, 5]
            for part in order:
                types = [1] if (not L["both"] and part > 1) else [0, 1]
                key = (li, part)
                units = []
                if part == 0:
                    units.append(lambda li=li: ada_prepare(li))
                for ch in range(2):
                    state = {}

                    def load_slot(kk, part=part, ch=ch, state=state):
                        sl = adas[ada_n[0] % NADA]
                        ada_n[0] += 1
                        c0 = part * D + ch * 512
                        src = W[kk * 256:kk * 256 + 256, c0:c0 + 512].rearrange("(k p) n -> p k n", p=128)
                        m = sl.load(PO, sl.ap[:], src)
                        state[kk] = (sl, m)

                    def work(kk, state=state, types=types, L=L, load_slot=load_slot):
                        if kk == 0:
                            state["buf"] = acc_n[0] % 2
                            acc_n[0] += 1
                            load_slot(0)
                            load_slot(1)
                        bi = state["buf"]
                        sl, m = state[kk]
                        for k in range(2):
                            for ty in types:
                                o = acc[:, bi, ty, :]
                                cc = sc[:, L["c"] + ty, kk * 2 + k:kk * 2 + k + 1]
                                if kk == 0 and k == 0:
                                    mk = ts(o, sl.ap[:, k, :], cc, None, ALU.mult, None, m, scd, acc_free[bi])
                                else:
                                    mk = stt(o, sl.ap[:, k, :], cc, o, ALU.mult, ALU.add, m, state[("m", ty)])
                                state[("m", ty)] = mk
                        sl.free = [mk]
                        if kk + 2 < 4:
                            load_slot(kk + 2)

                    for kk in range(4):
                        units.append(lambda kk=kk, work=work: work(kk))

                    def finish(part=part, ch=ch, state=state, types=types, li=li, L=L):
                        bi = state["buf"]
                        marks = [state[("m", ty)] for ty in types]
                        if part in (2, 5):
                            gi = 1 if part == 2 else 3
                            src = L["bia"][part * D + ch * 512:part * D + ch * 512 + 512]
                            g1 = gb.load(PO, gb.ap[:, 0, :], src.partition_broadcast(128))
                            gb.free = []
                            g2 = gb.load(PO, gb.ap[:, 1, :], L["g"][gi][ch * 512:ch * 512 + 512].partition_broadcast(128))
                            for ty in types:
                                b, fr = bank()
                                p = mm(b[:, :], ones[:], acc[:, bi, ty, :], True, True, (fr, marks, d_on), inc=True)
                                o = G[:, ty, ch * 512:ch * 512 + 512]
                                v = tt(o, b[:, :], gb.ap[:, 0, :], ALU.add, p, g2, G_free[0])
                                release(b, v)
                                v = tt(o, o, gb.ap[:, 1, :], ALU.mult, v, g2)
                            gb.free = [v]
                            acc_free[bi] = [p]
                            G_mark[(li, part)] = v
                        else:
                            pi = {0: 0, 1: 1, 3: 2, 4: 3}[part]
                            b, fr = bank()
                            PE.wait(fr, marks, d_on)
                            for n, ty in enumerate(types):
                                for mth in range(4):
                                    p = mm(b[:, n * 4 + mth:n * 4 + mth + 1], acc[:, bi, ty, mth * 128:mth * 128 + 128],
                                           ones[:, 0:1], True, True, inc=True)
                            acc_free[bi] = [p]
                            bc = bgc[:, li % 2, part * 8 + ch * 4:part * 8 + ch * 4 + 4]
                            gc0 = 48 + (0 if part == 1 else 2) * 8 + ch * 4
                            gc = bgc[:, li % 2, gc0:gc0 + 4]
                            for n, ty in enumerate(types):
                                o = mod[:, li % 2, pi, ty, ch * 4:ch * 4 + 4]
                                v = tt(o, b[:, n * 4:n * 4 + 4], bc, ALU.add, p, mod_mark[(li, "bg")])
                                if n == len(types) - 1:
                                    release(b, v)
                                if part in (1, 4):
                                    v = stt(o, o, 1.0, gc, ALU.add, ALU.mult, v)
                            mod_mark[(li, pi)] = v

                    units.append(finish)
                for n, u in enumerate(units):
                    bg.append((key, u, n == len(units) - 1))

        for li in range(4):
            ada_units(li)

        st_n = [0]

        stx = sb("stx", [128, 4, 5, 16])

        def stats():
            i = st_n[0] % 4
            st_n[0] += 1
            return stx[:, i, :, :]

        def rstd(s, n, width, marks):
            ss, va, r0, q1, r = (s[:, j, 0:n] for j in range(5))
            v = ts(va, ss, 1.0 / width, EPS, ALU.mult, ALU.add, marks)
            a = act(q1, va, ACT.Ln, v)
            a = act(r0, q1, ACT.Exp, a, scale=-0.5)
            v = tt(q1, r0, r0, ALU.mult, a)
            v = tt(q1, q1, va, ALU.mult, v)
            v = ts(q1, q1, -0.5, 1.5, ALU.mult, ALU.add, v)
            v = tt(r, q1, r0, ALU.mult, v)
            return r, v

        def sumsq(src, dst, junk, *marks):
            return act(junk, src, ACT.Square, *marks, accum_out=dst)

        def make_h(li, which, halves, xmarks, hfree, yfree):
            pi = 2 * which
            out_marks = []
            junkm = yfree
            for hf in halves:
                s = stats()
                m = None
                for t in range(2):
                    tt_ = hf * 2 + t
                    m = sumsq(X[:, tt_, :], s[:, 0, t:t + 1], Y4[:, tt_, :], xmarks[tt_], junkm)
                r, rm = rstd(s, 2, D, [m])
                xm = []
                for t in range(2):
                    tt_ = hf * 2 + t
                    xm.append(act(Y4[:, tt_, :], X[:, tt_, :], ACT.Copy, rm, m, scale=r[:, t:t + 1]))
                ensure((li, 0 if which == 0 else 3))
                ensure((li, 1 if which == 0 else 4))
                mB, mA = mod_mark[(li, pi)], mod_mark[(li, pi + 1)]
                for kp in range(4):
                    b, fr = bank()
                    PE.wait(fr)
                    for k in range(2):
                        for t in range(2):
                            kk = kp * 2 + k
                            tt_ = hf * 2 + t
                            p = tr(
                                b[:, k * 256 + t * 128:k * 256 + t * 128 + 128],
                                Y4[:, tt_, kk * 128:kk * 128 + 128], ident[:], xm[t], inc=True)
                    t1, tf, ti = tmp()
                    for k in range(2):
                        kk = kp * 2 + k
                        v = ts(t1[:, k * 256:k * 256 + 256], b[:, k * 256:k * 256 + 256],
                               mod[:, li % 2, pi + 1, hf, kk:kk + 1], mod[:, li % 2, pi, hf, kk:kk + 1],
                               ALU.mult, ALU.add, p, tf, mA, mB)
                    release(b, v)
                    t3 = t1[:, :].rearrange("p (k n) -> p k n", k=2)
                    oh = HH[:, kp * 2:kp * 2 + 2, hf * 256:hf * 256 + 256]
                    ol = HL[:, kp * 2:kp * 2 + 2, hf * 256:hf * 256 + 256]
                    a = act(oh, t3, ACT.Copy, v, hfree)
                    v = tt(ol, t3, oh.bitcast(F32), ALU.subtract, a, hfree)
                    tmp_free[ti] = [a, v]
                    out_marks.append(v)
                    out_marks.append(a)
            return [out_marks[-1], out_marks[-2]]

        def combine(li, part, tiles, ymarks):
            ensure((li, part))
            gm = G_mark[(li, part)]
            xm = {}
            for hf in sorted({t // 2 for t in tiles}):
                s = stats()
                for t in range(2):
                    tt_ = hf * 2 + t
                    t1, tf, ti = tmp()
                    t2, tf2, ti2 = tmp()
                    m1 = sumsq(Y4[:, tt_, 0:512], s[:, 0, 8 + 2 * t:9 + 2 * t], t1[:], ymarks[tt_], tf)
                    m = sumsq(Y4[:, tt_, 512:1024], s[:, 0, 9 + 2 * t:10 + 2 * t], t2[:], ymarks[tt_], tf2)
                    tmp_free[ti] = [m1]
                    tmp_free[ti2] = [m]
                v = tt(s[:, 0, 0:2], s[:, 0, 8:12].rearrange("p (a b) -> p a b", b=2)[:, :, 0],
                       s[:, 0, 8:12].rearrange("p (a b) -> p a b", b=2)[:, :, 1], ALU.add, m)
                r, rm = rstd(s, 2, D, [v])
                for t in range(2):
                    tt_ = hf * 2 + t
                    v = stt(Y4[:, tt_, :], Y4[:, tt_, :], r[:, t:t + 1], G[:, hf, :], ALU.mult, ALU.mult, rm, gm, m,
                            ymarks[tt_])
                    xm[tt_] = tt(X[:, tt_, :], X[:, tt_, :], Y4[:, tt_, :], ALU.add, v)
            G_free[0] = [v]
            return xm, xm[max(tiles)]

        def proj_feat(nblocks, src, c0, c1, evac, marks):
            H1, H2 = src
            N = c1 - c0
            for nb in range(nblocks):
                bs = [bank(), bank()]
                for kk in range(2):
                    k, wh, wl, wm = take()
                    for m in range(2):
                        b, fr = bs[m]
                        for q in range(4):
                            kt = kk * 4 + q
                            last = mm3(b[:, 0:N], (wh[:, q, m * 128:m * 128 + 128], wl[:, q, m * 128:m * 128 + 128]),
                                       (H1[:, kt, c0:c1], H2[:, kt, c0:c1]), kt == 0, kt == 7,
                                       (fr, wm, marks), inc=(q == 3))
                        if kk == 1:
                            bs[m] = (b, last)
                    gave(k, last)
                for m in range(2):
                    evac(nb * 2 + m, bs[m][0], bs[m][1])

        def proj_tok(src, nk, tiles, nhalves, evac, marks, width=512):
            H1, H2 = src
            for nh in range(nhalves):
                bs = {t: bank() for t in tiles}
                for kk in range(nk // 2):
                    k, wh, wl, wm = take()
                    for t in tiles:
                        b, fr = bs[t][0], bs[t][1]
                        for q in range(2):
                            kt = kk * 2 + q
                            last = mm3(b[:, 0:width], (H1[:, kt, t * 128:t * 128 + 128], H2[:, kt, t * 128:t * 128 + 128]),
                                       (wh[:, q, 0:width], wl[:, q, 0:width]), kt == 0, kt == nk - 1,
                                       (fr, wm, marks), inc=(q == 1))
                        if kk == nk // 2 - 1:
                            bs[t] = (b, last)
                    gave(k, last)
                for t in tiles:
                    evac(nh, t, bs[t][0], bs[t][1])

        flip = [0]

        def copy_out(o, i, *marks):
            flip[0] ^= 1
            if flip[0]:
                return act(o, i, ACT.Copy, *marks)
            return cp(o, i, *marks)

        def y_evac_for(ym, yfree, first=True):
            def f(nh, t, b, p):
                o = Y4[:, t, nh * 512:nh * 512 + 512]
                if first:
                    m = copy_out(o, b[:, :], p, yfree)
                else:
                    m = tt(o, o, b[:, :], ALU.add, p, ym.get((t, nh)))
                ym[(t, nh)] = m
                release(b, m)
            return f

        def ylist(ym, tiles):
            return {t: [ym[(t, 0)], ym[(t, 1)]] for t in tiles}

        def mlp(li, tiles, hm, stack):
            c0 = tiles[0] * 128
            N = len(tiles) * 128
            fz = fence()
            UH = sb(f"UH{li}", [128, 8, 512], F32R, stack)
            UL = sb(f"UL{li}", [128, 8, 512], F32R, stack)
            ym = {}
            ufree = [[fz] for _ in range(8)]
            for q in range(4):
                um = []

                def evac(n, b, p):
                    t1, tf, ti = tmp()
                    a = act(t1[:, 0:N], b[:, 0:N], ACT.Relu, p, tf)
                    release(b, a)
                    t2, tf2, ti2 = tmp()
                    v = tt(t2[:, 0:N], t1[:, 0:N], t1[:, 0:N], ALU.mult, a, tf2)
                    tmp_free[ti] = [v]
                    a = act(UH[:, n, 0:N], t2[:, 0:N], ACT.Copy, v, ufree[n])
                    v = tt(UL[:, n, 0:N], t2[:, 0:N], UH[:, n, 0:N].bitcast(F32), ALU.subtract, a, ufree[n])
                    tmp_free[ti2] = [a, v]
                    um.append([a, v])

                proj_feat(4, (HH, HL), c0, c0 + N, evac, hm)
                for nh in range(2):
                    bs = {t: bank() for t in tiles}
                    for kk in range(4):
                        k, wh, wl, wm = take()
                        for t in tiles:
                            b, fr = bs[t]
                            o = (t - tiles[0]) * 128
                            for r in range(2):
                                kt = kk * 2 + r
                                last = mm3(b[:, :], (UH[:, kt, o:o + 128], UL[:, kt, o:o + 128]),
                                           (wh[:, r, :], wl[:, r, :]), kt == 0, kt == 7,
                                           (fr, wm, um[kt]), inc=(r == 1))
                            if kk == 3:
                                bs[t] = (b, last)
                        gave(k, last)
                    for t in tiles:
                        y_evac_for(ym, hm, first=(q == 0))(nh, t, bs[t][0], bs[t][1])
                ufree = [[last] for _ in range(8)]
            return ylist(ym, tiles)

        def hi_lo(oh, ol, src, *marks):
            a = act(oh, src, ACT.Copy, *marks)
            v = tt(ol, src, oh.bitcast(F32), ALU.subtract, a, *marks)
            return [a, v]

        def mla(li, hm, stack):
            fz = fence()
            with ExitStack() as s1:
                CQH = sb("CQH", [128, 3, 512], F32R, s1)
                CQL = sb("CQL", [128, 3, 512], F32R, s1)
                CKH = sb("CKH", [128, 2, 512], F32R, s1)
                CKL = sb("CKL", [128, 2, 512], F32R, s1)
                krT = sb("krT", [64, 512], F32, s1)
                cs = sb("cs", [64, 2, 256], F32, s1)
                rot = sb("rot", [64, 64], F32, s1)
                grow = sb("grow", [5, 128], F32, s1)
                gcol = sb("gcol", [128, 5], F32, s1)
                qn = [sb(f"qn{i}", [128, 512], F32, s1) for i in range(2)]
                kn = [sb(f"kn{i}", [128, 512], F32, s1) for i in range(2)]
                qr = [sb(f"qr{i}", [64, 512], F32, s1) for i in range(2)]
                Pl = [sb(f"Pl{i}", [128, 512], F32, s1) for i in range(2)]
                Pc = [sb(f"Pc{i}", [128, 256], F32, s1) for i in range(2)]
                PTl = sb("PTl", [128, 4, 256], F32, s1)
                PTc = sb("PTc", [128, 2, 256], F32, s1)
                CQ = Y[:, 0:2816].rearrange("p (t n) -> p t n", t=4)
                VV = [Y[:, 2816 + 512 * i:3328 + 512 * i].rearrange("p (t n) -> p t n", t=4) for i in range(2)]
                mc1 = mload(cs[:, 0, :], cap("cos")[0:64, :], fz)
                mc2 = mload(cs[:, 1, :], cap("sin")[0:64, :], fz)
                mr = mload(rot[:], cap("rot")[0:64, :], fz)
                mg1 = mload(grow[0:3, :], A["mla_g_q"][0].rearrange("(r p) -> r p", p=128), fz)
                mg2 = mload(grow[3:5, :], A["mla_g_kv"][0].rearrange("(r p) -> r p", p=128), fz)
                b, fr = bank()
                p = tr(b[:, 0:5], grow[:], ident[0:5, 0:5], fr, mg1, mg2)
                mg = cp(gcol[:], b[:, 0:5], p, fz)
                release(b, mg)
                cm = {}

                def ev(off, w):
                    def f(nh, t, b, p):
                        m = copy_out(CQ[:, t, off:off + w], b[:, 0:w], p, fz, hm)
                        cm[(t, off)] = m
                        release(b, m)
                    return f

                proj_tok((HH, HL), 8, [0, 1, 2, 3], 1, ev(0, 384), [hm], width=384)
                proj_tok((HH, HL), 8, [0, 1, 2, 3], 1, ev(384, 320), [hm], width=320)
                s = stats()
                for t in range(4):
                    t1, tf, ti = tmp()
                    m1 = sumsq(CQ[:, t, 0:384], s[:, 0, t:t + 1], t1[:, 0:384], cm[(t, 0)], tf)
                    tmp_free[ti] = [m1]
                r, rm = rstd(s, 4, 384, [m1])
                s2 = stats()
                for t in range(4):
                    t1, tf, ti = tmp()
                    m2 = sumsq(CQ[:, t, 384:640], s2[:, 0, t:t + 1], t1[:, 0:256], cm[(t, 384)], tf)
                    tmp_free[ti] = [m2]
                r2, rm2 = rstd(s2, 4, 256, [m2])
                nm = []
                for t in range(4):
                    m = ts(CQ[:, t, 0:384], CQ[:, t, 0:384], r[:, t:t + 1], None, ALU.mult, None, rm, m1, cm[(t, 0)])
                    m = ts(CQ[:, t, 384:640], CQ[:, t, 384:640], r2[:, t:t + 1], None, ALU.mult, None, rm2, m2,
                           cm[(t, 384)])
                    nm.append(m)
                for f in range(6):
                    w = 128 if f < 5 else 64
                    b, fr = bank()
                    PE.wait(fr)
                    for t in range(4):
                        p = tr(
                            b[0:w, t * 128:t * 128 + 128], CQ[:, t, f * 128:f * 128 + w], ident[:],
                            nm[t], cm[(t, 384)])
                    if f < 5:
                        oh, ol = (CQH[:, f, :], CQL[:, f, :]) if f < 3 else (CKH[:, f - 3, :], CKL[:, f - 3, :])
                        a = act(oh, b[:, :], ACT.Copy, p, mg, fz, scale=gcol[:, f:f + 1])
                        v = stt(ol, b[:, :], gcol[:, f:f + 1], oh.bitcast(F32), ALU.mult, ALU.subtract, a)
                        release(b, v)
                        if f < 3:
                            cqm = [a, v]
                        else:
                            ckm = [a, v]
                    else:
                        a = cp(krT[:], b[0:64, :], p, fz)
                        release(b, a)
                        krm = a

                def rope(x, xm):
                    b, fr = bank()
                    p = mm(b[0:64, 0:256], rot[:], x[:, 256:512], True, True, (fr, xm, mr), inc=True)
                    t1, tf, ti = tmp()
                    v1 = tt(t1[0:64, 0:256], b[0:64, 0:256], cs[:, 1, :], ALU.mult, p, mc2, tf)
                    release(b, v1)
                    v2 = tt(x[:, 256:512], x[:, 256:512], cs[:, 0, :], ALU.mult, p, mc1, xm)
                    v3 = tt(x[:, 256:512], x[:, 256:512], t1[0:64, 0:256], ALU.add, v1, v2)
                    tmp_free[ti] = [v3]
                    return v3

                krm = rope(krT, krm)
                SC = 192.0 ** -0.5
                sfree = [[fz], [fz]]
                vfree = [[fz, cqm, ckm, krm], [fz, cqm, ckm, krm]]
                Plf = [[fz], [fz]]
                Pcf = [[fz], [fz]]
                PTfree = [fz]
                om = []

                def stage_a(h):
                    i = h % 2
                    k, wh, wl, wm = take()
                    b, fr = bank()
                    for q in range(3):
                        p = mm3(b[:, :], (wh[:, q, 0:128], wl[:, q, 0:128]), (CQH[:, q, :], CQL[:, q, :]),
                                q == 0, q == 2, (fr, wm, cqm), inc=(q == 2))
                    a1 = act(qn[i][:], b[:, :], ACT.Copy, p, sfree[i])
                    release(b, a1)
                    b, fr = bank()
                    for q in range(3):
                        p = mm3(b[0:64, :], (wh[:, q, 128:192], wl[:, q, 128:192]), (CQH[:, q, :], CQL[:, q, :]),
                                q == 0, q == 2, (fr,), inc=(q == 2))
                    gave(k, p)
                    v1 = cp(qr[i][:], b[0:64, :], p, sfree[i])
                    release(b, v1)
                    k, wh, wl, wm = take()
                    b, fr = bank()
                    for q in range(2):
                        p = mm3(b[:, :], (wh[:, q, 0:128], wl[:, q, 0:128]), (CKH[:, q, :], CKL[:, q, :]),
                                q == 0, q == 1, (fr, wm, ckm), inc=(q == 1))
                    a2 = act(kn[i][:], b[:, :], ACT.Copy, p, sfree[i])
                    release(b, a2)
                    b, fr = bank()
                    PE.wait(fr)
                    for t in range(4):
                        for q in range(2):
                            p = mm3(b[:, t * 128:t * 128 + 128],
                                    (CKH[:, q, t * 128:t * 128 + 128], CKL[:, q, t * 128:t * 128 + 128]),
                                    (wh[:, q, 128:256], wl[:, q, 128:256]), q == 0, q == 1, (),
                                    inc=(q == 1 and t == 3))
                    gave(k, p)
                    v2 = cp(VV[i], b[:, :].rearrange("p (t n) -> p t n", t=4), p,
                               vfree[i])
                    release(b, v2)
                    v1 = rope(qr[i], v1)
                    return (i, a1, a2, v1, v2)

                def stage_b(h, S):
                    i, a1, a2, v1, v2 = S
                    marks = (a1, a2, v1, krm)
                    pm = []
                    for half, nk, PB, PF in ((1, 512, Pl, Plf), (0, 256, Pc, Pcf)):
                        for t in range(2):
                            c = half * 256 + t * 128
                            b, fr = bank()
                            mm(b[:, 0:nk], qn[i][:, c:c + 128], kn[i][:, 0:nk], True, False, (fr, marks))
                            p = mm(b[:, 0:nk], qr[i][:, c:c + 128], krT[:, 0:nk], False, True, inc=True)
                            s = stats()
                            m = rmax(s[:, 0, 0:1], b[:, 0:nk], AX.X, p)
                            m = ts(s[:, 1, 0:1], s[:, 0, 0:1], -SC, None, ALU.mult, None, m)
                            a = act(PB[t][:, 0:nk], b[:, 0:nk], ACT.Exp, m, PF[t], bias=s[:, 1, 0:1], scale=SC,
                                    accum_out=s[:, 2, 0:1])
                            release(b, a)
                            m = rcp(s[:, 3, 0:1], s[:, 2, 0:1], a)
                            m = ts(PB[t][:, 0:nk], PB[t][:, 0:nk], s[:, 3, 0:1], None, ALU.mult, None, m)
                            pm.append(m)
                    sfree[i] = [p]
                    ptm = []
                    n = 0
                    for half, nk, PB, PF, PT in ((1, 4, Pl, Plf, PTl), (0, 2, Pc, Pcf, PTc)):
                        for t in range(2):
                            b, fr = bank()
                            PE.wait(fr, pm[n])
                            for kt in range(nk):
                                p = tr(
                                    b[:, kt * 128:kt * 128 + 128], PB[t][:, kt * 128:kt * 128 + 128], ident[:])
                            PF[t] = [p]
                            m = copy_out(PT[:, :, t * 128:t * 128 + 128],
                                         b[:, 0:nk * 128].rearrange("p (k n) -> p k n", k=nk), p, PTfree)
                            release(b, m)
                            ptm.append(m)
                            n += 1
                    b, fr = bank()
                    for kt in range(4):
                        mm(b[:, 256:512], VV[i][:, kt, :], PTl[:, kt, :], kt == 0, kt == 3, (fr, ptm, v2))
                    for kt in range(2):
                        p = mm(b[:, 0:256], VV[i][:, kt, :], PTc[:, kt, :], kt == 0, kt == 1, inc=(kt == 1))
                    PTfree[:] = [p]
                    vfree[i] = [p]
                    m = hi_lo(HH[:, h, :], HL[:, h, :], b[:, :], p)
                    release(b, m)
                    om.append(m)

                prev = None
                for h in range(9):
                    cur = stage_a(h) if h < 8 else None
                    if prev is not None:
                        stage_b(h - 1, prev)
                    prev = cur
                fz2 = fence()
            ym = {}
            proj_tok((HH, HL), 8, [0, 1, 2, 3], 2, y_evac_for(ym, fz2), [om])
            return ylist(ym, [0, 1, 2, 3])

        def gla(li, hm, stack):
            fz = fence()
            S = Y[:, 0:2048].rearrange("p (r h n) -> p r h n", r=2, h=4)
            VL = Y[:, 2048:4096].rearrange("p (t n) -> p t n", t=2)
            with ExitStack() as s1:
                cst = sb("g_cst", [128, 9, 128], F32, s1)
                mcs = mload(cst[:].rearrange("p a n -> p (a n)"), A["consts"][:, CONST_SLICES["cum"][0]:
                            CONST_SLICES["cum"][0] + 1152], fz)
                cum, end, endc = (lambda r: cst[:, r, :]), (lambda r: cst[:, 2 + r, :]), (lambda r: cst[:, 4 + r, :])
                tot, gmask = cst[:, 6, :], (lambda r: cst[:, 7 + r, :])
                z = sb("g_z", [65, 512], F32, s1)
                w2p = sb("g_w2p", [65, 2, 512], F32, s1)
                KLt = sb("g_klt", [128, 2, 512], F32, s1)
                v = mset(z[:], 1.0, fz)
                v0 = mset(w2p[:], 0.0, fz)
                zm0 = v
                wm2 = []
                for r in range(2):
                    wm2.append(mload(w2p[32 * r:32 * r + 16, r, :], A["gla_w_gate2"][0, r], v0))
                    wm2.append(mload(w2p[64:65, r, :], A["gla_b_gate"][0:1, r, :], v0))
                zc = []
                for r in range(2):
                    k, wh, wl, wm = take()
                    b, fr = bank()
                    for q in range(8):
                        p = mm3(b[0:16, :], (wh[:, q, :], wl[:, q, :]), (HH[:, q, :], HL[:, q, :]), q == 0, q == 7,
                                (fr, wm, hm), inc=(q == 7))
                    gave(k, p)
                    v = cp(z[32 * r:32 * r + 16, :], b[0:16, :], p, zm0)
                    release(b, v)
                    zc.append(v)
                gmarks = [zc, wm2]

                def log_gate(r, t, dst, *marks):
                    b, fr = bank()
                    p = mm(b[:, :], z[:, t * 128:t * 128 + 128], w2p[:, r, :], True, True, (fr, gmarks), inc=True)
                    t1, tf, ti = tmp()
                    a = act(t1[:], b[:, :], ACT.Abs, p, tf)
                    a = act(t1[:], t1[:], ACT.Exp, a, scale=-1.0)
                    a = act(t1[:], t1[:], ACT.Ln, a, bias=ones[:, 0:1])
                    v = stt(dst, b[:, :], 0.0, t1[:], ALU.min, ALU.subtract, a, marks)
                    release(b, v)
                    tmp_free[ti] = [v]
                    return v

                with ExitStack() as s2:
                    KC = sb("g_kc", [128, 2, 512], F32, s2)
                    VC = sb("g_vc", [128, 2, 1024], F32, s2)
                    gx = sb("g_gx", [128, 2, 512], F32, s2)
                    KE = sb("g_ke", [128, 2, 512], F32, s2)
                    km, vm = {}, {}

                    def evk(nh, t, b, p):
                        dst = KC[:, t, :] if t < 2 else KLt[:, t - 2, :]
                        km[t] = copy_out(dst, b[:, :], p, fz)
                        release(b, km[t])

                    def evv(nh, t, b, p):
                        dst = (VC[:, t, :] if t < 2 else VL[:, t - 2, :])[:, nh * 512:nh * 512 + 512]
                        vm[(t, nh)] = copy_out(dst, b[:, :], p, fz)
                        release(b, vm[(t, nh)])

                    proj_tok((HH, HL), 8, [0, 1, 2, 3], 1, evk, [hm])
                    proj_tok((HH, HL), 8, [0, 1, 2, 3], 2, evv, [hm])
                    Sm = {}
                    prev = None
                    for r in range(2):
                        gm = [log_gate(r, t, gx[:, t, :], prev) for t in range(2)]
                        kem = []
                        for t in range(2):
                            b, fr = bank()
                            far = 1 if r == 0 else 0
                            mm(b[:, :], endc(r), gx[:, t, :], True, t == far, (fr, gm, mcs), inc=False)
                            if t != far:
                                p = mm(b[:, :], tot, gx[:, far, :], False, True, inc=True)
                            else:
                                p = mm(b[:, :], endc(r), gx[:, t, :], True, True, inc=True)
                            a = act(KE[:, t, :], b[:, :], ACT.Exp, p, prev)
                            release(b, a)
                            kem.append(tt(KE[:, t, :], KE[:, t, :], KC[:, t, :], ALU.mult, a, km[t]))
                        for hp in range(2):
                            b, fr = bank()
                            PE.wait(fr, kem)
                            for hh in range(2):
                                h = hp * 2 + hh
                                for t in range(2):
                                    p = mm(b[:, hh * 256:hh * 256 + 256], KE[:, t, h * 128:h * 128 + 128],
                                           VC[:, t, h * 256:h * 256 + 256], t == 0, t == 1,
                                           (vm[(t, h // 2)],), inc=True)
                            m = copy_out(S[:, r, hp * 2:hp * 2 + 2, :],
                                         b[:, :].rearrange("p (h n) -> p h n", h=2), p, fz)
                            release(b, m)
                            Sm[(r, hp * 2)] = Sm[(r, hp * 2 + 1)] = m
                        prev = [p]
                    fz2 = fence()
                with ExitStack() as s2:
                    qT = sb("g_qT", [128, 4, 256], F32, s2)
                    kT = sb("g_kT", [128, 4, 256], F32, s2)
                    gx = sb("g_gl", [128, 2, 512], F32, s2)
                    EG = sb("g_eg", [128, 4, 128], F32, s2)
                    EN = sb("g_en", [128, 4, 128], F32, s2)
                    qt = sb("g_qt", [128, 4, 128], F32, s2)
                    kt_ = sb("g_ktt", [128, 4, 128], F32, s2)
                    KE = sb("g_kel", [128, 512], F32, s2)
                    AT = [sb(f"g_at{r}", [128, 4, 128], F32, s2) for r in range(2)]
                    az = [mset(AT[r][:], 0.0, fz2) for r in range(2)]
                    qm = {}

                    def evq(n, b, p):
                        qm[n] = act(qT[:, n, :], b[:, 0:256], ACT.Copy, p, fz2, scale=128.0 ** -0.5)
                        release(b, qm[n])

                    proj_feat(2, (HH, HL), 256, 512, evq, [hm])
                    ktm = {}
                    for hp in range(2):
                        b, fr = bank()
                        PE.wait(fr, km[2], km[3])
                        for hh in range(2):
                            h = hp * 2 + hh
                            for t in range(2):
                                p = tr(
                                    b[:, hh * 256 + t * 128:hh * 256 + t * 128 + 128],
                                    KLt[:, t, h * 128:h * 128 + 128], ident[:])
                        m = copy_out(kT[:, hp * 2:hp * 2 + 2, :], b[:, :].rearrange("p (h n) -> p h n", h=2), p, fz2)
                        release(b, m)
                        ktm[hp] = m
                    OB = [[bank() for _ in range(2)] for _ in range(2)]
                    started = set()
                    use = [None]
                    atfree = [None, None]
                    kefree = [None]
                    for r in range(2):
                        gm = [log_gate(r, 2 + t, gx[:, t, :], fz2, use[0]) for t in range(2)]
                        for ti_, t in enumerate([0, 1] if r == 0 else [1, 0]):
                            b, fr = bank()
                            PE.wait(fr, gm, mcs)
                            for h in range(4):
                                p = mm(b[:, h * 128:h * 128 + 128], gx[:, t, h * 128:h * 128 + 128], cum(r), True, True,
                                       inc=True)
                            bv = b[:, :].rearrange("p (h n) -> p h n", h=4)
                            a1 = act(EG[:], bv, ACT.Exp, p, use[0], fz2)
                            a2 = act(EN[:], bv, ACT.Exp, p, use[0], fz2, scale=-1.0)
                            release(b, a2)
                            v1 = tt(qt[:], EG[:], qT[:, :, t * 128:t * 128 + 128], ALU.mult, a1, list(qm.values()),
                                    use[0], fz2)
                            v2 = tt(kt_[:], EN[:], kT[:, :, t * 128:t * 128 + 128], ALU.mult, a2, ktm[0], ktm[1],
                                    use[0], fz2)
                            b, fr = bank()
                            p = mm(b[:, :], end(r), gx[:, t, :], True, True, (fr,), inc=True)
                            a3 = act(KE[:], b[:, :], ACT.Exp, p, kefree[0], fz2)
                            release(b, a3)
                            v3 = tt(KE[:], KE[:], KLt[:, t, :], ALU.mult, a3, km[2 + t])
                            b, fr = bank()
                            PE.wait(fr, v1, v2)
                            for h in range(4):
                                p = mm(b[:, h * 128:h * 128 + 128], kt_[:, h, :], qt[:, h, :], True, True, inc=True)
                            mk = gmask(r).bitcast(I32)
                            for h in range(4):
                                v4 = cpred(
                                    AT[r][:, h, :], mk, b[:, h * 128:h * 128 + 128], p, az, atfree[r], mcs)
                            release(b, v4)
                            for h in range(4):
                                ob, ofr = OB[t][h // 2]
                                first = (t, h // 2) not in started
                                started.add((t, h // 2))
                                p = mm(ob[:, (h % 2) * 256:(h % 2) * 256 + 256], AT[r][:, h, :],
                                       VL[:, t, h * 256:h * 256 + 256], first, False,
                                       (ofr, v4, vm[(2 + t, h // 2)]), inc=True)
                            atfree[r] = p
                            for ci, c in enumerate([0, 1] if r == 0 else [1, 0]):
                                last_chunk = ti_ == 1 and ci == 1
                                pr = {}
                                for h in range(4):
                                    ob = OB[t][h // 2][0]
                                    pr[h] = mm(ob[c * 64:c * 64 + 64, (h % 2) * 256:(h % 2) * 256 + 256],
                                               qt[:, h, c * 64:c * 64 + 64], S[:, r, h, :], False, False,
                                               (Sm[(r, h)],), inc=True)
                                use[0] = pr[3]
                                if last_chunk:
                                    continue
                                for hp in range(2):
                                    b, fr = bank()
                                    PE.wait(fr, v3)
                                    for hh in range(2):
                                        h = hp * 2 + hh
                                        p = mm(b[:, hh * 256:hh * 256 + 256],
                                               KE[c * 64:c * 64 + 64, h * 128:h * 128 + 128],
                                               VL[c * 64:c * 64 + 64, t, h * 256:h * 256 + 256], True, True, inc=True)
                                    for hh in range(2):
                                        h = hp * 2 + hh
                                        gi = c * 64 + (63 if r == 0 else 0)
                                        Sm[(r, h)] = stt(S[:, r, h, :], S[:, r, h, :], EG[:, h, gi:gi + 1],
                                                         b[:, hh * 256:hh * 256 + 256], ALU.mult, ALU.add, p, pr[h],
                                                         Sm[(r, h)])
                                    release(b, Sm[(r, h)])
                                kefree[0] = p
                                use[0] = [pr[3], Sm[(r, 3)], p]
                    of = PE.last()
                    fz3 = fence()
                with ExitStack() as s2:
                    sr = sb("g_sr", [128, 8, 256], F32, s2)
                    go = sb("g_go", [128, 2], F32, s2)
                    gor = sb("g_gor", [2, 128], F32, s2)
                    mg = mload(gor[:], A["gla_g_o"][0].rearrange("(r p) -> r p", p=128), fz3)
                    b, fr = bank()
                    p = tr(b[:, 0:2], gor[:], ident[0:2, 0:2], fr, mg)
                    gom = cp(go[:], b[:, 0:2], p, fz3)
                    release(b, gom)
                    Z = Y4[:, 0:2, :]
                    zm = []
                    s = stats()
                    s_ = None
                    for t in range(2):
                        for h in range(4):
                            ob = OB[t][h // 2][0]
                            t1, tf, ti = tmp()
                            m = sumsq(ob[:, (h % 2) * 256:(h % 2) * 256 + 256], s[:, 0, t * 4 + h:t * 4 + h + 1],
                                      t1[:, 0:256], of, tf)
                            tmp_free[ti] = [m]
                    rr, rm = rstd(s, 8, 256, [m])
                    for t in range(2):
                        for h in range(4):
                            ob = OB[t][h // 2][0]
                            m = act(Z[:, t, h * 256:h * 256 + 256], ob[:, (h % 2) * 256:(h % 2) * 256 + 256], ACT.Copy,
                                    rm, fz3, scale=rr[:, t * 4 + h:t * 4 + h + 1])
                            if h % 2 == 1:
                                release(ob, m)
                        zm.append(m)
                    srm = {}

                    def evr(n, b, p):
                        t1, tf, ti = tmp()
                        a = act(t1[:, 0:256], b[:, 0:256], ACT.Exp, p, tf, scale=-1.0)
                        v = ts(t1[:, 0:256], t1[:, 0:256], 1.0, None, ALU.add, None, a)
                        v = rcp(t1[:, 256:512], t1[:, 0:256], v)
                        v = tt(sr[:, n, :], b[:, 0:256], t1[:, 256:512], ALU.mult, v, fz3)
                        release(b, v)
                        tmp_free[ti] = [v]
                        srm[n] = v

                    proj_feat(4, (HH, HL), 256, 512, evr, [hm])
                    hfree = PE.last()
                    om = []
                    for fp in range(4):
                        b, fr = bank()
                        PE.wait(fr, zm)
                        for k in range(2):
                            f = fp * 2 + k
                            for t in range(2):
                                p = tr(
                                    b[:, k * 256 + t * 128:k * 256 + t * 128 + 128],
                                    Z[:, t, f * 128:f * 128 + 128], ident[:])
                        t1, tf, ti = tmp()
                        for k in range(2):
                            f = fp * 2 + k
                            v = stt(t1[:, k * 256:k * 256 + 256], b[:, k * 256:k * 256 + 256],
                                    go[:, f % 2:f % 2 + 1], sr[:, f, :], ALU.mult, ALU.mult, p, tf, gom, srm[f])
                        release(b, v)
                        m = hi_lo(HH[:, fp * 2:fp * 2 + 2, 256:512], HL[:, fp * 2:fp * 2 + 2, 256:512],
                                  t1[:, :].rearrange("p (k n) -> p k n", k=2), v, hfree)
                        tmp_free[ti] = m
                        om.append(m)
                    fz4 = fence()
            ym = {}
            proj_tok((HH, HL), 8, [2, 3], 2, y_evac_for(ym, fz4), [om])
            return ylist(ym, [2, 3])

        def conv(li, hm, stack):
            fz = fence()
            BH = sb("c_bh", [128, 8, 512], F32R, stack)
            BL = sb("c_bl", [128, 8, 512], F32R, stack)
            cu = [sb(f"c_cu{i}", [128, 522], F32, stack) for i in range(2)]
            cv = [sb(f"c_cv{i}", [128, 512], F32, stack) for i in range(2)]
            cwr = sb("c_wr", [24, 128], F32, stack)
            cwc = sb("c_wc", [128, 24], F32, stack)
            mw = mload(cwr[:], A["conv_w_2"][0].rearrange("a (r p) -> (a r) p", p=128), fz)
            b, fr = bank()
            p = tr(b[:, 0:24], cwr[:], ident[0:24, 0:24], fr, mw)
            cwm = cp(cwc[:], b[:, 0:24], p, fz)
            release(b, cwm)
            cz = [mset(cu[i][:], 0.0, fz) for i in range(2)]
            cufree = [None, None]
            cvfree = [None, None]
            om = []

            def view(i, sft, seg):
                if seg == 0:
                    return cu[i][:, 1 + sft:257 + sft]
                return cu[i][:, 258:522].rearrange("p (r n) -> p r n", r=4)[:, :, 1 + sft:65 + sft]

            for g in range(4):
                got = {}

                def ev(part):
                    def f(n, b, p):
                        d = g * 2 + n
                        i = n
                        if part == "c":
                            got[("c", i)] = act(cv[i][:], b[:, :], ACT.Copy, p, fz, cvfree[i])
                            release(b, got[("c", i)])
                        elif part == "u":
                            m = tt(view(i, 0, 0), b[:, 0:256], cv[i][:, 0:256], ALU.mult, p, got[("c", i)], cz,
                                   cufree[i])
                            m = tt(view(i, 0, 1), b[:, 256:512].rearrange("p (r n) -> p r n", r=4),
                                   cv[i][:, 256:512].rearrange("p (r n) -> p r n", r=4), ALU.mult)
                            release(b, m)
                            for seg in range(2):
                                o = cv[i][:, seg * 256:seg * 256 + 256]
                                if seg:
                                    o = o.rearrange("p (r n) -> p r n", r=4)
                                m = ts(o, view(i, -1, seg), cwc[:, d:d + 1], None, ALU.mult, None, m, cwm)
                                m = stt(o, view(i, 0, seg), cwc[:, 8 + d:9 + d], o, ALU.mult, ALU.add, m)
                                m = stt(o, view(i, 1, seg), cwc[:, 16 + d:17 + d], o, ALU.mult, ALU.add, m)
                            cufree[i] = m
                            got[("y", i)] = m
                        else:
                            m = tt(cv[i][:], cv[i][:], b[:, :], ALU.mult, p, got[("y", i)])
                            release(b, m)
                            m = hi_lo(BH[:, d, :], BL[:, d, :], cv[i][:], m, fz)
                            cvfree[i] = m
                            om.append(m)
                    return f

                proj_feat(1, (HH, HL), 0, 512, ev("c"), [hm])
                proj_feat(1, (HH, HL), 0, 512, ev("u"), [hm])
                proj_feat(1, (HH, HL), 0, 512, ev("b"), [hm])
            ym = {}
            proj_tok((BH, BL), 8, [0, 1, 2, 3], 2, y_evac_for(ym, fz), [om])
            return ylist(ym, [0, 1, 2, 3])

        def mlstm(li, hm, stack):
            fz = fence()
            ac_ = [Y[:, r * 2064:(r + 1) * 2064].rearrange("p (t h n) -> p t h n", t=2, h=8) for r in range(2)]
            with ExitStack() as s1:
                msk = sb("m_msk", [128, 2, 2, 256], F32, s1)
                mmk = mload(msk[:].rearrange("p a b n -> p (a b n)"), cap("mmask"), fz)
                sel = sb("m_sel", [8, 8, 128], F32, s1)
                msl = mload(sel[:].rearrange("p a n -> p (a n)"), cap("sel")[0:8, :], fz)
                qT = sb("m_qT", [128, 4, 256], F32, s1)
                kT = sb("m_kT", [128, 4, 256], F32, s1)
                VLe = sb("m_vl", [128, 2, 8, 129], F32, s1)
                C = sb("m_C", [128, 2, 4, 129], F32, s1)
                M = sb("m_M", [8, 2, 256], F32, s1)
                cols = sb("m_cols", [128, 2, 8, 8], F32, s1)
                on = mset(VLe[:, :, :, 128:129], 1.0, fz)
                with ExitStack() as s2:
                    KC = sb("m_kc", [128, 2, 512], F32, s2)
                    KW = sb("m_kw", [128, 2, 512], F32, s2)
                    VCe = sb("m_vc", [128, 2, 8, 129], F32, s2)
                    gt = sb("m_gt", [128, 4, 2, 16], F32, s2)
                    gbi = sb("m_gb", [128, 32], F32, s2)
                    f_a = sb("m_fa", [128, 4, 2, 8], F32, s2)
                    rw = sb("m_rw", [8, 5, 256], F32, s2)
                    o8 = sb("m_o8", [8, 256], F32, s2)
                    sm = sb("m_sm", [8, 2, 4], F32, s2)
                    mo8 = mset(o8[:], 1.0, fz)
                    on2 = mset(VCe[:, :, :, 128:129], 1.0, fz)
                    mgb = mload(gbi[:], A["ml_b_if_2"][0].rearrange("r g -> (r g)").partition_broadcast(128), fz)
                    b, fr = bank()
                    PE.wait(fr)
                    for r in range(2):
                        k, wh, wl, wm = take()
                        for t in range(4):
                            for q in range(8):
                                c = t * 128
                                p = mm3(b[:, r * 64 + t * 16:r * 64 + t * 16 + 16],
                                        (HH[:, q, c:c + 128], HL[:, q, c:c + 128]), (wh[:, q, :], wl[:, q, :]),
                                        q == 0, q == 7, (wm, hm), inc=(q == 7))
                        gave(k, p)
                    bv = b[:, 0:128].rearrange("p (r t g) -> p r t g", r=2, t=4)
                    for r in range(2):
                        v = tt(gt[:, :, r, :], bv[:, r, :, :],
                               gbi[:, r * 16:r * 16 + 16].unsqueeze(1).to_broadcast([128, 4, 16]), ALU.add, p, mgb, fz)
                    release(b, v)
                    fv = gt[:, :, :, 8:16]
                    a = act(f_a[:], fv, ACT.Abs, v, fz)
                    a = act(f_a[:], f_a[:], ACT.Exp, a, scale=-1.0)
                    a = act(f_a[:], f_a[:], ACT.Ln, a, bias=ones[:, 0:1])
                    v5 = ts(fv, fv, 0.0, None, ALU.min, None, v, a)
                    gtm = tt(fv, fv, f_a[:], ALU.subtract, v5, a)
                    km, vm = {}, {}

                    def evk(nh, t, b, p):
                        km[t] = copy_out(KC[:, t, :], b[:, :], p, fz)
                        release(b, km[t])

                    def evv(nh, t, b, p):
                        dst = (VCe[:, t, :, :] if t < 2 else VLe[:, t - 2, :, :])[:, nh * 4:nh * 4 + 4, 0:128]
                        vm[(t, nh)] = copy_out(dst, b[:, :].rearrange("p (h n) -> p h n", h=4), p, fz)
                        release(b, vm[(t, nh)])

                    proj_tok((HH, HL), 8, [0, 1], 1, evk, [hm])
                    rowm = {}
                    cm = []
                    for r in range(2):
                        bi, fri = bank()
                        bf, frf = bank()
                        PE.wait(fri, frf, gtm)
                        for t in range(4):
                            tr(bi[0:8, t * 128:t * 128 + 128],
                                                                       gt[:, t, r, 0:8], ident[:])
                            p = tr(bf[0:8, t * 128:t * 128 + 128],
                                                                           gt[:, t, r, 8:16], ident[:])
                        rv = (lambda x: x) if r == 0 else (lambda x: x[:, ::-1])
                        B, AA, WK = rw[:, 0, :], rw[:, 1, :], rw[:, 2, :]
                        prevc = cm[-1] if cm else None
                        v = scan(
                            rv(B), o8[:], rv(bf[0:8, 0:256]), 0.0, ALU.mult, ALU.add, p, mo8, fz, prevc)
                        v = tt(AA, bi[0:8, 0:256], B, ALU.subtract, v, p, prevc)
                        v = rmax(sm[:, r, 0:1], AA, AX.X, v)
                        v = ts(sm[:, r, 1:2], sm[:, r, 0:1], 0.0, -1.0, ALU.max, ALU.mult, v)
                        a = act(WK, AA, ACT.Exp, v, prevc, bias=sm[:, r, 1:2])
                        last = 255 if r == 0 else 0
                        mi = tt(sm[:, r, 2:3], B[:, last:last + 1], sm[:, r, 1:2], ALU.subtract, v)
                        BL_, AL_, WI, EM = rw[:, 3, :], rw[:, 4, :], rw[:, 0, :], rw[:, 1, :]
                        v = scan(
                            rv(BL_), o8[:], rv(bf[0:8, 256:512]), 0.0, ALU.mult, ALU.add, p, prevc)
                        release(bf, v)
                        v = tt(AL_, bi[0:8, 256:512], BL_, ALU.subtract, v)
                        release(bi, v)
                        MR = M[:, r, :]
                        v = scan(
                            rv(MR), rv(AL_), rv(AL_), sm[:, r, 2:3], ALU.max, ALU.max, v, mi)
                        rowm[r] = v
                        a2 = act(WI, MR, ACT.Exp, v, mi, prevc, scale=-1.0, bias=sm[:, r, 2:3])
                        v = tt(EM, BL_, MR, ALU.add, v, a)
                        a3 = act(EM, EM, ACT.Exp, v, scale=-1.0)
                        b, fr = bank()
                        PE.wait(fr, a, a2, a3)
                        for n, row in enumerate((WK, AL_, WI, EM)):
                            for t in range(2):
                                p = tr(
                                    b[:, (n * 2 + t) * 8:(n * 2 + t) * 8 + 8], row[:, t * 128:t * 128 + 128],
                                    ident[0:8, 0:8])
                        v = cp(cols[:, r, :, :].rearrange("p a h -> p (a h)"),
                                                                    b[:, 0:64], p, fz)
                        release(b, v)
                        cm.append([v, p])
                    proj_tok((HH, HL), 8, [0, 1, 2, 3], 2, evv, [hm])
                    Cm = {}
                    prev = None
                    for r in range(2):
                        kw = []
                        for t in range(2):
                            kw.append(tt(KW[:, t, :].rearrange("p (h n) -> p h n", h=8),
                                         KC[:, t, :].rearrange("p (h n) -> p h n", h=8),
                                         cols[:, r, t, :].unsqueeze(2).to_broadcast([128, 8, 64]), ALU.mult,
                                         km[t], cm[r], prev, fz))
                        for g2 in range(2):
                            b, fr = bank()
                            PE.wait(fr, kw, on2, list(vm.values()))
                            for pi in range(2):
                                for par in range(2):
                                    h = (g2 * 2 + pi) * 2 + par
                                    for t in range(2):
                                        p = mm(b[par * 64:par * 64 + 64, pi * 129:pi * 129 + 129],
                                               KW[:, t, h * 64:h * 64 + 64], VCe[:, t, h, :], t == 0, t == 1, inc=True)
                            Cm[(r, g2)] = copy_out(C[:, r, g2 * 2:g2 * 2 + 2, :],
                                                   b[:, 0:258].rearrange("p (h n) -> p h n", h=2), p, fz)
                            release(b, Cm[(r, g2)])
                        prev = p
                    fz2 = fence()
                qm, ktm = {}, {}

                def evq(n, b, p):
                    qm[n] = act(qT[:, n, :], b[:, 0:256], ACT.Copy, p, fz, scale=0.125)
                    release(b, qm[n])

                def evkt(n, b, p):
                    ktm[n] = cp(kT[:, n, :], b[:, 0:256], p, fz)
                    release(b, ktm[n])

                proj_feat(2, (HH, HL), 256, 512, evq, [hm])
                proj_feat(2, (HH, HL), 256, 512, evkt, [hm])
                with ExitStack() as s2:
                    DD = [sb(f"m_D{i}", [128, 2, 256], F32, s2) for i in range(2)]
                    SS = [sb(f"m_S{i}", [128, 2, 256], F32, s2) for i in range(2)]
                    TI = [sb(f"m_T{i}", [128, 2, 129], F32, s2) for i in range(2)]
                    dfree, sfree2, tfree = [[fz2], [fz2]], [[fz2], [fz2]], [[fz2], [fz2]]
                    am = {}
                    steps = [(h, r) for h in range(8) for r in range(2)]
                    sbk = {}

                    def front(h, r):
                        base = (h % 2) * 64
                        pr = h // 2
                        i = (h * 2 + r) % 2
                        if r == 0:
                            b, fr = bank()
                            PE.wait(fr, qm[pr], ktm[pr])
                            for s_ in range(2):
                                p = mm(b[:, s_ * 256:s_ * 256 + 256], kT[base:base + 64, pr, s_ * 128:s_ * 128 + 128],
                                       qT[base:base + 64, pr, :], True, True, inc=True)
                            sbk[h] = (b, p)
                        b, fr = bank()
                        p = mm(b[:, 0:256], sel[:, h, :], M[:, r, :], True, True, (fr, rowm[r], msl), inc=True)
                        v = stt(DD[i][:], b[:, 0:256].unsqueeze(1).to_broadcast([128, 2, 256]), -1.0, msk[:, r, :, :],
                                ALU.mult, ALU.add, p, mmk, dfree[i])
                        release(b, v)
                        for s_ in range(2):
                            a = act(DD[i][:, s_, :], DD[i][:, s_, :], ACT.Exp, v, cm[r][0],
                                    bias=cols[:, r, 2 + s_, h:h + 1])
                        sb_, sp_ = sbk[h]
                        v = tt(SS[i][:], sb_[:, :].rearrange("p (s n) -> p s n", s=2), DD[i][:], ALU.mult, a, sp_,
                               sfree2[i])
                        dfree[i] = [v]
                        if r == 1:
                            release(sb_, v)
                        return v

                    def back(h, r, v):
                        base = (h % 2) * 64
                        pr = h // 2
                        i = (h * 2 + r) % 2
                        b1, fr1 = bank()
                        b2, fr2 = bank()
                        PE.wait(fr1, fr2, v, on, vm[(2, h // 4)], vm[(3, h // 4)], Cm[(r, pr // 2)])
                        for t in range(2):
                            p2 = mm(b2[:, t * 129:t * 129 + 129], qT[base:base + 64, pr, t * 128:t * 128 + 128],
                                    C[base:base + 64, r, pr, :], True, True, inc=True)
                        for t in range(2):
                            ss_ = [q for q in range(2) if (q <= t if r == 0 else q >= t)]
                            for n, q in enumerate(ss_):
                                p1 = mm(b1[:, t * 129:t * 129 + 129], SS[i][:, q, t * 128:t * 128 + 128],
                                        VLe[:, q, h, :], n == 0, n == len(ss_) - 1, inc=True)
                        for t in range(2):
                            a = act(TI[i][:, t, :], b2[:, t * 129:t * 129 + 129], ACT.Copy, p2, tfree[i], cm[r][0],
                                    scale=cols[:, r, 4 + t, h:h + 1])
                        release(b2, a)
                        sfree2[i] = [p1]
                        v = tt(ac_[r][:, :, h, :], b1[:, 0:258].rearrange("p (t n) -> p t n", t=2), TI[i][:], ALU.add,
                               p1, a, fz)
                        release(b1, v)
                        tfree[i] = [v]
                        am[(h, r)] = v

                    pend = None
                    for h, r in steps:
                        v = front(h, r)
                        if pend is not None:
                            back(*pend)
                        pend = (h, r, v)
                    back(*pend)
                    den = sb("m_den", [128, 2, 16], F32, s2)
                    for r in range(2):
                        dv = den[:, r, :].rearrange("p (t h) -> p t h", t=2)
                        m = stt(dv, ac_[r][:, :, :, 128], -1.0, ac_[r][:, :, :, 128], ALU.mult, ALU.max, am[(7, r)], fz2)
                        m = tt(dv, dv, cols[:, r, 6:8, :], ALU.max, m)
                        m = rcp(den[:, r, :], den[:, r, :], m)
                        for t in range(2):
                            o = ac_[r][:, t, :, 0:128]
                            m2 = tt(o, o, den[:, r, t * 8:t * 8 + 8].unsqueeze(2).to_broadcast([128, 8, 128]),
                                    ALU.mult, m)
                    hsm = []
                    for t in range(2):
                        o = ac_[0][:, t, :, 0:128]
                        hsm.append(tt(o, o, ac_[1][:, t, :, 0:128], ALU.add, m2))
                    s = stats()
                    for t in range(2):
                        sq = ac_[1][:, t, :, 0:128]
                        o = ac_[0][:, t, :, 0:128]
                        m = tt(sq, o, o, ALU.mult, hsm[t])
                        m = rsum(s[:, 0, t * 8:t * 8 + 8], sq, AX.X, m)
                    r_, rm = rstd(s, 16, 128, [m])
                    hz = []
                    for t in range(2):
                        o = ac_[0][:, t, :, 0:128]
                        hz.append(tt(o, o, r_[:, t * 8:t * 8 + 8].unsqueeze(2).to_broadcast([128, 8, 128]), ALU.mult,
                                     rm, hsm[t]))
                    fz3 = fence()
            with ExitStack() as s1:
                so = sb("m_so", [128, 8, 256], F32, s1)
                nwr = sb("m_nwr", [8, 128], F32, s1)
                nwc = sb("m_nwc", [128, 8], F32, s1)
                mg = mload(nwr[:], A["ml_norm_w_2"][0].rearrange("(r p) -> r p", p=128), fz3)
                b, fr = bank()
                p = tr(b[:, 0:8], nwr[:], ident[0:8, 0:8], fr, mg)
                nwm = cp(nwc[:], b[:, 0:8], p, fz3)
                release(b, nwm)
                som = {}

                def evo(n, b, p):
                    t1, tf, ti = tmp()
                    a = act(t1[:, 0:256], b[:, 0:256], ACT.Exp, p, tf, scale=-1.0)
                    release(b, a)
                    v = ts(t1[:, 0:256], t1[:, 0:256], 1.0, None, ALU.add, None, a)
                    v = rcp(so[:, n, :], t1[:, 0:256], v, fz3)
                    tmp_free[ti] = [v]
                    som[n] = v

                proj_feat(4, (HH, HL), 256, 512, evo, [hm])
                hfree = PE.last()
                om = []
                for fp in range(4):
                    b, fr = bank()
                    PE.wait(fr, hz)
                    for k in range(2):
                        f = fp * 2 + k
                        for t in range(2):
                            p = tr(
                                b[:, k * 256 + t * 128:k * 256 + t * 128 + 128], ac_[0][:, t, f, 0:128], ident[:])
                    t1, tf, ti = tmp()
                    for k in range(2):
                        f = fp * 2 + k
                        v = stt(t1[:, k * 256:k * 256 + 256], b[:, k * 256:k * 256 + 256], nwc[:, f:f + 1], so[:, f, :],
                                ALU.mult, ALU.mult, p, tf, nwm, som[f])
                    release(b, v)
                    m = hi_lo(HH[:, fp * 2:fp * 2 + 2, 256:512], HL[:, fp * 2:fp * 2 + 2, 256:512],
                              t1[:, :].rearrange("p (k n) -> p k n", k=2), v, hfree)
                    tmp_free[ti] = m
                    om.append(m)
                fz4 = fence()
            ym = {}
            proj_tok((HH, HL), 8, [2, 3], 2, y_evac_for(ym, fz4), [om])
            return ylist(ym, [2, 3])

        mixers = [mla, gla, conv, mlstm]
        xm = {t: d_x[t] for t in range(4)}
        yfree = None
        for li in range(4):
            both = LAYERS[li]["both"]
            tiles = [0, 1, 2, 3] if both else [2, 3]
            halves = [0, 1]
            if li == 2:
                z = PE.last()
                for t in range(2):
                    xm[t] = mload(X[:, t, :], A["ctx_2"][t * 128:t * 128 + 128, :], fence(), q=PO)
            PUMP[0] = 1
            hm = make_h(li, 0, halves, xm, [PE.last()], fence())
            for part in (0, 1, 3, 4, 2):
                allow.add((li, part))
            with ExitStack() as ls:
                ym = mixers[li](li, hm, ls)
            xn, last = combine(li, 2, tiles, ym)
            xm.update(xn)
            hm = make_h(li, 1, [0, 1] if both else [1], xm, [PE.last()], fence())
            allow.add((li, 5))
            if li < 3:
                for part in (0, 1, 3, 4):
                    allow.add((li + 1, part))
            with ExitStack() as ls:
                ym = mlp(li, tiles, hm, ls)
            xn, last = combine(li, 5, tiles, ym)
            xm.update(xn)
        assert w_at[0] == len(WL) and not bg
        outs = []
        for t in range(2):
            outs.append(mload(out[t * 128:t * 128 + 128, :], X[:, 2 + t, :], xm[2 + t], q=SP))
        SP.wait(*outs)

        block = ctx.enter_context(nc.Block())

        @block.sync
        def _(e):
            SP.play(e)

        @block.gpsimd
        def _(e):
            PO.play(e)

        @block.scalar
        def _(e):
            AC.play(e)

        @block.vector
        def _(e):
            DV.play(e)

        @block.tensor
        def _(e):
            PE.play(e)


_INS = ['x', 'c', 'ctx', 'c_ctx', 'ada_w', 'ada_b', 'norm_g', 'mlp_w1', 'mlp_w2', 'mla_w_dq', 'mla_g_q', 'mla_w_uq',
        'mla_w_dkv', 'mla_g_kv', 'mla_w_ukv', 'mla_w_o', 'gla_w_q', 'gla_w_k', 'gla_w_v', 'gla_w_r', 'gla_w_gate1',
        'gla_w_gate2', 'gla_b_gate', 'gla_g_o', 'gla_w_o', 'c_2', 'ctx_2', 'c_ctx_2', 'norm_w_2', 'mod_w_2', 'mod_b_2',
        'mlp_w1_2', 'mlp_w2_2', 'conv_w_in_2', 'conv_w_2', 'conv_w_out_2', 'ml_w_qkvo_2', 'ml_w_if_2', 'ml_b_if_2',
        'ml_norm_w_2', 'ml_w_out_2']


def kernel(**inputs):
    import numpy as _np
    import concourse.bacc as _bacc
    from concourse import mybir as _mybir
    from concourse.bass_utils import run_bass_kernel_spmd as _run

    nc = _bacc.Bacc("TRN2", target_bir_lowering=False, num_devices=1)
    arrays, aps = {}, {}
    for name in _INS:
        a = _np.ascontiguousarray(inputs[name])
        if name in ("x", "ctx", "ctx_2"):
            a = a.reshape(256, 1024)
        if name in ("c", "c_ctx", "c_2", "c_ctx_2"):
            a = a.reshape(8, 128)
        arrays[f"in_{name}"] = a
        aps[name] = nc.dram_tensor(f"in_{name}", a.shape, _mybir.dt.from_np(a.dtype), kind="ExternalInput").ap()
    arrays["in_consts"] = CONSTS
    aps["consts"] = nc.dram_tensor("in_consts", CONSTS.shape, _mybir.dt.float32, kind="ExternalInput").ap()
    o = nc.dram_tensor("out_0", (256, 1024), _mybir.dt.float32, kind="ExternalOutput").ap()
    build(nc, aps, o)
    r = _run(nc, [arrays], core_ids=[0])
    return r.results[0]["out_0"].reshape(1, 256, 1024)
```

```python
from contextlib import ExitStack

import numpy as np

import concourse.bass as bass
from concourse import mybir

F32 = mybir.dt.float32
F32R = mybir.dt.float32r
I32 = mybir.dt.int32
ALU = mybir.AluOpType
ACT = mybir.ActivationFunctionType
AX = mybir.AxisListType

D = 1024
FF = 4096
EPS = 1e-6
NRAW = 3
NSPL = 4
NADA = 3
NTMP = 3

CONST_SLICES = {}


def const_table():
    parts = []
    at = [0]

    def add(name, a):
        full = np.zeros((128, a.shape[1]), np.float32)
        full[:a.shape[0]] = a
        CONST_SLICES[name] = (at[0], a.shape[1])
        at[0] += a.shape[1]
        parts.append(full)

    j = np.arange(128)[:, None]
    i = np.arange(128)[None, :]
    same = (j // 64) == (i // 64)
    add("ident", np.eye(128, dtype=np.float32))
    add("ones", np.ones((128, 128), np.float32))
    s = 1.0 / 16.0
    add("cum", np.concatenate([(same & (j <= i)) * s, (same & (j >= i)) * s], 1).astype(np.float32))
    add("end", np.concatenate([(same & (j > i)) * s, (same & (j < i)) * s], 1).astype(np.float32))
    add("endc", np.concatenate([(j > i) * s, (j < i) * s], 1).astype(np.float32))
    add("sum", np.full((128, 128), s, np.float32))
    add("gmask", np.concatenate([same & (j <= i), same & (j >= i)], 1).astype(np.float32))
    t = np.arange(256)[None, :]
    p = np.arange(128)[:, None]
    neg = np.float32(-1e30)
    mf = [np.where(p + 128 * q <= t, np.float32(0), neg) for q in range(2)]
    mb = [np.where(p + 128 * q >= t, np.float32(0), neg) for q in range(2)]
    add("mmask", np.concatenate(mf + mb, 1).astype(np.float32))
    sel = np.zeros((8, 8, 128), np.float32)
    for h in range(8):
        sel[h, h, :] = 1.0
    add("sel", sel.reshape(8, 1024))
    rot = np.zeros((64, 64), np.float32)
    for base in (0, 32):
        for q in range(16):
            rot[base + q + 16, base + q] = -1.0
            rot[base + q, base + q + 16] = 1.0
    add("rot", rot)
    half = 32
    inv = (np.float32(10000.0) ** (-np.arange(0, half, 2, dtype=np.float32) / np.float32(half))).astype(np.float32)
    row = np.repeat(np.arange(4, dtype=np.float32), 64)
    col = np.tile(np.arange(64, dtype=np.float32), 4)
    ar = (row[None, :] * inv[:, None]).astype(np.float32)
    ac = (col[None, :] * inv[:, None]).astype(np.float32)
    ang = np.concatenate([ar, ar, ac, ac], 0)
    add("cos", np.cos(ang).astype(np.float32))
    add("sin", np.sin(ang).astype(np.float32))
    return np.ascontiguousarray(np.concatenate(parts, 1))


CONSTS = const_table()


class Queue:

    def __init__(self, sem):
        self.sem = sem
        self.n = 0
        self.ops = []
        self.seen = {}

    def wait(self, *marks):
        for m in marks:
            if m is None or len(m) == 0:
                continue
            if isinstance(m, list) or not isinstance(m[0], int):
                self.wait(*m)
                continue
            key, sem, v = m
            if self.seen.get(key, 0) >= v:
                continue
            self.seen[key] = v
            self.ops.append(lambda e, sem=sem, v=v: e.wait_ge(sem, v))

    def do(self, fn, *marks, inc=True):
        self.wait(*marks)
        if inc:
            self.n += 1
            self.ops.append(lambda e: fn(e).then_inc(self.sem, 1))
            return (id(self), self.sem, self.n)
        self.ops.append(fn)
        return None

    def last(self):
        return (id(self), self.sem, self.n) if self.n else None

    def play(self, e):
        for op in self.ops:
            op(e)


class Slot:

    def __init__(self, ap, sem):
        self.ap = ap
        self.sem = sem
        self.n = 0
        self.free = []

    def load(self, q, dst, src, *marks):
        q.wait(self.free, *marks)
        self.n += 16
        sem = self.sem
        q.ops.append(lambda e: e.dma_start(dst, src).then_inc(sem, 16))
        return (id(self), sem, self.n)


def build(nc, A, out):
    ctx = ExitStack()
    with ctx:
        def sb(name, shape, dt=F32, stack=ctx):
            return stack.enter_context(nc.sbuf_tensor(name, shape, dt))

        def semf(name):
            return ctx.enter_context(nc.semaphore(name))

        banks = [ctx.enter_context(nc.psum_tensor(f"bank{i}", [128, 512], F32)) for i in range(8)]
        PE, AC, DV, PO, SP = (Queue(semf(n)) for n in ("s_pe", "s_act", "s_dve", "s_pool", "s_sp"))

        free_banks = [(b, []) for b in banks]

        def bank():
            b, marks = free_banks.pop(0)
            return b, list(marks)

        def release(b, *marks):
            free_banks.append((b, [m for m in marks]))

        X = sb("X", [128, 4, D])
        HH = sb("HH", [128, 8, 512], F32R)
        HL = sb("HL", [128, 8, 512], F32R)
        Y = sb("Y", [128, 4224])
        Y4 = Y[:, 0:4096].rearrange("p (t n) -> p t n", t=4)
        G = sb("G", [128, 2, D])
        raws = [Slot(sb(f"raw{i}", [128, 1024]), semf(f"s_raw{i}")) for i in range(NRAW)]
        spl = [(sb(f"wh{i}", [128, 1024], F32R), sb(f"wl{i}", [128, 1024], F32R)) for i in range(NSPL)]
        spl_free = [None] * NSPL
        adas = [Slot(sb(f"ada{i}", [128, 2, 512]), semf(f"s_ada{i}")) for i in range(NADA)]
        acc = sb("acc", [128, 2, 2, 512])
        gb = Slot(sb("gb", [128, 2, 512]), semf("s_gb"))
        ident = sb("ident", [128, 128])
        ones = sb("ones", [128, 128])
        tmps = [sb(f"tmp{i}", [128, 512]) for i in range(NTMP)]
        tmp_free = [[] for _ in range(NTMP)]
        tmp_n = [0]
        sc = sb("sc", [128, 4, 8])
        bgc = sb("bgc", [128, 2, 80])
        mod = sb("mod", [128, 2, 4, 2, 8])

        def tmp():
            i = tmp_n[0] % NTMP
            tmp_n[0] += 1
            return tmps[i], list(tmp_free[i]), i

        def fence():
            return [q.last() for q in (PE, AC, DV, PO)]

        def cap(name):
            a, n = CONST_SLICES[name]
            return A["consts"][:, a:a + n]

        def mload(dst, src, *marks, q=PO):
            return misc_load(q, dst, src, marks)

        misc_slots = {id(q): [Slot(None, semf(f"s_m{j}_{i}")) for i in range(10)] for j, q in enumerate((SP, PO))}
        misc_n = {id(SP): 0, id(PO): 0}

        def misc_load(q, dst, src, marks):
            sl = misc_slots[id(q)][misc_n[id(q)] % 10]
            misc_n[id(q)] += 1
            if sl.n:
                q.wait((id(sl), sl.sem, sl.n))
            return sl.load(q, dst, src, *marks)

        def tr(o, i, idn, *marks, inc=True):
            return PE.do(lambda e: e.transpose(o, i, idn), *marks, inc=inc)

        def cp(o, i, *marks):
            return DV.do(lambda e: e.tensor_copy(o, i), *marks)

        def rcp(o, i, *marks):
            return DV.do(lambda e: e.reciprocal(o, i), *marks)

        def rmax(o, i, ax, *marks):
            return DV.do(lambda e: e.reduce_max(o, i, ax), *marks)

        def rsum(o, i, ax, *marks):
            return DV.do(lambda e: e.reduce_sum(o, i, ax), *marks)

        def mset(o, v, *marks):
            return DV.do(lambda e: e.memset(o, v), *marks)

        def scan(o, a, b_, init, op0, op1, *marks):
            return DV.do(lambda e: e.tensor_tensor_scan(o, a, b_, init, op0, op1), *marks)

        def cpred(o, m, i, *marks):
            return DV.do(lambda e: e.copy_predicated(o, m, i), *marks)

        def act(o, i, f, *marks, **kw):
            return AC.do(lambda e: e.activation(o, i, f, **kw), *marks)

        def tt(o, a, b_, op, *marks, q=DV):
            return q.do(lambda e: e.tensor_tensor(o, a, b_, op), *marks)

        def ts(o, a, s1, s2, op0, op1, *marks, q=DV):
            if op1 is None:
                return q.do(lambda e: e.tensor_scalar(o, a, s1, None, op0), *marks)
            return q.do(lambda e: e.tensor_scalar(o, a, s1, s2, op0, op1), *marks)

        def stt(o, a, s, b_, op0, op1, *marks):
            return DV.do(lambda e: e.scalar_tensor_tensor(out=o, in0=a, scalar=s, in1=b_, op0=op0, op1=op1), *marks)

        d_id = mload(ident[:], cap("ident"), q=SP)
        junk = sb("junk", [128, 1024], mybir.dt.bfloat16)
        junk_mark = [None]
        ysq = sb("ysq", [128, 8])
        crow = Y[0:8, 0:512].rearrange("p (i n) -> p i n", i=4)
        d_c = [mload(crow[:, i, :], A[n], q=SP) for i, n in enumerate(("c_ctx", "c", "c_ctx_2", "c_2"))]
        d_on = mload(ones[:], cap("ones"))
        d_x = [None] * 4

        b, fr = bank()
        for i in range(4):
            pt = tr(b[:, 8 * i:8 * i + 8], crow[:, i, :], ident[0:8, 0:8],
                       fr, d_id, d_c[i])
        t1, tf, ti = tmp()
        a1 = act(t1[:, 0:32], b[:, 0:32], ACT.Exp, pt, tf, scale=-1.0)
        v1 = ts(t1[:, 32:64], t1[:, 0:32], 1.0, None, ALU.add, None, a1)
        v2 = rcp(t1[:, 64:96], t1[:, 32:64], v1)
        scd = tt(sc[:].rearrange("p a k -> p (a k)"), b[:, 0:32], t1[:, 64:96], ALU.mult, v2)
        tmp_free[ti] = [scd]
        release(b, scd)

        LAYERS = [
            dict(w=A["ada_w"][0], bia=A["ada_b"][0], g=A["norm_g"][0], c=0, both=True, w1=A["mlp_w1"][0], w2=A["mlp_w2"][0]),
            dict(w=A["ada_w"][1], bia=A["ada_b"][1], g=A["norm_g"][1], c=0, both=False, w1=A["mlp_w1"][1], w2=A["mlp_w2"][1]),
            dict(w=A["mod_w_2"][0], bia=A["mod_b_2"][0], g=A["norm_w_2"][0], c=2, both=True, w1=A["mlp_w1_2"][0], w2=A["mlp_w2_2"][0]),
            dict(w=A["mod_w_2"][1], bia=A["mod_b_2"][1], g=A["norm_w_2"][1], c=2, both=False, w1=A["mlp_w1_2"][1], w2=A["mlp_w2_2"][1]),
        ]

        def feat(W, c0, ncols, rows=D):
            for cb in range(c0, c0 + ncols, 256):
                for kk in range(0, rows, 512):
                    yield W[kk:kk + 512, cb:cb + 256].rearrange("(k p) n -> p k n", p=128)

        def tokw(W, r0, rows, c0, ncols):
            for cb in range(c0, c0 + ncols, 512):
                for kk in range(r0, r0 + rows, 256):
                    yield W[kk:kk + 256, cb:cb + 512].rearrange("(k p) n -> p k n", p=128)

        def mlp_stream(L):
            for q in range(4):
                yield from feat(L["w1"], q * 1024, 1024)
                yield from tokw(L["w2"], q * 1024, 1024, 0, 1024)

        def stream():
            for k in range(0, D, 256):
                yield A["mla_w_dq"][0][k:k + 256, :].rearrange("(k p) n -> p k n", p=128)
            for k in range(0, D, 256):
                yield A["mla_w_dkv"][0][k:k + 256, :].rearrange("(k p) n -> p k n", p=128)
            for h in range(8):
                yield A["mla_w_uq"][0][:, h * 192:(h + 1) * 192].rearrange("(k p) n -> p k n", p=128)
                yield A["mla_w_ukv"][0][:, h * 256:(h + 1) * 256].rearrange("(k p) n -> p k n", p=128)
            yield from tokw(A["mla_w_o"][0], 0, D, 0, D)
            yield from mlp_stream(LAYERS[0])
            for r in range(2):
                yield A["gla_w_gate1"][0, r].rearrange("(k p) n -> p k n", p=128)
            yield from tokw(A["gla_w_k"][0], 0, D, 0, 512)
            yield from tokw(A["gla_w_v"][0], 0, D, 0, 1024)
            yield from feat(A["gla_w_q"][0], 0, 512)
            yield from feat(A["gla_w_r"][0], 0, 1024)
            yield from tokw(A["gla_w_o"][0], 0, D, 0, D)
            yield from mlp_stream(LAYERS[1])
            W = A["conv_w_in_2"][0]
            for c in range(0, D, 256):
                yield from feat(W, D + c, 256)
                yield from feat(W, 2 * D + c, 256)
                yield from feat(W, c, 256)
            yield from tokw(A["conv_w_out_2"][0], 0, D, 0, D)
            yield from mlp_stream(LAYERS[2])
            W = A["ml_w_qkvo_2"][0]
            for r in range(2):
                yield A["ml_w_if_2"][0, r].rearrange("(k p) n -> p k n", p=128)
            yield from tokw(W, 0, D, 512, 512)
            yield from tokw(W, 0, D, 1024, 1024)
            yield from feat(W, 0, 512)
            yield from feat(W, 512, 512)
            yield from feat(W, 2048, 1024)
            yield from tokw(A["ml_w_out_2"][0], 0, D, 0, D)
            yield from mlp_stream(LAYERS[3])

        WL = list(stream())
        w_at = [0]
        w_split = [0]
        w_dma = [0]
        w_mark = {}
        w_done = {}
        w_raw = {}

        def shape2(ap):
            return ap.shape[1], ap.shape[2]

        def issue_dma():
            k = w_dma[0]
            if k >= len(WL):
                return
            sl = raws[k % NRAW]
            a, n = shape2(WL[k])
            w_raw[k] = sl.load(SP, sl.ap[:, 0:a * n].rearrange("p (a n) -> p a n", a=a), WL[k])
            w_dma[0] += 1

        def issue_split():
            k = w_split[0]
            if k >= len(WL):
                return
            while w_dma[0] <= k:
                issue_dma()
            sl = raws[k % NRAW]
            hi, lo = spl[k % NSPL]
            a, n = shape2(WL[k])
            m = a * n
            done = w_done[k - NSPL] if k >= NSPL else None
            r = sl.ap
            t1 = AC.do(lambda e: e.activation(hi[:, 0:m], r[:, 0:m], ACT.Copy), w_raw[k], done)
            t2 = DV.do(lambda e: e.tensor_tensor(lo[:, 0:m], r[:, 0:m], hi[:, 0:m].bitcast(F32), ALU.subtract),
                       w_raw[k], t1, done)
            sl.free = [t1, t2]
            w_mark[k] = [t1, t2]
            w_split[0] += 1
            issue_dma()

        bg = []
        bg_done = set()
        allow = set()
        closing = []
        RATE = [0.6]
        credit = [0.0]

        def step_bg():
            key, fn, close = bg.pop(0)
            fn()
            for c in closing:
                c[0] -= 1
            flush_bg(0)
            if close is not None:
                closing.append([3, key, close])

        def flush_bg(limit):
            while closing and closing[0][0] <= limit:
                _, key, fn = closing.pop(0)
                if fn():
                    bg_done.add(key)

        def pump():
            credit[0] += RATE[0]
            while credit[0] >= 1.0:
                credit[0] -= 1.0
                if bg and bg[0][0] in allow:
                    step_bg()
                else:
                    flush_bg(9)

        def ensure(key):
            allow.add(key)
            while key not in bg_done:
                if any(b_[0] == key for b_ in bg):
                    assert bg[0][0] in allow, (bg[0][0], key)
                    step_bg()
                else:
                    flush_bg(9)

        def take():
            k = w_at[0]
            while w_split[0] < min(k + NSPL, len(WL)):
                issue_split()
            w_at[0] += 1
            pump()
            hi, lo = spl[k % NSPL]
            a, n = shape2(WL[k])
            v = [x[:, 0:a * n].rearrange("p (a n) -> p a n", a=a) for x in (hi, lo)]
            return k, v[0], v[1], w_mark[k]

        def take4():
            k0 = w_at[0]
            while w_split[0] < k0 + NSPL:
                issue_split()
            w_at[0] += NSPL
            out_ = []
            for k in range(k0, k0 + NSPL):
                hi, lo = spl[k % NSPL]
                a, n = shape2(WL[k])
                out_.append((k, hi[:, 0:a * n].rearrange("p (a n) -> p a n", a=a),
                             lo[:, 0:a * n].rearrange("p (a n) -> p a n", a=a), w_mark[k]))
                pump()
            return out_

        def gave(k, mark):
            w_done[k] = mark

        def mm3(o, s, m, start, stop, marks=(), inc=False):
            PE.wait(*marks)
            sh, sl_ = s
            mh, ml = m
            PE.do(lambda e: e.matmul(o, sh, mh, start=start, stop=False, skip_group_check=True), inc=False)
            PE.do(lambda e: e.matmul(o, sh, ml, start=False, stop=False, skip_group_check=True), inc=False)
            return PE.do(lambda e: e.matmul(o, sl_, mh, start=False, stop=stop, skip_group_check=True), inc=inc)

        def mm(o, s, m, start, stop, marks=(), inc=False):
            PE.wait(*marks)
            return PE.do(lambda e: e.matmul(o, s, m, start=start, stop=stop, skip_group_check=True), inc=inc)

        ada_n = [0]
        acc_free = [[], []]
        acc_n = [0]
        G_free = [None]
        mod_mark = {}
        G_mark = {}

        def ada_prepare(li):
            L = LAYERS[li]
            t1, tf, ti = tmp()
            m1 = mload(t1[0:48, 0:128], L["bia"].rearrange("(r p) -> r p", p=128), tf)
            m2 = mload(t1[0:32, 128:256], L["g"].rearrange("a (r p) -> (a r) p", p=128), tf)
            b, fr = bank()
            tr(b[:, 0:48], t1[0:48, 0:128], ident[0:48, 0:48], fr, m1, d_id, inc=False)
            p = tr(b[:, 48:80], t1[0:32, 128:256], ident[0:32, 0:32], m2)
            v = cp(bgc[:, li % 2, :], b[:, 0:80], p)
            tmp_free[ti] = [p]
            release(b, v)
            mod_mark[(li, "bg")] = v

        def ada_units(li):
            L = LAYERS[li]
            W = L["w"]
            order = [0, 1, 3, 4, 2, 5]
            for part in order:
                types = [1] if (not L["both"] and part > 1) else [0, 1]
                key = (li, part)
                units = []
                if part == 0:
                    units.append((lambda li=li: ada_prepare(li), None))
                lead = li == 0 and part < 2
                for ch in range(1 if lead else 2):
                    state = {}

                    def load_slot(kk, part=part, ch=ch, state=state):
                        sl = adas[ada_n[0] % NADA]
                        ada_n[0] += 1
                        c0 = part * D + ch * 512
                        src = W[kk * 256:kk * 256 + 256, c0:c0 + 512].rearrange("(k p) n -> p k n", p=128)
                        m = sl.load(PO, sl.ap[:], src)
                        state[kk] = (sl, m)

                    def work(kk, state=state, types=types, L=L, load_slot=load_slot):
                        if kk == 0:
                            state["buf"] = acc_n[0] % 2
                            acc_n[0] += 1
                            load_slot(0)
                            load_slot(1)
                        bi = state["buf"]
                        sl, m = state[kk]
                        for k in range(2):
                            for ty in types:
                                o = acc[:, bi, ty, :]
                                cc = sc[:, L["c"] + ty, kk * 2 + k:kk * 2 + k + 1]
                                if kk == 0 and k == 0:
                                    mk = ts(o, sl.ap[:, k, :], cc, None, ALU.mult, None, m, scd, acc_free[bi])
                                else:
                                    mk = stt(o, sl.ap[:, k, :], cc, o, ALU.mult, ALU.add, m, state[("m", ty)])
                                state[("m", ty)] = mk
                        sl.free = [mk]
                        if kk + 2 < 4:
                            load_slot(kk + 2)


                    def finish(part=part, ch=ch, state=state, types=types, li=li, L=L, lead=lead):
                        bi = state["buf"]
                        marks = [state[("m", ty)] for ty in types]
                        if part in (2, 5):
                            gi = 1 if part == 2 else 3
                            src = L["bia"][part * D + ch * 512:part * D + ch * 512 + 512]
                            g1 = gb.load(PO, gb.ap[:, 0, :], src.partition_broadcast(128))
                            gb.free = []
                            g2 = gb.load(PO, gb.ap[:, 1, :], L["g"][gi][ch * 512:ch * 512 + 512].partition_broadcast(128))
                            for ty in types:
                                b, fr = bank()
                                p = mm(b[:, :], ones[:], acc[:, bi, ty, :], True, True, (fr, marks, d_on), inc=True)
                                o = G[:, ty, ch * 512:ch * 512 + 512]
                                v = tt(o, b[:, :], gb.ap[:, 0, :], ALU.add, p, g2, G_free[0])
                                release(b, v)
                                v = tt(o, o, gb.ap[:, 1, :], ALU.mult, v, g2)
                            gb.free = [v]
                            acc_free[bi] = [p]
                            G_mark[(li, part)] = v
                            return ch == 1
                        else:
                            pi = {0: 0, 1: 1, 3: 2, 4: 3}[part]
                            b, fr = bank()
                            PE.wait(fr, marks, d_on)
                            for n, ty in enumerate(types):
                                for mth in range(4):
                                    p = mm(b[:, n * 4 + mth:n * 4 + mth + 1], acc[:, bi, ty, mth * 128:mth * 128 + 128],
                                           ones[:, 0:1], True, True, inc=True)
                            acc_free[bi] = [p]
                            bc = bgc[:, li % 2, part * 8 + ch * 4:part * 8 + ch * 4 + 4]
                            gc0 = 48 + (0 if part == 1 else 2) * 8 + ch * 4
                            gc = bgc[:, li % 2, gc0:gc0 + 4]
                            for n, ty in enumerate(types):
                                o = mod[:, li % 2, pi, ty, ch * 4:ch * 4 + 4]
                                v = tt(o, b[:, n * 4:n * 4 + 4], bc, ALU.add, p, mod_mark[(li, "bg")])
                                if n == len(types) - 1:
                                    release(b, v)
                                if part in (1, 4):
                                    v = stt(o, o, 1.0, gc, ALU.add, ALU.mult, v)
                            mod_mark.setdefault((li, pi), []).append(v)
                            return ch == 1 or lead

                    for kk in range(4):
                        units.append((lambda kk=kk, work=work: work(kk), finish if kk == 3 else None))
                for u, close in units:
                    bg.append((key, u, close))

        for li in range(4):
            ada_units(li)

        def direct(part, lo_k):
            b, fr = bank()
            PE.wait(fr, scd)
            for kk in range(4):
                n = lo_k + kk
                sl = raws[n % NRAW]
                src = A["ada_w"][0][kk * 256:kk * 256 + 256, part * D + 512:part * D + 1024]
                v3 = sl.ap.rearrange("p (k n) -> p k n", k=2)
                m = sl.load(SP, v3, src.rearrange("(k p) n -> p k n", p=128))
                if n == NRAW - 1:
                    for t in range(4):
                        xs = A["ctx"] if t < 2 else A["x"]
                        d_x[t] = mload(X[:, t, :], xs[(t % 2) * 128:(t % 2) * 128 + 128, :], q=SP)
                for mth in range(4):
                    for k in range(2):
                        p = mm(b[:, mth * 2:mth * 2 + 2], v3[:, k, mth * 128:mth * 128 + 128], sc[:, 0:2, kk * 2 + k],
                               kk == 0 and k == 0 and mth == 0, kk == 3 and k == 1, (m,), inc=(mth == 3 and k == 1))
                sl.free = [p]
            return b, p

        def direct_out(part, b, p):
            bc = bgc[:, 0, part * 8 + 4:part * 8 + 8]
            gc = bgc[:, 0, 52:56]
            bv = b[:, 0:8].rearrange("p (m t) -> p t m", t=2)
            for ty in range(2):
                o = mod[:, 0, part, ty, 4:8]
                v = tt(o, bv[:, ty, :], bc, ALU.add, p, mod_mark[(0, "bg")])
                if ty == 1:
                    release(b, v)
                if part == 1:
                    v = stt(o, o, 1.0, gc, ALU.add, ALU.mult, v)
            mod_mark.setdefault((0, part), []).append(v)

        st_n = [0]

        stx = sb("stx", [128, 4, 5, 16])

        def stats():
            i = st_n[0] % 4
            st_n[0] += 1
            return stx[:, i, :, :]

        def rstd(s, n, width, marks):
            ss, va, r, q1, _ = (s[:, j, 0:n] for j in range(5))
            v = ts(va, ss, 1.0 / width, EPS, ALU.mult, ALU.add, marks)
            v = ts(q1.bitcast(I32), va.bitcast(I32), 1, None, ALU.logical_shift_right, None, v)
            v = ts(r.bitcast(I32), q1.bitcast(I32), -1.0, 1597463007.0, ALU.mult, ALU.add, v)
            for _ in range(3):
                v = stt(q1, r, -0.5, r, ALU.mult, ALU.mult, v)
                v = tt(q1, q1, va, ALU.mult, v)
                v = stt(r, q1, 1.5, r, ALU.add, ALU.mult, v)
            return r, v

        def sumsq(src, dst, *marks):
            n = 1
            for d in src.shape[1:]:
                n *= d
            m = act(junk[:, 0:n], src, ACT.Square, junk_mark[0], *marks, accum_out=dst)
            junk_mark[0] = m
            return m

        def prep(g, xm, dg, yfree=()):
            s = stats()
            for n, t in enumerate(g):
                m = sumsq(X[:, t, :], s[:, 0, n:n + 1], xm[t])
            r, rm = rstd(s, len(g), D, [m])
            for n, t in enumerate(g):
                dg[t] = ts(Y4[:, t, 0:128], ident[:], r[:, n:n + 1], None, ALU.mult, None, rm, d_id, yfree, xm[t])

        def make_h(li, which, halves, dg, xm):
            pi = 2 * which
            hfree = PE.last()
            ensure((li, 0 if which == 0 else 3))
            ensure((li, 1 if which == 0 else 4))
            mB, mA = mod_mark[(li, pi)], mod_mark[(li, pi + 1)]
            hmk = {}
            for kp in range(4):
                for hf in halves:
                    b, fr = bank()
                    PE.wait(fr)
                    for k in range(2):
                        for t in range(2):
                            kk = kp * 2 + k
                            tt_ = hf * 2 + t
                            p = mm(b[:, k * 256 + t * 128:k * 256 + t * 128 + 128], X[:, tt_, kk * 128:kk * 128 + 128],
                                   Y4[:, tt_, 0:128], True, True, (dg[tt_], xm[tt_]), inc=(t == 1 and k == 1))
                    t1, tf, ti = tmp()
                    for k in range(2):
                        kk = kp * 2 + k
                        a = act(t1[:, k * 256:k * 256 + 256], b[:, k * 256:k * 256 + 256], ACT.Identity, p, tf, mA, mB,
                                scale=mod[:, li % 2, pi + 1, hf, kk:kk + 1], bias=mod[:, li % 2, pi, hf, kk:kk + 1])
                    release(b, a)
                    t3 = t1[:, :].rearrange("p (k n) -> p k n", k=2)
                    oh = HH[:, kp * 2:kp * 2 + 2, hf * 256:hf * 256 + 256]
                    ol = HL[:, kp * 2:kp * 2 + 2, hf * 256:hf * 256 + 256]
                    v = cp(oh, t3, a, hfree)
                    v = tt(ol, t3, oh.bitcast(F32), ALU.subtract, v)
                    tmp_free[ti] = [v]
                    hmk.setdefault(kp * 2, []).append(v)
                hmk[kp * 2 + 1] = hmk[kp * 2]
            return lambda kt: hmk[kt]

        def combine(li, part, g, ym, xm):
            gm = G_mark[(li, part)]
            hf = g[0] // 2
            s = stats()
            yq = ysq[:, g[0] * 2:g[0] * 2 + 2 * len(g)].rearrange("p (a b) -> p a b", b=2)
            v = tt(s[:, 0, 0:len(g)], yq[:, :, 0], yq[:, :, 1], ALU.add, [ym[(t, nh)] for t in g for nh in range(2)])
            r, rm = rstd(s, len(g), D, [v])
            for n, t in enumerate(g):
                v = stt(Y4[:, t, :], Y4[:, t, :], r[:, n:n + 1], G[:, hf, :], ALU.mult, ALU.mult, rm, gm)
                xm[t] = tt(X[:, t, :], X[:, t, :], Y4[:, t, :], ALU.add, v, q=PO if n == 0 and len(g) == 2 else DV)
            G_free[0] = v

        def boundary(li, part, tiles, pend, ym, xm, dg, nxt):
            ensure((li, part))
            for g in ([[0, 1], [2, 3]] if len(tiles) == 4 else [[2], [3]]):
                for t in g:
                    pend[t]()
                combine(li, part, g, ym, xm)
                if nxt:
                    prep(g, xm, dg)

        def proj_feat(nblocks, src, c0, c1, evac, marks):
            H1, H2 = src
            N = c1 - c0
            at = marks if callable(marks) else (lambda kt: marks)
            for nb in range(nblocks):
                bs = [bank(), bank()]
                for kk in range(2):
                    k, wh, wl, wm = take()
                    for m in range(2):
                        b, fr = bs[m]
                        for q in range(4):
                            kt = kk * 4 + q
                            last = mm3(b[:, 0:N], (wh[:, q, m * 128:m * 128 + 128], wl[:, q, m * 128:m * 128 + 128]),
                                       (H1[:, kt, c0:c1], H2[:, kt, c0:c1]), kt == 0, kt == 7,
                                       (fr, wm, at(kt)), inc=(q == 3))
                        if kk == 1:
                            bs[m] = (b, last)
                    gave(k, last)
                for m in range(2):
                    evac(nb * 2 + m, bs[m][0], bs[m][1])

        def proj_tok(src, nk, tiles, nhalves, evac, marks, width=512, off=0):
            H1, H2 = src
            at = marks if callable(marks) else (lambda kt: marks)
            for nh in range(nhalves):
                bs = {t: bank() for t in tiles}
                for kk in range(nk // 2):
                    k, wh, wl, wm = take()
                    for t in tiles:
                        b, fr = bs[t][0], bs[t][1]
                        o = (t - off) * 128
                        for q in range(2):
                            kt = kk * 2 + q
                            last = mm3(b[:, 0:width], (H1[:, kt, o:o + 128], H2[:, kt, o:o + 128]),
                                       (wh[:, q, 0:width], wl[:, q, 0:width]), kt == 0, kt == nk - 1,
                                       (fr, wm, at(kt)), inc=(q == 1))
                        if kk == nk // 2 - 1:
                            bs[t] = (b, last)
                    gave(k, last)
                for t in tiles:
                    evac(nh, t, bs[t][0], bs[t][1])

        def proj_last(src, tiles, evac, marks, off=0):
            H1, H2 = src
            at = marks if callable(marks) else (lambda kt: marks)
            proj_tok(src, 8, tiles, 1, evac, marks, off=off)
            slots = take4()
            pend = {}
            for t in tiles:
                b, fr = bank()
                o = (t - off) * 128
                for kk in range(4):
                    k, wh, wl, wm = slots[kk]
                    for q in range(2):
                        kt = kk * 2 + q
                        last = mm3(b[:, :], (H1[:, kt, o:o + 128], H2[:, kt, o:o + 128]), (wh[:, q, :], wl[:, q, :]),
                                   kt == 0, kt == 7, (fr, wm, at(kt)), inc=(q == 1))
                    if t == tiles[-1]:
                        gave(k, last)
                pend[t] = lambda t=t, b=b, last=last: evac(1, t, b, last)
            return pend

        flip = [0]

        def copy_out(o, i, *marks):
            flip[0] ^= 1
            if flip[0]:
                return act(o, i, ACT.Copy, *marks)
            return cp(o, i, *marks)

        def y_evac_for(ym, yfree, first=True, final=True):
            def f(nh, t, b, p):
                o = Y4[:, t, nh * 512:nh * 512 + 512]
                if first:
                    m = copy_out(o, b[:, :], p, yfree)
                else:
                    m = tt(o, o, b[:, :], ALU.add, p, ym.get((t, nh)))
                release(b, m)
                if final:
                    m = [m, sumsq(o, ysq[:, t * 2 + nh:t * 2 + nh + 1], m)]
                ym[(t, nh)] = m
            return f

        def mlp(li, tiles, hm, stack):
            c0 = tiles[0] * 128
            N = len(tiles) * 128
            fz = fence()
            UH = sb(f"UH{li}", [128, 8, 512], F32R, stack)
            UL = sb(f"UL{li}", [128, 8, 512], F32R, stack)
            ym = {}
            ufree = [[fz] for _ in range(8)]
            for q in range(4):
                um = []

                def evac(n, b, p, um=um):
                    t1, tf, ti = tmp()
                    a = act(t1[:, 0:N], b[:, 0:N], ACT.Relu, p, tf)
                    release(b, a)
                    t2, tf2, ti2 = tmp()
                    g = tt(t2[:, 0:N], t1[:, 0:N], t1[:, 0:N], ALU.mult, a, tf2, q=PO)
                    a = act(UH[:, n, 0:N], t1[:, 0:N], ACT.Square, a, ufree[n])
                    tmp_free[ti] = [g, a]
                    v = tt(UL[:, n, 0:N], t2[:, 0:N], UH[:, n, 0:N].bitcast(F32), ALU.subtract, a, g, ufree[n])
                    tmp_free[ti2] = [v]
                    um.append([a, v])

                proj_feat(4, (HH, HL), c0, c0 + N, evac, hm)
                if q < 3:
                    proj_tok((UH, UL), 8, tiles, 2, y_evac_for(ym, fz, q == 0, False), lambda kt: um[kt], off=tiles[0])
                else:
                    pend = proj_last((UH, UL), tiles, y_evac_for(ym, fz, False, True), lambda kt: um[kt], off=tiles[0])
                ufree = [[PE.last()] for _ in range(8)]
            return pend, ym

        def hi_lo(oh, ol, src, *marks):
            a = act(oh, src, ACT.Copy, *marks)
            v = tt(ol, src, oh.bitcast(F32), ALU.subtract, a, *marks)
            return [a, v]

        def mla(li, hm, stack):
            fz = fence()
            with ExitStack() as s1:
                CQH = sb("CQH", [128, 3, 512], F32R, s1)
                CQL = sb("CQL", [128, 3, 512], F32R, s1)
                CKH = sb("CKH", [128, 2, 512], F32R, s1)
                CKL = sb("CKL", [128, 2, 512], F32R, s1)
                krT = sb("krT", [64, 512], F32, s1)
                cs = sb("cs", [64, 2, 256], F32, s1)
                rot = sb("rot", [64, 64], F32, s1)
                grow = sb("grow", [5, 128], F32, s1)
                gcol = sb("gcol", [128, 5], F32, s1)
                qn = [sb(f"qn{i}", [128, 512], F32, s1) for i in range(2)]
                kn = [sb(f"kn{i}", [128, 512], F32, s1) for i in range(2)]
                qr = [sb(f"qr{i}", [64, 512], F32, s1) for i in range(2)]
                Pl = [sb(f"Pl{i}", [128, 512], F32, s1) for i in range(4)]
                Pc = [sb(f"Pc{i}", [128, 256], F32, s1) for i in range(4)]
                PTl = sb("PTl", [128, 4, 256], F32, s1)
                PTc = sb("PTc", [128, 2, 256], F32, s1)
                CQ = Y[:, 0:2816].rearrange("p (t n) -> p t n", t=4)
                VV = [Y[:, 2816 + 512 * i:3328 + 512 * i].rearrange("p (t n) -> p t n", t=4) for i in range(2)]
                mc1 = mload(cs[:, 0, :], cap("cos")[0:64, :], fz)
                mc2 = mload(cs[:, 1, :], cap("sin")[0:64, :], fz)
                mr = mload(rot[:], cap("rot")[0:64, :], fz)
                mg1 = mload(grow[0:3, :], A["mla_g_q"][0].rearrange("(r p) -> r p", p=128), fz)
                mg2 = mload(grow[3:5, :], A["mla_g_kv"][0].rearrange("(r p) -> r p", p=128), fz)
                b, fr = bank()
                p = tr(b[:, 0:5], grow[:], ident[0:5, 0:5], fr, mg1, mg2)
                mg = cp(gcol[:], b[:, 0:5], p, fz)
                release(b, mg)
                cm = {}

                def ev(off, w):
                    def f(nh, t, b, p):
                        m = copy_out(CQ[:, t, off:off + w], b[:, 0:w], p, fz)
                        cm[(t, off)] = m
                        release(b, m)
                    return f

                proj_tok((HH, HL), 8, [0, 1, 2, 3], 1, ev(0, 384), hm, width=384)
                proj_tok((HH, HL), 8, [0, 1, 2, 3], 1, ev(384, 320), hm, width=320)
                s = stats()
                for t in range(4):
                    m1 = sumsq(CQ[:, t, 0:384], s[:, 0, t:t + 1], cm[(t, 0)])
                r, rm = rstd(s, 4, 384, [m1])
                s2 = stats()
                for t in range(4):
                    m2 = sumsq(CQ[:, t, 384:640], s2[:, 0, t:t + 1], cm[(t, 384)])
                r2, rm2 = rstd(s2, 4, 256, [m2])
                nm = []
                for t in range(4):
                    m = ts(CQ[:, t, 0:384], CQ[:, t, 0:384], r[:, t:t + 1], None, ALU.mult, None, rm, m1, cm[(t, 0)])
                    m = ts(CQ[:, t, 384:640], CQ[:, t, 384:640], r2[:, t:t + 1], None, ALU.mult, None, rm2, m2,
                           cm[(t, 384)])
                    nm.append(m)
                for f in range(6):
                    w = 128 if f < 5 else 64
                    b, fr = bank()
                    PE.wait(fr)
                    for t in range(4):
                        p = tr(
                            b[0:w, t * 128:t * 128 + 128], CQ[:, t, f * 128:f * 128 + w], ident[:],
                            nm[t], cm[(t, 384)])
                    if f < 5:
                        oh, ol = (CQH[:, f, :], CQL[:, f, :]) if f < 3 else (CKH[:, f - 3, :], CKL[:, f - 3, :])
                        a = act(oh, b[:, :], ACT.Copy, p, mg, fz, scale=gcol[:, f:f + 1])
                        v = stt(ol, b[:, :], gcol[:, f:f + 1], oh.bitcast(F32), ALU.mult, ALU.subtract, a)
                        release(b, v)
                        if f < 3:
                            cqm = [a, v]
                        else:
                            ckm = [a, v]
                    else:
                        a = cp(krT[:], b[0:64, :], p, fz)
                        release(b, a)
                        krm = a

                def rope(x, xm):
                    b, fr = bank()
                    p = mm(b[0:64, 0:256], rot[:], x[:, 256:512], True, True, (fr, xm, mr), inc=True)
                    t1, tf, ti = tmp()
                    v1 = tt(t1[0:64, 0:256], b[0:64, 0:256], cs[:, 1, :], ALU.mult, p, mc2, tf)
                    release(b, v1)
                    v2 = tt(x[:, 256:512], x[:, 256:512], cs[:, 0, :], ALU.mult, p, mc1, xm)
                    v3 = tt(x[:, 256:512], x[:, 256:512], t1[0:64, 0:256], ALU.add, v1, v2)
                    tmp_free[ti] = [v3]
                    return v3

                krm = rope(krT, krm)
                SC = 192.0 ** -0.5
                sfree = [[fz], [fz]]
                vfree = [[fz, cqm, ckm, krm], [fz, cqm, ckm, krm]]
                Plf = [[fz] for _ in range(4)]
                Pcf = [[fz] for _ in range(4)]
                PTfree = [fz]
                om = []

                def stage_a(h):
                    i = h % 2
                    k, wh, wl, wm = take()
                    b, fr = bank()
                    for q in range(3):
                        p = mm3(b[:, :], (wh[:, q, 0:128], wl[:, q, 0:128]), (CQH[:, q, :], CQL[:, q, :]),
                                q == 0, q == 2, (fr, wm, cqm), inc=(q == 2))
                    a1 = act(qn[i][:], b[:, :], ACT.Copy, p, sfree[i])
                    release(b, a1)
                    b, fr = bank()
                    for q in range(3):
                        p = mm3(b[0:64, :], (wh[:, q, 128:192], wl[:, q, 128:192]), (CQH[:, q, :], CQL[:, q, :]),
                                q == 0, q == 2, (fr,), inc=(q == 2))
                    gave(k, p)
                    v1 = cp(qr[i][:], b[0:64, :], p, sfree[i])
                    release(b, v1)
                    k, wh, wl, wm = take()
                    b, fr = bank()
                    for q in range(2):
                        p = mm3(b[:, :], (wh[:, q, 0:128], wl[:, q, 0:128]), (CKH[:, q, :], CKL[:, q, :]),
                                q == 0, q == 1, (fr, wm, ckm), inc=(q == 1))
                    a2 = act(kn[i][:], b[:, :], ACT.Copy, p, sfree[i])
                    release(b, a2)
                    b, fr = bank()
                    PE.wait(fr)
                    for t in range(4):
                        for q in range(2):
                            p = mm3(b[:, t * 128:t * 128 + 128],
                                    (CKH[:, q, t * 128:t * 128 + 128], CKL[:, q, t * 128:t * 128 + 128]),
                                    (wh[:, q, 128:256], wl[:, q, 128:256]), q == 0, q == 1, (),
                                    inc=(q == 1 and t == 3))
                    gave(k, p)
                    v2 = cp(VV[i], b[:, :].rearrange("p (t n) -> p t n", t=4), p,
                               vfree[i])
                    release(b, v2)
                    v1 = rope(qr[i], v1)
                    return (i, a1, a2, v1, v2)

                def scores(h, S):
                    i, a1, a2, v1, v2 = S
                    marks = (a1, a2, v1, krm)
                    pm = []
                    for half, nk, PB, PF in ((1, 512, Pl, Plf), (0, 256, Pc, Pcf)):
                        for t in range(2):
                            c = half * 256 + t * 128
                            b, fr = bank()
                            mm(b[:, 0:nk], qn[i][:, c:c + 128], kn[i][:, 0:nk], True, False, (fr, marks))
                            p = mm(b[:, 0:nk], qr[i][:, c:c + 128], krT[:, 0:nk], False, True, inc=True)
                            s = stats()
                            m = rmax(s[:, 0, 0:1], b[:, 0:nk], AX.X, p)
                            m = ts(s[:, 1, 0:1], s[:, 0, 0:1], -SC, None, ALU.mult, None, m)
                            a = act(PB[2 * i + t][:, 0:nk], b[:, 0:nk], ACT.Exp, m, PF[2 * i + t], bias=s[:, 1, 0:1], scale=SC,
                                    accum_out=s[:, 2, 0:1])
                            release(b, a)
                            m = rcp(s[:, 3, 0:1], s[:, 2, 0:1], a)
                            m = ts(PB[2 * i + t][:, 0:nk], PB[2 * i + t][:, 0:nk], s[:, 3, 0:1], None, ALU.mult, None, m)
                            pm.append(m)
                    sfree[i] = [p]
                    return pm

                def values(h, S, pm):
                    i, a1, a2, v1, v2 = S
                    ptm = []
                    n = 0
                    for half, nk, PB, PF, PT in ((1, 4, Pl, Plf, PTl), (0, 2, Pc, Pcf, PTc)):
                        for t in range(2):
                            b, fr = bank()
                            PE.wait(fr, pm[n])
                            for kt in range(nk):
                                p = tr(
                                    b[:, kt * 128:kt * 128 + 128], PB[2 * i + t][:, kt * 128:kt * 128 + 128], ident[:])
                            PF[2 * i + t] = [p]
                            m = copy_out(PT[:, :, t * 128:t * 128 + 128],
                                         b[:, 0:nk * 128].rearrange("p (k n) -> p k n", k=nk), p, PTfree)
                            release(b, m)
                            ptm.append(m)
                            n += 1
                    b, fr = bank()
                    for kt in range(4):
                        mm(b[:, 256:512], VV[i][:, kt, :], PTl[:, kt, :], kt == 0, kt == 3, (fr, ptm, v2))
                    for kt in range(2):
                        p = mm(b[:, 0:256], VV[i][:, kt, :], PTc[:, kt, :], kt == 0, kt == 1, inc=(kt == 1))
                    PTfree[:] = [p]
                    vfree[i] = [p]
                    m = hi_lo(HH[:, h, :], HL[:, h, :], b[:, :], p)
                    release(b, m)
                    om.append(m)

                prev = None
                for h in range(9):
                    cur = None
                    if h < 8:
                        cur = stage_a(h)
                        cur = (cur, scores(h, cur))
                    if prev is not None:
                        values(h - 1, *prev)
                    prev = cur
                fz2 = fence()
            ym = {}
            return proj_last((HH, HL), [0, 1, 2, 3], y_evac_for(ym, fz2), lambda kt: om[kt]), ym

        def gla(li, hm, stack):
            fz = fence()
            S = Y[:, 0:2048].rearrange("p (r h n) -> p r h n", r=2, h=4)
            VL = Y[:, 2048:4096].rearrange("p (t n) -> p t n", t=2)
            with ExitStack() as s1:
                cst = sb("g_cst", [128, 9, 128], F32, s1)
                mcs = mload(cst[:].rearrange("p a n -> p (a n)"), A["consts"][:, CONST_SLICES["cum"][0]:
                            CONST_SLICES["cum"][0] + 1152], fz)
                cum, end, endc = (lambda r: cst[:, r, :]), (lambda r: cst[:, 2 + r, :]), (lambda r: cst[:, 4 + r, :])
                tot, gmask = cst[:, 6, :], (lambda r: cst[:, 7 + r, :])
                z = sb("g_z", [65, 512], F32, s1)
                w2p = sb("g_w2p", [65, 2, 512], F32, s1)
                KLt = sb("g_klt", [128, 2, 512], F32, s1)
                v = mset(z[:], 1.0, fz)
                v0 = mset(w2p[:], 0.0, fz)
                zm0 = v
                wm2 = []
                for r in range(2):
                    wm2.append(mload(w2p[32 * r:32 * r + 16, r, :], A["gla_w_gate2"][0, r], v0))
                    wm2.append(mload(w2p[64:65, r, :], A["gla_b_gate"][0:1, r, :], v0))
                zc = []
                for r in range(2):
                    k, wh, wl, wm = take()
                    b, fr = bank()
                    for q in range(8):
                        p = mm3(b[0:16, :], (wh[:, q, :], wl[:, q, :]), (HH[:, q, :], HL[:, q, :]), q == 0, q == 7,
                                (fr, wm, hm(q)), inc=(q == 7))
                    gave(k, p)
                    v = cp(z[32 * r:32 * r + 16, :], b[0:16, :], p, zm0)
                    release(b, v)
                    zc.append(v)
                gmarks = [zc, wm2]

                def log_gate(r, t, dst, *marks):
                    b, fr = bank()
                    p = mm(b[:, :], z[:, t * 128:t * 128 + 128], w2p[:, r, :], True, True, (fr, gmarks), inc=True)
                    t1, tf, ti = tmp()
                    a = act(t1[:], b[:, :], ACT.Abs, p, tf)
                    a = act(t1[:], t1[:], ACT.Exp, a, scale=-1.0)
                    a = act(t1[:], t1[:], ACT.Ln, a, bias=ones[:, 0:1])
                    v = stt(dst, b[:, :], 0.0, t1[:], ALU.min, ALU.subtract, a, marks)
                    release(b, v)
                    tmp_free[ti] = [v]
                    return v

                with ExitStack() as s2:
                    KC = sb("g_kc", [128, 2, 512], F32, s2)
                    VC = sb("g_vc", [128, 2, 1024], F32, s2)
                    gx = sb("g_gx", [128, 2, 512], F32, s2)
                    KE = sb("g_ke", [128, 2, 512], F32, s2)
                    km, vm = {}, {}

                    def evk(nh, t, b, p):
                        dst = KC[:, t, :] if t < 2 else KLt[:, t - 2, :]
                        km[t] = copy_out(dst, b[:, :], p, fz)
                        release(b, km[t])

                    def evv(nh, t, b, p):
                        dst = (VC[:, t, :] if t < 2 else VL[:, t - 2, :])[:, nh * 512:nh * 512 + 512]
                        vm[(t, nh)] = copy_out(dst, b[:, :], p, fz)
                        release(b, vm[(t, nh)])

                    proj_tok((HH, HL), 8, [0, 1, 2, 3], 1, evk, hm)
                    proj_tok((HH, HL), 8, [0, 1, 2, 3], 2, evv, hm)
                    Sm = {}
                    prev = None
                    for r in range(2):
                        gm = [log_gate(r, t, gx[:, t, :], prev) for t in range(2)]
                        kem = []
                        for t in range(2):
                            b, fr = bank()
                            far = 1 if r == 0 else 0
                            mm(b[:, :], endc(r), gx[:, t, :], True, t == far, (fr, gm, mcs), inc=False)
                            if t != far:
                                p = mm(b[:, :], tot, gx[:, far, :], False, True, inc=True)
                            else:
                                p = mm(b[:, :], endc(r), gx[:, t, :], True, True, inc=True)
                            a = act(KE[:, t, :], b[:, :], ACT.Exp, p, prev)
                            release(b, a)
                            kem.append(tt(KE[:, t, :], KE[:, t, :], KC[:, t, :], ALU.mult, a, km[t]))
                        for hp in range(2):
                            b, fr = bank()
                            PE.wait(fr, kem)
                            for hh in range(2):
                                h = hp * 2 + hh
                                for t in range(2):
                                    p = mm(b[:, hh * 256:hh * 256 + 256], KE[:, t, h * 128:h * 128 + 128],
                                           VC[:, t, h * 256:h * 256 + 256], t == 0, t == 1,
                                           (vm[(t, h // 2)],), inc=True)
                            m = copy_out(S[:, r, hp * 2:hp * 2 + 2, :],
                                         b[:, :].rearrange("p (h n) -> p h n", h=2), p, fz)
                            release(b, m)
                            Sm[(r, hp * 2)] = Sm[(r, hp * 2 + 1)] = m
                        prev = [p]
                    fz2 = fence()
                with ExitStack() as s2:
                    qT = sb("g_qT", [128, 4, 256], F32, s2)
                    kT = sb("g_kT", [128, 4, 256], F32, s2)
                    gx = sb("g_gl", [128, 2, 512], F32, s2)
                    EG = sb("g_eg", [128, 4, 128], F32, s2)
                    EN = sb("g_en", [128, 4, 128], F32, s2)
                    qt = sb("g_qt", [128, 4, 128], F32, s2)
                    kt_ = sb("g_ktt", [128, 4, 128], F32, s2)
                    KE = sb("g_kel", [128, 512], F32, s2)
                    AT = [sb(f"g_at{r}", [128, 4, 128], F32, s2) for r in range(2)]
                    az = [mset(AT[r][:], 0.0, fz2) for r in range(2)]
                    qm = {}

                    def evq(n, b, p):
                        qm[n] = act(qT[:, n, :], b[:, 0:256], ACT.Copy, p, fz2, scale=128.0 ** -0.5)
                        release(b, qm[n])

                    proj_feat(2, (HH, HL), 256, 512, evq, hm)
                    ktm = {}
                    for hp in range(2):
                        b, fr = bank()
                        PE.wait(fr, km[2], km[3])
                        for hh in range(2):
                            h = hp * 2 + hh
                            for t in range(2):
                                p = tr(
                                    b[:, hh * 256 + t * 128:hh * 256 + t * 128 + 128],
                                    KLt[:, t, h * 128:h * 128 + 128], ident[:])
                        m = copy_out(kT[:, hp * 2:hp * 2 + 2, :], b[:, :].rearrange("p (h n) -> p h n", h=2), p, fz2)
                        release(b, m)
                        ktm[hp] = m
                    OB = [[bank() for _ in range(2)] for _ in range(2)]
                    started = set()
                    use = [None]
                    atfree = [None, None]
                    kefree = [None]
                    for r in range(2):
                        gm = [log_gate(r, 2 + t, gx[:, t, :], fz2, use[0]) for t in range(2)]
                        for ti_, t in enumerate([0, 1] if r == 0 else [1, 0]):
                            b, fr = bank()
                            PE.wait(fr, gm, mcs)
                            for h in range(4):
                                p = mm(b[:, h * 128:h * 128 + 128], gx[:, t, h * 128:h * 128 + 128], cum(r), True, True,
                                       inc=True)
                            bv = b[:, :].rearrange("p (h n) -> p h n", h=4)
                            a1 = act(EG[:], bv, ACT.Exp, p, use[0], fz2)
                            a2 = act(EN[:], bv, ACT.Exp, p, use[0], fz2, scale=-1.0)
                            release(b, a2)
                            v1 = tt(qt[:], EG[:], qT[:, :, t * 128:t * 128 + 128], ALU.mult, a1, list(qm.values()),
                                    use[0], fz2)
                            v2 = tt(kt_[:], EN[:], kT[:, :, t * 128:t * 128 + 128], ALU.mult, a2, ktm[0], ktm[1],
                                    use[0], fz2)
                            b, fr = bank()
                            p = mm(b[:, :], end(r), gx[:, t, :], True, True, (fr,), inc=True)
                            a3 = act(KE[:], b[:, :], ACT.Exp, p, kefree[0], fz2)
                            release(b, a3)
                            v3 = tt(KE[:], KE[:], KLt[:, t, :], ALU.mult, a3, km[2 + t])
                            b, fr = bank()
                            PE.wait(fr, v1, v2)
                            for h in range(4):
                                p = mm(b[:, h * 128:h * 128 + 128], kt_[:, h, :], qt[:, h, :], True, True, inc=True)
                            mk = gmask(r).bitcast(I32)
                            for h in range(4):
                                v4 = cpred(
                                    AT[r][:, h, :], mk, b[:, h * 128:h * 128 + 128], p, az, atfree[r], mcs)
                            release(b, v4)
                            for h in range(4):
                                ob, ofr = OB[t][h // 2]
                                first = (t, h // 2) not in started
                                started.add((t, h // 2))
                                p = mm(ob[:, (h % 2) * 256:(h % 2) * 256 + 256], AT[r][:, h, :],
                                       VL[:, t, h * 256:h * 256 + 256], first, False,
                                       (ofr, v4, vm[(2 + t, h // 2)]), inc=True)
                            atfree[r] = p
                            for ci, c in enumerate([0, 1] if r == 0 else [1, 0]):
                                last_chunk = ti_ == 1 and ci == 1
                                pr = {}
                                for h in range(4):
                                    ob = OB[t][h // 2][0]
                                    pr[h] = mm(ob[c * 64:c * 64 + 64, (h % 2) * 256:(h % 2) * 256 + 256],
                                               qt[:, h, c * 64:c * 64 + 64], S[:, r, h, :], False, False,
                                               (Sm[(r, h)],), inc=True)
                                use[0] = pr[3]
                                if last_chunk:
                                    continue
                                for hp in range(2):
                                    b, fr = bank()
                                    PE.wait(fr, v3)
                                    for hh in range(2):
                                        h = hp * 2 + hh
                                        p = mm(b[:, hh * 256:hh * 256 + 256],
                                               KE[c * 64:c * 64 + 64, h * 128:h * 128 + 128],
                                               VL[c * 64:c * 64 + 64, t, h * 256:h * 256 + 256], True, True, inc=True)
                                    for hh in range(2):
                                        h = hp * 2 + hh
                                        gi = c * 64 + (63 if r == 0 else 0)
                                        Sm[(r, h)] = stt(S[:, r, h, :], S[:, r, h, :], EG[:, h, gi:gi + 1],
                                                         b[:, hh * 256:hh * 256 + 256], ALU.mult, ALU.add, p, pr[h],
                                                         Sm[(r, h)])
                                    release(b, Sm[(r, h)])
                                kefree[0] = p
                                use[0] = [pr[3], Sm[(r, 3)], p]
                    of = PE.last()
                    fz3 = fence()
                with ExitStack() as s2:
                    sr = sb("g_sr", [128, 8, 256], F32, s2)
                    go = sb("g_go", [128, 2], F32, s2)
                    gor = sb("g_gor", [2, 128], F32, s2)
                    mg = mload(gor[:], A["gla_g_o"][0].rearrange("(r p) -> r p", p=128), fz3)
                    b, fr = bank()
                    p = tr(b[:, 0:2], gor[:], ident[0:2, 0:2], fr, mg)
                    gom = cp(go[:], b[:, 0:2], p, fz3)
                    release(b, gom)
                    Z = Y4[:, 0:2, :]
                    zm = []
                    s = stats()
                    s_ = None
                    for t in range(2):
                        for h in range(4):
                            ob = OB[t][h // 2][0]
                            m = sumsq(ob[:, (h % 2) * 256:(h % 2) * 256 + 256], s[:, 0, t * 4 + h:t * 4 + h + 1], of)
                    rr, rm = rstd(s, 8, 256, [m])
                    for t in range(2):
                        for h in range(4):
                            ob = OB[t][h // 2][0]
                            m = act(Z[:, t, h * 256:h * 256 + 256], ob[:, (h % 2) * 256:(h % 2) * 256 + 256], ACT.Copy,
                                    rm, fz3, scale=rr[:, t * 4 + h:t * 4 + h + 1])
                            if h % 2 == 1:
                                release(ob, m)
                        zm.append(m)
                    srm = {}

                    def evr(n, b, p):
                        t1, tf, ti = tmp()
                        a = act(t1[:, 0:256], b[:, 0:256], ACT.Exp, p, tf, scale=-1.0)
                        v = ts(t1[:, 0:256], t1[:, 0:256], 1.0, None, ALU.add, None, a)
                        v = rcp(t1[:, 256:512], t1[:, 0:256], v)
                        v = tt(sr[:, n, :], b[:, 0:256], t1[:, 256:512], ALU.mult, v, fz3)
                        release(b, v)
                        tmp_free[ti] = [v]
                        srm[n] = v

                    proj_feat(4, (HH, HL), 256, 512, evr, hm)
                    hfree = PE.last()
                    om = []
                    for fp in range(4):
                        b, fr = bank()
                        PE.wait(fr, zm)
                        for k in range(2):
                            f = fp * 2 + k
                            for t in range(2):
                                p = tr(
                                    b[:, k * 256 + t * 128:k * 256 + t * 128 + 128],
                                    Z[:, t, f * 128:f * 128 + 128], ident[:])
                        t1, tf, ti = tmp()
                        for k in range(2):
                            f = fp * 2 + k
                            v = stt(t1[:, k * 256:k * 256 + 256], b[:, k * 256:k * 256 + 256],
                                    go[:, f % 2:f % 2 + 1], sr[:, f, :], ALU.mult, ALU.mult, p, tf, gom, srm[f])
                        release(b, v)
                        m = hi_lo(HH[:, fp * 2:fp * 2 + 2, 256:512], HL[:, fp * 2:fp * 2 + 2, 256:512],
                                  t1[:, :].rearrange("p (k n) -> p k n", k=2), v, hfree)
                        tmp_free[ti] = m
                        om.append(m)
                    fz4 = fence()
            ym = {}
            return proj_last((HH, HL), [2, 3], y_evac_for(ym, fz4), lambda kt: om[kt // 2]), ym

        def conv(li, hm, stack):
            fz = fence()
            BH = sb("c_bh", [128, 8, 512], F32R, stack)
            BL = sb("c_bl", [128, 8, 512], F32R, stack)
            cu = [sb(f"c_cu{i}", [128, 522], F32, stack) for i in range(2)]
            cv = [sb(f"c_cv{i}", [128, 512], F32, stack) for i in range(2)]
            cwr = sb("c_wr", [24, 128], F32, stack)
            cwc = sb("c_wc", [128, 24], F32, stack)
            mw = mload(cwr[:], A["conv_w_2"][0].rearrange("a (r p) -> (a r) p", p=128), fz)
            b, fr = bank()
            p = tr(b[:, 0:24], cwr[:], ident[0:24, 0:24], fr, mw)
            cwm = cp(cwc[:], b[:, 0:24], p, fz)
            release(b, cwm)
            cz = [mset(cu[i][:], 0.0, fz) for i in range(2)]
            cufree = [None, None]
            cvfree = [None, None]
            om = []

            def view(i, sft, seg):
                if seg == 0:
                    return cu[i][:, 1 + sft:257 + sft]
                return cu[i][:, 258:522].rearrange("p (r n) -> p r n", r=4)[:, :, 1 + sft:65 + sft]

            for g in range(4):
                got = {}

                def ev(part):
                    def f(n, b, p):
                        d = g * 2 + n
                        i = n
                        if part == "c":
                            got[("c", i)] = act(cv[i][:], b[:, :], ACT.Copy, p, fz, cvfree[i])
                            release(b, got[("c", i)])
                        elif part == "u":
                            m = tt(view(i, 0, 0), b[:, 0:256], cv[i][:, 0:256], ALU.mult, p, got[("c", i)], cz,
                                   cufree[i])
                            m = tt(view(i, 0, 1), b[:, 256:512].rearrange("p (r n) -> p r n", r=4),
                                   cv[i][:, 256:512].rearrange("p (r n) -> p r n", r=4), ALU.mult)
                            release(b, m)
                            for seg in range(2):
                                o = cv[i][:, seg * 256:seg * 256 + 256]
                                if seg:
                                    o = o.rearrange("p (r n) -> p r n", r=4)
                                m = ts(o, view(i, -1, seg), cwc[:, d:d + 1], None, ALU.mult, None, m, cwm)
                                m = stt(o, view(i, 0, seg), cwc[:, 8 + d:9 + d], o, ALU.mult, ALU.add, m)
                                m = stt(o, view(i, 1, seg), cwc[:, 16 + d:17 + d], o, ALU.mult, ALU.add, m)
                            cufree[i] = m
                            got[("y", i)] = m
                        else:
                            m = tt(cv[i][:], cv[i][:], b[:, :], ALU.mult, p, got[("y", i)])
                            release(b, m)
                            m = hi_lo(BH[:, d, :], BL[:, d, :], cv[i][:], m, fz)
                            cvfree[i] = m
                            om.append(m)
                    return f

                proj_feat(1, (HH, HL), 0, 512, ev("c"), hm)
                proj_feat(1, (HH, HL), 0, 512, ev("u"), hm)
                proj_feat(1, (HH, HL), 0, 512, ev("b"), hm)
            ym = {}
            return proj_last((BH, BL), [0, 1, 2, 3], y_evac_for(ym, fz), lambda kt: om[kt]), ym

        def mlstm(li, hm, stack):
            fz = fence()
            ac_ = [Y[:, r * 2064:(r + 1) * 2064].rearrange("p (t h n) -> p t h n", t=2, h=8) for r in range(2)]
            with ExitStack() as s1:
                msk = sb("m_msk", [128, 2, 2, 256], F32, s1)
                mmk = mload(msk[:].rearrange("p a b n -> p (a b n)"), cap("mmask"), fz)
                sel = sb("m_sel", [8, 8, 128], F32, s1)
                msl = mload(sel[:].rearrange("p a n -> p (a n)"), cap("sel")[0:8, :], fz)
                qT = sb("m_qT", [128, 4, 256], F32, s1)
                kT = sb("m_kT", [128, 4, 256], F32, s1)
                VLe = sb("m_vl", [128, 2, 8, 129], F32, s1)
                C = sb("m_C", [128, 2, 4, 129], F32, s1)
                M = sb("m_M", [8, 2, 256], F32, s1)
                cols = sb("m_cols", [128, 2, 8, 8], F32, s1)
                on = mset(VLe[:, :, :, 128:129], 1.0, fz)
                with ExitStack() as s2:
                    KC = sb("m_kc", [128, 2, 512], F32, s2)
                    KW = sb("m_kw", [128, 2, 512], F32, s2)
                    VCe = sb("m_vc", [128, 2, 8, 129], F32, s2)
                    gt = sb("m_gt", [128, 4, 2, 16], F32, s2)
                    gbi = sb("m_gb", [128, 32], F32, s2)
                    f_a = sb("m_fa", [128, 4, 2, 8], F32, s2)
                    rw = sb("m_rw", [8, 5, 256], F32, s2)
                    o8 = sb("m_o8", [8, 256], F32, s2)
                    sm = sb("m_sm", [8, 2, 4], F32, s2)
                    mo8 = mset(o8[:], 1.0, fz)
                    on2 = mset(VCe[:, :, :, 128:129], 1.0, fz)
                    mgb = mload(gbi[:], A["ml_b_if_2"][0].rearrange("r g -> (r g)").partition_broadcast(128), fz)
                    gr = sb("m_gr", [16, 512], F32, s2)
                    b2, fr2 = bank()
                    grf = fz
                    for r in range(2):
                        k, wh, wl, wm = take()
                        b, fr = bank()
                        for q in range(8):
                            p = mm3(b[0:16, :], (wh[:, q, :], wl[:, q, :]), (HH[:, q, :], HL[:, q, :]), q == 0, q == 7,
                                    (fr, wm, hm(q)), inc=(q == 7))
                        gave(k, p)
                        v = cp(gr[:], b[0:16, :], p, grf)
                        release(b, v)
                        for t in range(4):
                            p = tr(b2[:, r * 64 + t * 16:r * 64 + t * 16 + 16], gr[:, t * 128:t * 128 + 128],
                                   ident[0:16, 0:16], fr2, v)
                        grf = p
                    bv = b2[:, 0:128].rearrange("p (r t g) -> p r t g", r=2, t=4)
                    for r in range(2):
                        v = tt(gt[:, :, r, :], bv[:, r, :, :],
                               gbi[:, r * 16:r * 16 + 16].unsqueeze(1).to_broadcast([128, 4, 16]), ALU.add, p, mgb, fz)
                    release(b2, v)
                    fv = gt[:, :, :, 8:16]
                    a = act(f_a[:], fv, ACT.Abs, v, fz)
                    a = act(f_a[:], f_a[:], ACT.Exp, a, scale=-1.0)
                    a = act(f_a[:], f_a[:], ACT.Ln, a, bias=ones[:, 0:1])
                    v5 = ts(fv, fv, 0.0, None, ALU.min, None, v, a)
                    gtm = tt(fv, fv, f_a[:], ALU.subtract, v5, a)
                    km, vm = {}, {}

                    def evk(nh, t, b, p):
                        km[t] = copy_out(KC[:, t, :], b[:, :], p, fz)
                        release(b, km[t])

                    def evv(nh, t, b, p):
                        dst = (VCe[:, t, :, :] if t < 2 else VLe[:, t - 2, :, :])[:, nh * 4:nh * 4 + 4, 0:128]
                        vm[(t, nh)] = copy_out(dst, b[:, :].rearrange("p (h n) -> p h n", h=4), p, fz)
                        release(b, vm[(t, nh)])

                    proj_tok((HH, HL), 8, [0, 1], 1, evk, hm)
                    rowm = {}
                    cm = []
                    for r in range(2):
                        bi, fri = bank()
                        bf, frf = bank()
                        PE.wait(fri, frf, gtm)
                        for t in range(4):
                            tr(bi[0:8, t * 128:t * 128 + 128],
                                                                       gt[:, t, r, 0:8], ident[:])
                            p = tr(bf[0:8, t * 128:t * 128 + 128],
                                                                           gt[:, t, r, 8:16], ident[:])
                        rv = (lambda x: x) if r == 0 else (lambda x: x[:, ::-1])
                        B, AA, WK = rw[:, 0, :], rw[:, 1, :], rw[:, 2, :]
                        prevc = cm[-1] if cm else None
                        v = scan(
                            rv(B), o8[:], rv(bf[0:8, 0:256]), 0.0, ALU.mult, ALU.add, p, mo8, fz, prevc)
                        v = tt(AA, bi[0:8, 0:256], B, ALU.subtract, v, p, prevc)
                        v = rmax(sm[:, r, 0:1], AA, AX.X, v)
                        v = ts(sm[:, r, 1:2], sm[:, r, 0:1], 0.0, -1.0, ALU.max, ALU.mult, v)
                        a = act(WK, AA, ACT.Exp, v, prevc, bias=sm[:, r, 1:2])
                        last = 255 if r == 0 else 0
                        mi = tt(sm[:, r, 2:3], B[:, last:last + 1], sm[:, r, 1:2], ALU.subtract, v)
                        BL_, AL_, WI, EM = rw[:, 3, :], rw[:, 4, :], rw[:, 0, :], rw[:, 1, :]
                        v = scan(
                            rv(BL_), o8[:], rv(bf[0:8, 256:512]), 0.0, ALU.mult, ALU.add, p, prevc)
                        release(bf, v)
                        v = tt(AL_, bi[0:8, 256:512], BL_, ALU.subtract, v)
                        release(bi, v)
                        MR = M[:, r, :]
                        v = scan(
                            rv(MR), rv(AL_), rv(AL_), sm[:, r, 2:3], ALU.max, ALU.max, v, mi)
                        rowm[r] = v
                        a2 = act(WI, MR, ACT.Exp, v, mi, prevc, scale=-1.0, bias=sm[:, r, 2:3])
                        v = tt(EM, BL_, MR, ALU.add, v, a)
                        a3 = act(EM, EM, ACT.Exp, v, scale=-1.0)
                        b, fr = bank()
                        PE.wait(fr, a, a2, a3)
                        for n, row in enumerate((WK, AL_, WI, EM)):
                            for t in range(2):
                                p = tr(
                                    b[:, (n * 2 + t) * 8:(n * 2 + t) * 8 + 8], row[:, t * 128:t * 128 + 128],
                                    ident[0:8, 0:8])
                        v = cp(cols[:, r, :, :].rearrange("p a h -> p (a h)"),
                                                                    b[:, 0:64], p, fz)
                        release(b, v)
                        cm.append([v, p])
                    proj_tok((HH, HL), 8, [0, 1, 2, 3], 2, evv, hm)
                    Cm = {}
                    prev = None
                    for r in range(2):
                        kw = []
                        for t in range(2):
                            kw.append(tt(KW[:, t, :].rearrange("p (h n) -> p h n", h=8),
                                         KC[:, t, :].rearrange("p (h n) -> p h n", h=8),
                                         cols[:, r, t, :].unsqueeze(2).to_broadcast([128, 8, 64]), ALU.mult,
                                         km[t], cm[r], prev, fz))
                        for g2 in range(2):
                            b, fr = bank()
                            PE.wait(fr, kw, on2, list(vm.values()))
                            for pi in range(2):
                                for par in range(2):
                                    h = (g2 * 2 + pi) * 2 + par
                                    for t in range(2):
                                        p = mm(b[par * 64:par * 64 + 64, pi * 129:pi * 129 + 129],
                                               KW[:, t, h * 64:h * 64 + 64], VCe[:, t, h, :], t == 0, t == 1, inc=True)
                            Cm[(r, g2)] = copy_out(C[:, r, g2 * 2:g2 * 2 + 2, :],
                                                   b[:, 0:258].rearrange("p (h n) -> p h n", h=2), p, fz)
                            release(b, Cm[(r, g2)])
                        prev = p
                    fz2 = fence()
                qm, ktm = {}, {}

                def evq(n, b, p):
                    qm[n] = act(qT[:, n, :], b[:, 0:256], ACT.Copy, p, fz, scale=0.125)
                    release(b, qm[n])

                def evkt(n, b, p):
                    ktm[n] = cp(kT[:, n, :], b[:, 0:256], p, fz)
                    release(b, ktm[n])

                proj_feat(2, (HH, HL), 256, 512, evq, hm)
                proj_feat(2, (HH, HL), 256, 512, evkt, hm)
                with ExitStack() as s2:
                    DD = [sb(f"m_D{i}", [128, 2, 256], F32, s2) for i in range(2)]
                    SS = [sb(f"m_S{i}", [128, 2, 256], F32, s2) for i in range(2)]
                    TI = [sb(f"m_T{i}", [128, 2, 129], F32, s2) for i in range(2)]
                    dfree, sfree2, tfree = [[fz2], [fz2]], [[fz2], [fz2]], [[fz2], [fz2]]
                    am = {}
                    steps = [(h, r) for h in range(8) for r in range(2)]
                    sbk = {}

                    def front(h, r):
                        base = (h % 2) * 64
                        pr = h // 2
                        i = (h * 2 + r) % 2
                        if r == 0:
                            b, fr = bank()
                            PE.wait(fr, qm[pr], ktm[pr])
                            for s_ in range(2):
                                p = mm(b[:, s_ * 256:s_ * 256 + 256], kT[base:base + 64, pr, s_ * 128:s_ * 128 + 128],
                                       qT[base:base + 64, pr, :], True, True, inc=True)
                            sbk[h] = (b, p)
                        b, fr = bank()
                        p = mm(b[:, 0:256], sel[:, h, :], M[:, r, :], True, True, (fr, rowm[r], msl), inc=True)
                        v = stt(DD[i][:], b[:, 0:256].unsqueeze(1).to_broadcast([128, 2, 256]), -1.0, msk[:, r, :, :],
                                ALU.mult, ALU.add, p, mmk, dfree[i])
                        release(b, v)
                        for s_ in range(2):
                            a = act(DD[i][:, s_, :], DD[i][:, s_, :], ACT.Exp, v, cm[r][0],
                                    bias=cols[:, r, 2 + s_, h:h + 1])
                        sb_, sp_ = sbk[h]
                        v = tt(SS[i][:], sb_[:, :].rearrange("p (s n) -> p s n", s=2), DD[i][:], ALU.mult, a, sp_,
                               sfree2[i])
                        dfree[i] = [v]
                        if r == 1:
                            release(sb_, v)
                        return v

                    def back(h, r, v):
                        base = (h % 2) * 64
                        pr = h // 2
                        i = (h * 2 + r) % 2
                        b1, fr1 = bank()
                        b2, fr2 = bank()
                        PE.wait(fr1, fr2, v, on, vm[(2, h // 4)], vm[(3, h // 4)], Cm[(r, pr // 2)])
                        for t in range(2):
                            p2 = mm(b2[:, t * 129:t * 129 + 129], qT[base:base + 64, pr, t * 128:t * 128 + 128],
                                    C[base:base + 64, r, pr, :], True, True, inc=True)
                        for t in range(2):
                            ss_ = [q for q in range(2) if (q <= t if r == 0 else q >= t)]
                            for n, q in enumerate(ss_):
                                p1 = mm(b1[:, t * 129:t * 129 + 129], SS[i][:, q, t * 128:t * 128 + 128],
                                        VLe[:, q, h, :], n == 0, n == len(ss_) - 1, inc=True)
                        for t in range(2):
                            a = act(TI[i][:, t, :], b2[:, t * 129:t * 129 + 129], ACT.Copy, p2, tfree[i], cm[r][0],
                                    scale=cols[:, r, 4 + t, h:h + 1])
                        release(b2, a)
                        sfree2[i] = [p1]
                        v = tt(ac_[r][:, :, h, :], b1[:, 0:258].rearrange("p (t n) -> p t n", t=2), TI[i][:], ALU.add,
                               p1, a, fz)
                        release(b1, v)
                        tfree[i] = [v]
                        am[(h, r)] = v

                    pend = None
                    for h, r in steps:
                        v = front(h, r)
                        if pend is not None:
                            back(*pend)
                        pend = (h, r, v)
                    back(*pend)
                    den = sb("m_den", [128, 2, 16], F32, s2)
                    for r in range(2):
                        dv = den[:, r, :].rearrange("p (t h) -> p t h", t=2)
                        m = stt(dv, ac_[r][:, :, :, 128], -1.0, ac_[r][:, :, :, 128], ALU.mult, ALU.max, am[(7, r)], fz2)
                        m = tt(dv, dv, cols[:, r, 6:8, :], ALU.max, m)
                        m = rcp(den[:, r, :], den[:, r, :], m)
                        for t in range(2):
                            o = ac_[r][:, t, :, 0:128]
                            m2 = tt(o, o, den[:, r, t * 8:t * 8 + 8].unsqueeze(2).to_broadcast([128, 8, 128]),
                                    ALU.mult, m)
                    hsm = []
                    for t in range(2):
                        o = ac_[0][:, t, :, 0:128]
                        hsm.append(tt(o, o, ac_[1][:, t, :, 0:128], ALU.add, m2))
                    s = stats()
                    for t in range(2):
                        sq = ac_[1][:, t, :, 0:128]
                        o = ac_[0][:, t, :, 0:128]
                        m = tt(sq, o, o, ALU.mult, hsm[t])
                        m = rsum(s[:, 0, t * 8:t * 8 + 8], sq, AX.X, m)
                    r_, rm = rstd(s, 16, 128, [m])
                    hz = []
                    for t in range(2):
                        o = ac_[0][:, t, :, 0:128]
                        hz.append(tt(o, o, r_[:, t * 8:t * 8 + 8].unsqueeze(2).to_broadcast([128, 8, 128]), ALU.mult,
                                     rm, hsm[t]))
                    fz3 = fence()
            with ExitStack() as s1:
                so = sb("m_so", [128, 8, 256], F32, s1)
                nwr = sb("m_nwr", [8, 128], F32, s1)
                nwc = sb("m_nwc", [128, 8], F32, s1)
                mg = mload(nwr[:], A["ml_norm_w_2"][0].rearrange("(r p) -> r p", p=128), fz3)
                b, fr = bank()
                p = tr(b[:, 0:8], nwr[:], ident[0:8, 0:8], fr, mg)
                nwm = cp(nwc[:], b[:, 0:8], p, fz3)
                release(b, nwm)
                som = {}

                def evo(n, b, p):
                    t1, tf, ti = tmp()
                    a = act(t1[:, 0:256], b[:, 0:256], ACT.Exp, p, tf, scale=-1.0)
                    release(b, a)
                    v = ts(t1[:, 0:256], t1[:, 0:256], 1.0, None, ALU.add, None, a)
                    v = rcp(so[:, n, :], t1[:, 0:256], v, fz3)
                    tmp_free[ti] = [v]
                    som[n] = v

                proj_feat(4, (HH, HL), 256, 512, evo, hm)
                hfree = PE.last()
                om = []
                for fp in range(4):
                    b, fr = bank()
                    PE.wait(fr, hz)
                    for k in range(2):
                        f = fp * 2 + k
                        for t in range(2):
                            p = tr(
                                b[:, k * 256 + t * 128:k * 256 + t * 128 + 128], ac_[0][:, t, f, 0:128], ident[:])
                    t1, tf, ti = tmp()
                    for k in range(2):
                        f = fp * 2 + k
                        v = stt(t1[:, k * 256:k * 256 + 256], b[:, k * 256:k * 256 + 256], nwc[:, f:f + 1], so[:, f, :],
                                ALU.mult, ALU.mult, p, tf, nwm, som[f])
                    release(b, v)
                    m = hi_lo(HH[:, fp * 2:fp * 2 + 2, 256:512], HL[:, fp * 2:fp * 2 + 2, 256:512],
                              t1[:, :].rearrange("p (k n) -> p k n", k=2), v, hfree)
                    tmp_free[ti] = m
                    om.append(m)
                fz4 = fence()
            ym = {}
            return proj_last((HH, HL), [2, 3], y_evac_for(ym, fz4), lambda kt: om[kt // 2]), ym

        mixers = [mla, gla, conv, mlstm]
        allow.update({(0, 0), (0, 1)})
        while (0, "bg") not in mod_mark:
            step_bg()
        parts = [direct(0, 0), direct(1, 4)]
        xm = {t: d_x[t] for t in range(4)}
        dg = {}
        prep([0, 1], xm, dg, fence())
        prep([2, 3], xm, dg)
        ensure((0, 0))
        direct_out(0, *parts[0])
        ensure((0, 1))
        direct_out(1, *parts[1])
        for li in range(4):
            both = LAYERS[li]["both"]
            tiles = [0, 1, 2, 3] if both else [2, 3]
            hm = make_h(li, 0, [0, 1], dg, xm)
            if li == 1:
                fx = fence()
                for t in range(2):
                    xm[t] = mload(X[:, t, :], A["ctx_2"][t * 128:t * 128 + 128, :], fx)
            for part in (0, 1, 3, 4, 2):
                allow.add((li, part))
            with ExitStack() as ls:
                pend, ym = mixers[li](li, hm, ls)
                boundary(li, 2, tiles, pend, ym, xm, dg, True)
            hm = make_h(li, 1, [0, 1] if both else [1], dg, xm)
            if li == 1:
                prep([0, 1], xm, dg, fence())
            allow.add((li, 5))
            if li < 3:
                for part in (0, 1, 3, 4):
                    allow.add((li + 1, part))
            with ExitStack() as ls:
                pend, ym = mlp(li, tiles, hm, ls)
                boundary(li, 5, tiles, pend, ym, xm, dg, li < 3)
        assert w_at[0] == len(WL) and not bg and not closing
        outs = []
        for t in range(2):
            outs.append(mload(out[t * 128:t * 128 + 128, :], X[:, 2 + t, :], xm[2 + t], q=SP))
        SP.wait(*outs)

        block = ctx.enter_context(nc.Block())

        @block.sync
        def _(e):
            SP.play(e)

        @block.gpsimd
        def _(e):
            PO.play(e)

        @block.scalar
        def _(e):
            AC.play(e)

        @block.vector
        def _(e):
            DV.play(e)

        @block.tensor
        def _(e):
            PE.play(e)


_INS = ['x', 'c', 'ctx', 'c_ctx', 'ada_w', 'ada_b', 'norm_g', 'mlp_w1', 'mlp_w2', 'mla_w_dq', 'mla_g_q', 'mla_w_uq',
        'mla_w_dkv', 'mla_g_kv', 'mla_w_ukv', 'mla_w_o', 'gla_w_q', 'gla_w_k', 'gla_w_v', 'gla_w_r', 'gla_w_gate1',
        'gla_w_gate2', 'gla_b_gate', 'gla_g_o', 'gla_w_o', 'c_2', 'ctx_2', 'c_ctx_2', 'norm_w_2', 'mod_w_2', 'mod_b_2',
        'mlp_w1_2', 'mlp_w2_2', 'conv_w_in_2', 'conv_w_2', 'conv_w_out_2', 'ml_w_qkvo_2', 'ml_w_if_2', 'ml_b_if_2',
        'ml_norm_w_2', 'ml_w_out_2']


def kernel(**inputs):
    import numpy as _np
    import concourse.bacc as _bacc
    from concourse import mybir as _mybir
    from concourse.bass_utils import run_bass_kernel_spmd as _run

    nc = _bacc.Bacc("TRN2", target_bir_lowering=False, num_devices=1)
    arrays, aps = {}, {}
    for name in _INS:
        a = _np.ascontiguousarray(inputs[name])
        if name in ("x", "ctx", "ctx_2"):
            a = a.reshape(256, 1024)
        if name in ("c", "c_ctx", "c_2", "c_ctx_2"):
            a = a.reshape(8, 128)
        arrays[f"in_{name}"] = a
        aps[name] = nc.dram_tensor(f"in_{name}", a.shape, _mybir.dt.from_np(a.dtype), kind="ExternalInput").ap()
    arrays["in_consts"] = CONSTS
    aps["consts"] = nc.dram_tensor("in_consts", CONSTS.shape, _mybir.dt.float32, kind="ExternalInput").ap()
    o = nc.dram_tensor("out_0", (256, 1024), _mybir.dt.float32, kind="ExternalOutput").ap()
    build(nc, aps, o)
    r = _run(nc, [arrays], core_ids=[0])
    return r.results[0]["out_0"].reshape(1, 256, 1024)
```

```python
from contextlib import ExitStack

import numpy as np

import concourse.bass as bass
from concourse import mybir

F32 = mybir.dt.float32
F32R = mybir.dt.float32r
I32 = mybir.dt.int32
ALU = mybir.AluOpType
ACT = mybir.ActivationFunctionType
AX = mybir.AxisListType

D = 1024
FF = 4096
EPS = 1e-6
NRAW = 3
NSPL = 4
NADA = 3
NTMP = 3

CONST_SLICES = {}


def const_table():
    parts = []
    at = [0]

    def add(name, a):
        full = np.zeros((128, a.shape[1]), np.float32)
        full[:a.shape[0]] = a
        CONST_SLICES[name] = (at[0], a.shape[1])
        at[0] += a.shape[1]
        parts.append(full)

    j = np.arange(128)[:, None]
    i = np.arange(128)[None, :]
    same = (j // 64) == (i // 64)
    add("ident", np.eye(128, dtype=np.float32))
    add("ones", np.ones((128, 128), np.float32))
    s = 1.0 / 16.0
    add("cum", np.concatenate([(same & (j <= i)) * s, (same & (j >= i)) * s], 1).astype(np.float32))
    add("end", np.concatenate([(same & (j > i)) * s, (same & (j < i)) * s], 1).astype(np.float32))
    add("endc", np.concatenate([(j > i) * s, (j < i) * s], 1).astype(np.float32))
    add("sum", np.full((128, 128), s, np.float32))
    add("gmask", np.concatenate([same & (j <= i), same & (j >= i)], 1).astype(np.float32))
    t = np.arange(256)[None, :]
    p = np.arange(128)[:, None]
    neg = np.float32(-1e30)
    mf = [np.where(p + 128 * q <= t, np.float32(0), neg) for q in range(2)]
    mb = [np.where(p + 128 * q >= t, np.float32(0), neg) for q in range(2)]
    add("mmask", np.concatenate(mf + mb, 1).astype(np.float32))
    sel = np.zeros((8, 8, 128), np.float32)
    for h in range(8):
        sel[h, h, :] = 1.0
    add("sel", sel.reshape(8, 1024))
    rot = np.zeros((64, 64), np.float32)
    for base in (0, 32):
        for q in range(16):
            rot[base + q + 16, base + q] = -1.0
            rot[base + q, base + q + 16] = 1.0
    add("rot", rot)
    half = 32
    inv = (np.float32(10000.0) ** (-np.arange(0, half, 2, dtype=np.float32) / np.float32(half))).astype(np.float32)
    row = np.repeat(np.arange(4, dtype=np.float32), 64)
    col = np.tile(np.arange(64, dtype=np.float32), 4)
    ar = (row[None, :] * inv[:, None]).astype(np.float32)
    ac = (col[None, :] * inv[:, None]).astype(np.float32)
    ang = np.concatenate([ar, ar, ac, ac], 0)
    add("cos", np.cos(ang).astype(np.float32))
    add("sin", np.sin(ang).astype(np.float32))
    return np.ascontiguousarray(np.concatenate(parts, 1))


CONSTS = const_table()


class Queue:

    def __init__(self, sem):
        self.sem = sem
        self.n = 0
        self.ops = []
        self.seen = {}

    def wait(self, *marks):
        for m in marks:
            if m is None or len(m) == 0:
                continue
            if isinstance(m, list) or not isinstance(m[0], int):
                self.wait(*m)
                continue
            key, sem, v = m
            if self.seen.get(key, 0) >= v:
                continue
            self.seen[key] = v
            self.ops.append(lambda e, sem=sem, v=v: e.wait_ge(sem, v))

    def do(self, fn, *marks, inc=True):
        self.wait(*marks)
        if inc:
            self.n += 1
            self.ops.append(lambda e: fn(e).then_inc(self.sem, 1))
            return (id(self), self.sem, self.n)
        self.ops.append(fn)
        return None

    def last(self):
        return (id(self), self.sem, self.n) if self.n else None

    def play(self, e):
        for op in self.ops:
            op(e)


class Slot:

    def __init__(self, ap, sem):
        self.ap = ap
        self.sem = sem
        self.n = 0
        self.free = []

    def load(self, q, dst, src, *marks):
        q.wait(self.free, *marks)
        self.n += 16
        sem = self.sem
        q.ops.append(lambda e: e.dma_start(dst, src).then_inc(sem, 16))
        return (id(self), sem, self.n)


def build(nc, A, out):
    ctx = ExitStack()
    with ctx:
        def sb(name, shape, dt=F32, stack=ctx):
            return stack.enter_context(nc.sbuf_tensor(name, shape, dt))

        def semf(name):
            return ctx.enter_context(nc.semaphore(name))

        banks = [ctx.enter_context(nc.psum_tensor(f"bank{i}", [128, 512], F32)) for i in range(8)]
        PE, AC, DV, PO, SP = (Queue(semf(n)) for n in ("s_pe", "s_act", "s_dve", "s_pool", "s_sp"))

        free_banks = [(b, []) for b in banks]

        def bank():
            b, marks = free_banks.pop(0)
            return b, list(marks)

        def release(b, *marks):
            free_banks.append((b, [m for m in marks]))

        X = sb("X", [128, 4, D])
        HH = sb("HH", [128, 8, 512], F32R)
        HL = sb("HL", [128, 8, 512], F32R)
        Y = sb("Y", [128, 4224])
        Y4 = Y[:, 0:4096].rearrange("p (t n) -> p t n", t=4)
        G = sb("G", [128, 2, D])
        raws = [Slot(sb(f"raw{i}", [128, 1024]), semf(f"s_raw{i}")) for i in range(NRAW)]
        spl = [(sb(f"wh{i}", [128, 1024], F32R), sb(f"wl{i}", [128, 1024], F32R)) for i in range(NSPL)]
        spl_free = [None] * NSPL
        adas = [Slot(sb(f"ada{i}", [128, 2, 512]), semf(f"s_ada{i}")) for i in range(NADA)]
        acc = sb("acc", [128, 2, 2, 512])
        gb = Slot(sb("gb", [128, 2, 512]), semf("s_gb"))
        ident = sb("ident", [128, 128])
        ones = sb("ones", [128, 128])
        tmps = [sb(f"tmp{i}", [128, 512]) for i in range(NTMP)]
        tmp_free = [[] for _ in range(NTMP)]
        tmp_n = [0]
        sc = sb("sc", [128, 4, 8])
        bgc = sb("bgc", [128, 2, 80])
        mod = sb("mod", [128, 2, 4, 2, 8])

        def tmp():
            i = tmp_n[0] % NTMP
            tmp_n[0] += 1
            return tmps[i], list(tmp_free[i]), i

        def fence():
            return [q.last() for q in (PE, AC, DV, PO)]

        def cap(name):
            a, n = CONST_SLICES[name]
            return A["consts"][:, a:a + n]

        def mload(dst, src, *marks, q=PO):
            return misc_load(q, dst, src, marks)

        misc_slots = {id(q): [Slot(None, semf(f"s_m{j}_{i}")) for i in range(10)] for j, q in enumerate((SP, PO))}
        misc_n = {id(SP): 0, id(PO): 0}

        def misc_load(q, dst, src, marks):
            sl = misc_slots[id(q)][misc_n[id(q)] % 10]
            misc_n[id(q)] += 1
            if sl.n:
                q.wait((id(sl), sl.sem, sl.n))
            return sl.load(q, dst, src, *marks)

        def tr(o, i, idn, *marks, inc=True):
            return PE.do(lambda e: e.transpose(o, i, idn), *marks, inc=inc)

        def cp(o, i, *marks):
            return DV.do(lambda e: e.tensor_copy(o, i), *marks)

        def rcp(o, i, *marks):
            return DV.do(lambda e: e.reciprocal(o, i), *marks)

        def rmax(o, i, ax, *marks):
            return DV.do(lambda e: e.reduce_max(o, i, ax), *marks)

        def rsum(o, i, ax, *marks):
            return DV.do(lambda e: e.reduce_sum(o, i, ax), *marks)

        def mset(o, v, *marks):
            return DV.do(lambda e: e.memset(o, v), *marks)

        def scan(o, a, b_, init, op0, op1, *marks):
            return DV.do(lambda e: e.tensor_tensor_scan(o, a, b_, init, op0, op1), *marks)

        def cpred(o, m, i, *marks):
            return DV.do(lambda e: e.copy_predicated(o, m, i), *marks)

        def act(o, i, f, *marks, **kw):
            return AC.do(lambda e: e.activation(o, i, f, **kw), *marks)

        def tt(o, a, b_, op, *marks, q=DV):
            return q.do(lambda e: e.tensor_tensor(o, a, b_, op), *marks)

        def ts(o, a, s1, s2, op0, op1, *marks, q=DV):
            if op1 is None:
                return q.do(lambda e: e.tensor_scalar(o, a, s1, None, op0), *marks)
            return q.do(lambda e: e.tensor_scalar(o, a, s1, s2, op0, op1), *marks)

        def stt(o, a, s, b_, op0, op1, *marks):
            return DV.do(lambda e: e.scalar_tensor_tensor(out=o, in0=a, scalar=s, in1=b_, op0=op0, op1=op1), *marks)

        d_id = mload(ident[:], cap("ident"), q=SP)
        junk = sb("junk", [128, 1024], mybir.dt.bfloat16)
        junk_mark = [None]
        ysq = sb("ysq", [128, 8])
        crow = Y[0:8, 0:512].rearrange("p (i n) -> p i n", i=4)
        d_c = [mload(crow[:, i, :], A[n], q=SP) for i, n in enumerate(("c_ctx", "c", "c_ctx_2", "c_2"))]
        d_on = mload(ones[:], cap("ones"))
        d_x = [None] * 4

        fence_mark = []
        b, fr = bank()
        for i in range(4):
            pt = tr(b[:, 8 * i:8 * i + 8], crow[:, i, :], ident[0:8, 0:8],
                       fr, d_id, d_c[i])
        t1, tf, ti = tmp()
        a1 = act(t1[:, 0:32], b[:, 0:32], ACT.Exp, pt, tf, scale=-1.0)
        v1 = ts(t1[:, 32:64], t1[:, 0:32], 1.0, None, ALU.add, None, a1)
        v2 = rcp(t1[:, 64:96], t1[:, 32:64], v1)
        scd = tt(sc[:].rearrange("p a k -> p (a k)"), b[:, 0:32], t1[:, 64:96], ALU.mult, v2)
        tmp_free[ti] = [scd]
        release(b, scd)
        fence_mark.append(pt)

        LAYERS = [
            dict(w=A["ada_w"][0], bia=A["ada_b"][0], g=A["norm_g"][0], c=0, both=True, w1=A["mlp_w1"][0], w2=A["mlp_w2"][0]),
            dict(w=A["ada_w"][1], bia=A["ada_b"][1], g=A["norm_g"][1], c=0, both=False, w1=A["mlp_w1"][1], w2=A["mlp_w2"][1]),
            dict(w=A["mod_w_2"][0], bia=A["mod_b_2"][0], g=A["norm_w_2"][0], c=2, both=True, w1=A["mlp_w1_2"][0], w2=A["mlp_w2_2"][0]),
            dict(w=A["mod_w_2"][1], bia=A["mod_b_2"][1], g=A["norm_w_2"][1], c=2, both=False, w1=A["mlp_w1_2"][1], w2=A["mlp_w2_2"][1]),
        ]

        def feat(W, c0, ncols, rows=D):
            for cb in range(c0, c0 + ncols, 256):
                for kk in range(0, rows, 512):
                    yield W[kk:kk + 512, cb:cb + 256].rearrange("(k p) n -> p k n", p=128)

        def tokw(W, r0, rows, c0, ncols):
            for cb in range(c0, c0 + ncols, 512):
                for kk in range(r0, r0 + rows, 256):
                    yield W[kk:kk + 256, cb:cb + 512].rearrange("(k p) n -> p k n", p=128)

        def mlp_stream(L):
            for q in range(4):
                yield from feat(L["w1"], q * 1024, 1024)
                yield from tokw(L["w2"], q * 1024, 1024, 0, 1024)

        def stream():
            for k in range(0, D, 256):
                yield A["mla_w_dq"][0][k:k + 256, :].rearrange("(k p) n -> p k n", p=128)
            for k in range(0, D, 256):
                yield A["mla_w_dkv"][0][k:k + 256, :].rearrange("(k p) n -> p k n", p=128)
            for h in range(8):
                yield A["mla_w_uq"][0][:, h * 192:(h + 1) * 192].rearrange("(k p) n -> p k n", p=128)
                yield A["mla_w_ukv"][0][:, h * 256:(h + 1) * 256].rearrange("(k p) n -> p k n", p=128)
            yield from tokw(A["mla_w_o"][0], 0, D, 0, D)
            yield from mlp_stream(LAYERS[0])
            yield from tokw(A["gla_w_k"][0], 0, D, 0, 512)
            for r in range(2):
                yield A["gla_w_gate1"][0, r].rearrange("(k p) n -> p k n", p=128)
            yield from tokw(A["gla_w_v"][0], 0, D, 0, 1024)
            yield from feat(A["gla_w_q"][0], 0, 512)
            yield from feat(A["gla_w_r"][0], 0, 1024)
            yield from tokw(A["gla_w_o"][0], 0, D, 0, D)
            yield from mlp_stream(LAYERS[1])
            W = A["conv_w_in_2"][0]
            for c in range(0, D, 256):
                yield from feat(W, D + c, 256)
                yield from feat(W, 2 * D + c, 256)
                yield from feat(W, c, 256)
            yield from tokw(A["conv_w_out_2"][0], 0, D, 0, D)
            yield from mlp_stream(LAYERS[2])
            W = A["ml_w_qkvo_2"][0]
            yield from tokw(W, 0, D, 512, 512)
            for r in range(2):
                yield A["ml_w_if_2"][0, r].rearrange("(k p) n -> p k n", p=128)
            yield from tokw(W, 0, D, 1024, 1024)
            yield from feat(W, 0, 512)
            yield from feat(W, 512, 512)
            yield from feat(W, 2048, 1024)
            yield from tokw(A["ml_w_out_2"][0], 0, D, 0, D)
            yield from mlp_stream(LAYERS[3])

        WL = list(stream())
        w_at = [0]
        w_split = [0]
        w_dma = [0]
        w_mark = {}
        w_done = {}
        w_raw = {}

        def shape2(ap):
            return ap.shape[1], ap.shape[2]

        def issue_dma():
            k = w_dma[0]
            if k >= len(WL):
                return
            sl = raws[k % NRAW]
            a, n = shape2(WL[k])
            w_raw[k] = sl.load(SP, sl.ap[:, 0:a * n].rearrange("p (a n) -> p a n", a=a), WL[k])
            w_dma[0] += 1

        def issue_split(q=DV):
            k = w_split[0]
            if k >= len(WL):
                return
            while w_dma[0] <= k:
                issue_dma()
            sl = raws[k % NRAW]
            hi, lo = spl[k % NSPL]
            a, n = shape2(WL[k])
            m = a * n
            done = w_done[k - NSPL] if k >= NSPL else None
            r = sl.ap
            t1 = AC.do(lambda e: e.activation(hi[:, 0:m], r[:, 0:m], ACT.Copy), w_raw[k], done)
            t2 = q.do(lambda e: e.tensor_tensor(lo[:, 0:m], r[:, 0:m], hi[:, 0:m].bitcast(F32), ALU.subtract),
                       w_raw[k], t1, done)
            sl.free = [t1, t2]
            w_mark[k] = [t1, t2]
            w_split[0] += 1
            issue_dma()

        bg = []
        bg_done = set()
        allow = set()
        closing = []
        LAG = [3]
        RATE = [0.6]
        credit = [0.0]

        def step_bg():
            key, fn, close = bg.pop(0)
            fn()
            for c in closing:
                c[0] -= 1
            flush_bg(0)
            if close is not None:
                closing.append([LAG[0], key, close])

        def flush_bg(limit):
            while closing and closing[0][0] <= limit:
                _, key, fn = closing.pop(0)
                if fn():
                    bg_done.add(key)

        def pump():
            credit[0] += RATE[0]
            while credit[0] >= 1.0:
                credit[0] -= 1.0
                if bg and bg[0][0] in allow:
                    step_bg()
                else:
                    for c in closing:
                        c[0] -= 1
                    flush_bg(0)

        def ensure(key):
            allow.add(key)
            while key not in bg_done:
                if any(b_[0] == key for b_ in bg):
                    assert bg[0][0] in allow, (bg[0][0], key)
                    step_bg()
                else:
                    flush_bg(9)

        def take():
            k = w_at[0]
            while w_split[0] < min(k + NSPL, len(WL)):
                issue_split()
            w_at[0] += 1
            pump()
            hi, lo = spl[k % NSPL]
            a, n = shape2(WL[k])
            v = [x[:, 0:a * n].rearrange("p (a n) -> p a n", a=a) for x in (hi, lo)]
            return k, v[0], v[1], w_mark[k]

        def take4(background=True):
            k0 = w_at[0]
            while w_split[0] < k0 + NSPL:
                issue_split()
            w_at[0] += NSPL
            out_ = []
            for k in range(k0, k0 + NSPL):
                hi, lo = spl[k % NSPL]
                a, n = shape2(WL[k])
                out_.append((k, hi[:, 0:a * n].rearrange("p (a n) -> p a n", a=a),
                             lo[:, 0:a * n].rearrange("p (a n) -> p a n", a=a), w_mark[k]))
                if background:
                    pump()
            return out_

        def gave(k, mark):
            w_done[k] = mark

        def mm3(o, s, m, start, stop, marks=(), inc=False):
            PE.wait(*marks)
            sh, sl_ = s
            mh, ml = m
            PE.do(lambda e: e.matmul(o, sh, mh, start=start, stop=False, skip_group_check=True), inc=False)
            PE.do(lambda e: e.matmul(o, sh, ml, start=False, stop=False, skip_group_check=True), inc=False)
            return PE.do(lambda e: e.matmul(o, sl_, mh, start=False, stop=stop, skip_group_check=True), inc=inc)

        def mm(o, s, m, start, stop, marks=(), inc=False):
            PE.wait(*marks)
            return PE.do(lambda e: e.matmul(o, s, m, start=start, stop=stop, skip_group_check=True), inc=inc)

        ada_n = [0]
        acc_free = [[], []]
        acc_n = [0]
        G_free = [None]
        mod_mark = {}
        G_mark = {}

        def ada_rows(li):
            L = LAYERS[li]
            m1 = gb.load(PO, gb.ap[0:48, 0, 0:128], L["bia"].rearrange("(r p) -> r p", p=128))
            gb.free = []
            m2 = gb.load(PO, gb.ap[0:32, 1, 0:128], L["g"].rearrange("a (r p) -> (a r) p", p=128))
            mod_mark[(li, "rows")] = [m1, m2]

        def ada_columns(li):
            b, fr = bank()
            tr(b[:, 0:48], gb.ap[0:48, 0, 0:128], ident[0:48, 0:48], fr, mod_mark[(li, "rows")], d_id, inc=False)
            p = tr(b[:, 48:80], gb.ap[0:32, 1, 0:128], ident[0:32, 0:32])
            v = cp(bgc[:, li % 2, :], b[:, 0:80], p)
            gb.free = [p]
            release(b, v)
            mod_mark[(li, "bg")] = v

        def ada_units(li):
            L = LAYERS[li]
            W = L["w"]
            order = [0, 1, 3, 4, 2, 5]
            for part in order:
                types = [1] if (not L["both"] and part > 1) else [0, 1]
                key = (li, part)
                units = []
                if part == 0:
                    units.append((lambda: None, lambda li=li: ada_rows(li)))
                lead = li == 0 and part < 2
                for ch in range(1 if lead else 2):
                    state = {}

                    def load_slot(kk, part=part, ch=ch, state=state):
                        sl = adas[ada_n[0] % NADA]
                        ada_n[0] += 1
                        c0 = part * D + ch * 512
                        src = W[kk * 256:kk * 256 + 256, c0:c0 + 512].rearrange("(k p) n -> p k n", p=128)
                        m = sl.load(PO, sl.ap[:], src)
                        state[kk] = (sl, m)

                    def work(kk, state=state, types=types, L=L, load_slot=load_slot):
                        if kk == 0:
                            state["buf"] = acc_n[0] % 2
                            acc_n[0] += 1
                            load_slot(0)
                            load_slot(1)
                        bi = state["buf"]
                        sl, m = state[kk]
                        for k in range(2):
                            for ty in types:
                                o = acc[:, bi, ty, :]
                                cc = sc[:, L["c"] + ty, kk * 2 + k:kk * 2 + k + 1]
                                if kk == 0 and k == 0:
                                    mk = ts(o, sl.ap[:, k, :], cc, None, ALU.mult, None, m, scd, acc_free[bi])
                                else:
                                    mk = stt(o, sl.ap[:, k, :], cc, o, ALU.mult, ALU.add, m, state[("m", ty)])
                                state[("m", ty)] = mk
                        sl.free = [mk]
                        if kk + 2 < 4:
                            load_slot(kk + 2)


                    def finish(part=part, ch=ch, state=state, types=types, li=li, L=L, lead=lead):
                        bi = state["buf"]
                        marks = [state[("m", ty)] for ty in types]
                        if part in (2, 5):
                            gi = 1 if part == 2 else 3
                            src = L["bia"][part * D + ch * 512:part * D + ch * 512 + 512]
                            g1 = gb.load(PO, gb.ap[:, 0, :], src.partition_broadcast(128))
                            gb.free = []
                            g2 = gb.load(PO, gb.ap[:, 1, :], L["g"][gi][ch * 512:ch * 512 + 512].partition_broadcast(128))
                            for ty in types:
                                b, fr = bank()
                                p = mm(b[:, :], ones[:], acc[:, bi, ty, :], True, True, (fr, marks, d_on), inc=True)
                                o = G[:, ty, ch * 512:ch * 512 + 512]
                                v = tt(o, b[:, :], gb.ap[:, 0, :], ALU.add, p, g2, G_free[0])
                                release(b, v)
                                v = tt(o, o, gb.ap[:, 1, :], ALU.mult, v, g2)
                            gb.free = [v]
                            acc_free[bi] = [p]
                            G_mark[(li, part)] = v
                            return ch == 1
                        else:
                            pi = {0: 0, 1: 1, 3: 2, 4: 3}[part]
                            b, fr = bank()
                            PE.wait(fr, marks, d_on)
                            for n, ty in enumerate(types):
                                for mth in range(4):
                                    p = mm(b[:, n * 4 + mth:n * 4 + mth + 1], acc[:, bi, ty, mth * 128:mth * 128 + 128],
                                           ones[:, 0:1], True, True, inc=True)
                            acc_free[bi] = [p]
                            bc = bgc[:, li % 2, part * 8 + ch * 4:part * 8 + ch * 4 + 4]
                            gc0 = 48 + (0 if part == 1 else 2) * 8 + ch * 4
                            gc = bgc[:, li % 2, gc0:gc0 + 4]
                            for n, ty in enumerate(types):
                                o = mod[:, li % 2, pi, ty, ch * 4:ch * 4 + 4]
                                v = tt(o, b[:, n * 4:n * 4 + 4], bc, ALU.add, p, mod_mark[(li, "bg")])
                                if n == len(types) - 1:
                                    release(b, v)
                                if part in (1, 4):
                                    v = stt(o, o, 1.0, gc, ALU.add, ALU.mult, v)
                            mod_mark.setdefault((li, pi), []).append(v)
                            return ch == 1 or lead

                    for kk in range(4):
                        close = finish if kk == 3 else None
                        if part == 0 and ch == 0 and kk == 1:
                            close = lambda li=li: ada_columns(li)
                        units.append((lambda kk=kk, work=work: work(kk), close))
                for u, close in units:
                    bg.append((key, u, close))

        for li in range(4):
            ada_units(li)

        def direct(part, lo_k):
            b, fr = bank()
            PE.wait(fr, scd)
            for kk in range(4):
                n = lo_k + kk
                sl = raws[n % NRAW]
                src = A["ada_w"][0][kk * 256:kk * 256 + 256, part * D + 512:part * D + 1024]
                v3 = sl.ap.rearrange("p (k n) -> p k n", k=2)
                m = sl.load(SP, v3, src.rearrange("(k p) n -> p k n", p=128))
                if n == NRAW - 1:
                    for t in range(4):
                        xs = A["ctx"] if t < 2 else A["x"]
                        d_x[t] = mload(X[:, t, :], xs[(t % 2) * 128:(t % 2) * 128 + 128, :], q=SP)
                for mth in range(4):
                    for k in range(2):
                        p = mm(b[:, mth * 2:mth * 2 + 2], v3[:, k, mth * 128:mth * 128 + 128], sc[:, 0:2, kk * 2 + k],
                               kk == 0 and k == 0 and mth == 0, kk == 3 and k == 1, (m,), inc=(mth == 3 and k == 1))
                sl.free = [p]
            return b, p

        def direct_out(part, b, p):
            bc = bgc[:, 0, part * 8 + 4:part * 8 + 8]
            gc = bgc[:, 0, 52:56]
            bv = b[:, 0:8].rearrange("p (m t) -> p t m", t=2)
            for ty in range(2):
                o = mod[:, 0, part, ty, 4:8]
                v = tt(o, bv[:, ty, :], bc, ALU.add, p, mod_mark[(0, "bg")])
                if ty == 1:
                    release(b, v)
                if part == 1:
                    v = stt(o, o, 1.0, gc, ALU.add, ALU.mult, v)
            mod_mark.setdefault((0, part), []).append(v)

        st_n = [0]

        stx = sb("stx", [128, 4, 5, 16])

        def stats():
            i = st_n[0] % 4
            st_n[0] += 1
            return stx[:, i, :, :]

        def rstd(s, n, width, marks):
            ss, va, r, q1, _ = (s[:, j, 0:n] for j in range(5))
            v = ts(va, ss, 1.0 / width, EPS, ALU.mult, ALU.add, marks)
            v = ts(q1.bitcast(I32), va.bitcast(I32), 1, None, ALU.logical_shift_right, None, v)
            v = ts(r.bitcast(I32), q1.bitcast(I32), -1.0, 1597463007.0, ALU.mult, ALU.add, v)
            for _ in range(3):
                v = stt(q1, r, -0.5, r, ALU.mult, ALU.mult, v)
                v = tt(q1, q1, va, ALU.mult, v)
                v = stt(r, q1, 1.5, r, ALU.add, ALU.mult, v)
            return r, v

        def sumsq(src, dst, *marks):
            n = 1
            for d in src.shape[1:]:
                n *= d
            m = act(junk[:, 0:n], src, ACT.Square, junk_mark[0], *marks, accum_out=dst)
            junk_mark[0] = m
            return m

        def prep(g, xm, dg, yfree=()):
            s = stats()
            for n, t in enumerate(g):
                m = sumsq(X[:, t, :], s[:, 0, n:n + 1], xm[t])
            r, rm = rstd(s, len(g), D, [m])
            for n, t in enumerate(g):
                dg[t] = ts(Y4[:, t, 0:128], ident[:], r[:, n:n + 1], None, ALU.mult, None, rm, d_id, yfree, xm[t])

        class Hidden:

            def __init__(self, li, which, dg, xm):
                self.li, self.which, self.dg, self.xm = li, which, dg, xm
                self.hfree = PE.last()
                self.marks = {}
                self.later = []
                ensure((li, 3 * which))
                ensure((li, 3 * which + 1))

            def make(self, hf):
                li, pi, dg, xm = self.li, 2 * self.which, self.dg, self.xm
                mB, mA = mod_mark[(li, pi)], mod_mark[(li, pi + 1)]
                for kp in range(4):
                    b, fr = bank()
                    PE.wait(fr)
                    for k in range(2):
                        for t in range(2):
                            kk = kp * 2 + k
                            tt_ = hf * 2 + t
                            p = mm(b[:, k * 256 + t * 128:k * 256 + t * 128 + 128], X[:, tt_, kk * 128:kk * 128 + 128],
                                   Y4[:, tt_, 0:128], True, True, (dg[tt_], xm[tt_]), inc=(t == 1 and k == 1))
                    t1, tf, ti = tmp()
                    for k in range(2):
                        kk = kp * 2 + k
                        a = act(t1[:, k * 256:k * 256 + 256], b[:, k * 256:k * 256 + 256], ACT.Identity, p, tf, mA, mB,
                                scale=mod[:, li % 2, pi + 1, hf, kk:kk + 1], bias=mod[:, li % 2, pi, hf, kk:kk + 1])
                    release(b, a)
                    t3 = t1[:, :].rearrange("p (k n) -> p k n", k=2)
                    oh = HH[:, kp * 2:kp * 2 + 2, hf * 256:hf * 256 + 256]
                    ol = HL[:, kp * 2:kp * 2 + 2, hf * 256:hf * 256 + 256]
                    v = cp(oh, t3, a, self.hfree)
                    v = tt(ol, t3, oh.bitcast(F32), ALU.subtract, v)
                    tmp_free[ti] = [v]
                    self.marks[(kp * 2, hf)] = self.marks[(kp * 2 + 1, hf)] = v

            def rest(self):
                while self.later:
                    self.later.pop(0)()

            def at(self, kt, hf):
                return self.marks[(kt, hf)]

            def __call__(self, kt):
                return [self.marks[(kt, hf)] for hf in range(2) if (kt, hf) in self.marks]

        def combine(li, part, g, ym, xm):
            gm = G_mark[(li, part)]
            hf = g[0] // 2
            s = stats()
            yq = ysq[:, g[0] * 2:g[0] * 2 + 2 * len(g)].rearrange("p (a b) -> p a b", b=2)
            v = tt(s[:, 0, 0:len(g)], yq[:, :, 0], yq[:, :, 1], ALU.add, [ym[(t, nh)] for t in g for nh in range(2)])
            r, rm = rstd(s, len(g), D, [v])
            for n, t in enumerate(g):
                v = stt(Y4[:, t, :], Y4[:, t, :], r[:, n:n + 1], G[:, hf, :], ALU.mult, ALU.mult, rm, gm)
                xm[t] = tt(X[:, t, :], X[:, t, :], Y4[:, t, :], ALU.add, v, q=PO if n == 0 and len(g) == 2 else DV)
            G_free[0] = v

        def transition(li, part, tiles, pend, ym, xm, dg, nxt, allowed):

            def group(g):
                for t in g:
                    pend[t]()
                combine(li, part, g, ym, xm)
                if nxt is not None:
                    prep(g, xm, dg)

            if len(tiles) == 4:
                group([0, 1])
                late = [2, 3]
            else:
                late = [2, 3]
            if nxt is None:
                return group(late)
            H = early_h.pop() if early_h else Hidden(nxt[0], nxt[1], dg, xm)
            if nxt[2]:
                issue_split()
                issue_split()
                if (0, 0) not in H.marks:
                    H.make(0)
                issue_split(PO)
                issue_split()
            H.later = [lambda: group(late)] + ([] if nxt[2] else [lambda: issue_split(PO)] * 2)
            H.later += [lambda: H.make(1), lambda: allow.update(allowed)]
            return H

        def proj_feat(nblocks, src, c0, c1, evac, marks):
            H1, H2 = src
            N = c1 - c0
            at = marks if callable(marks) else (lambda kt: marks)
            for nb in range(nblocks):
                bs = [bank(), bank()]
                for kk in range(2):
                    k, wh, wl, wm = take()
                    for m in range(2):
                        b, fr = bs[m]
                        for q in range(4):
                            kt = kk * 4 + q
                            last = mm3(b[:, 0:N], (wh[:, q, m * 128:m * 128 + 128], wl[:, q, m * 128:m * 128 + 128]),
                                       (H1[:, kt, c0:c1], H2[:, kt, c0:c1]), kt == 0, kt == 7,
                                       (fr, wm, at(kt)), inc=(q == 3))
                        if kk == 1:
                            bs[m] = (b, last)
                    gave(k, last)
                for m in range(2):
                    evac(nb * 2 + m, bs[m][0], bs[m][1])

        def proj_feat_halves(src, H, evac):
            H1, H2 = src
            slots = take4(False)
            bs = [bank() for _ in range(4)]
            for hf in range(2):
                if hf == 1:
                    H.rest()
                c = hf * 256
                for nb in range(2):
                    for kk in range(2):
                        k, wh, wl, wm = slots[nb * 2 + kk]
                        for m in range(2):
                            b, fr = bs[nb * 2 + m][0], bs[nb * 2 + m][1]
                            for q in range(4):
                                kt = kk * 4 + q
                                last = mm3(b[:, c:c + 256], (wh[:, q, m * 128:m * 128 + 128], wl[:, q, m * 128:m * 128 + 128]),
                                           (H1[:, kt, c:c + 256], H2[:, kt, c:c + 256]), kt == 0, kt == 7,
                                           (fr, wm, H.at(kt, hf)), inc=(q == 3))
                            if hf == 1 and kk == 1:
                                bs[nb * 2 + m] = (b, last)
                        if hf == 1:
                            gave(k, last)
            issue_split()
            issue_split()
            for n in range(4):
                evac(n, bs[n][0], bs[n][1])

        def proj_tok_halves(src, tiles, H, evac):
            H1, H2 = src
            slots = take4(False)
            got = []
            for t in tiles:
                if t == 2:
                    H.rest()
                b, fr = bank()
                for kk in range(4):
                    k, wh, wl, wm = slots[kk]
                    for q in range(2):
                        kt = kk * 2 + q
                        last = mm3(b[:, :], (H1[:, kt, t * 128:t * 128 + 128], H2[:, kt, t * 128:t * 128 + 128]),
                                   (wh[:, q, :], wl[:, q, :]), kt == 0, kt == 7, (fr, wm, H.at(kt, t // 2)), inc=(q == 1))
                    if t == tiles[-1]:
                        gave(k, last)
                got.append((t, b, last))
            H.rest()
            issue_split()
            issue_split()
            for t, b, last in got:
                evac(0, t, b, last)

        def proj_tok(src, nk, tiles, nhalves, evac, marks, width=512, off=0, first=0):
            H1, H2 = src
            at = marks if callable(marks) else (lambda kt: marks)
            for nh in range(first, first + nhalves):
                bs = {t: bank() for t in tiles}
                for kk in range(nk // 2):
                    k, wh, wl, wm = take()
                    for t in tiles:
                        b, fr = bs[t][0], bs[t][1]
                        o = (t - off) * 128
                        for q in range(2):
                            kt = kk * 2 + q
                            last = mm3(b[:, 0:width], (H1[:, kt, o:o + 128], H2[:, kt, o:o + 128]),
                                       (wh[:, q, 0:width], wl[:, q, 0:width]), kt == 0, kt == nk - 1,
                                       (fr, wm, at(kt)), inc=(q == 1))
                        if kk == nk // 2 - 1:
                            bs[t] = (b, last)
                    gave(k, last)
                for t in tiles:
                    evac(nh, t, bs[t][0], bs[t][1])

        def proj_last(src, tiles, evac, marks, off=0):
            H1, H2 = src
            at = marks if callable(marks) else (lambda kt: marks)
            proj_tok(src, 8, tiles, 1, evac, marks, off=off)
            for key in needed:
                ensure(key)
            while early:
                early.pop(0)()
            slots = take4()
            pend = {}
            for t in tiles:
                b, fr = bank()
                o = (t - off) * 128
                for kk in range(4):
                    k, wh, wl, wm = slots[kk]
                    for q in range(2):
                        kt = kk * 2 + q
                        last = mm3(b[:, :], (H1[:, kt, o:o + 128], H2[:, kt, o:o + 128]), (wh[:, q, :], wl[:, q, :]),
                                   kt == 0, kt == 7, (fr, wm, at(kt)), inc=(q == 1))
                    if t == tiles[-1]:
                        gave(k, last)
                pend[t] = lambda t=t, b=b, last=last: evac(1, t, b, last)
            return pend

        needed = []
        early = []
        early_h = []
        flip = [0]

        def copy_out(o, i, *marks):
            flip[0] ^= 1
            if flip[0]:
                return act(o, i, ACT.Copy, *marks)
            return cp(o, i, *marks)

        def y_evac_for(ym, yfree, first=True, final=True):
            def f(nh, t, b, p):
                o = Y4[:, t, nh * 512:nh * 512 + 512]
                if first:
                    m = copy_out(o, b[:, :], p, yfree)
                else:
                    m = tt(o, o, b[:, :], ALU.add, p, ym.get((t, nh)))
                release(b, m)
                if final:
                    m = [m, sumsq(o, ysq[:, t * 2 + nh:t * 2 + nh + 1], m)]
                ym[(t, nh)] = m
            return f

        def shifted(evac, d):
            return lambda n, b, p: evac(n + d, b, p)

        def mlp(li, tiles, hm, stack):
            c0 = tiles[0] * 128
            N = len(tiles) * 128
            if len(tiles) == 2:
                hm.rest()
            fz = fence()
            UH = sb(f"UH{li}", [128, 8, 512], F32R, stack)
            UL = sb(f"UL{li}", [128, 8, 512], F32R, stack)
            ym = {}
            ufree = [[fz] for _ in range(8)]
            for q in range(4):
                um = []

                def evac(n, b, p, um=um):
                    t1, tf, ti = tmp()
                    a = act(t1[:, 0:N], b[:, 0:N], ACT.Relu, p, tf)
                    release(b, a)
                    t2, tf2, ti2 = tmp()
                    g = tt(t2[:, 0:N], t1[:, 0:N], t1[:, 0:N], ALU.mult, a, tf2, q=PO)
                    a = act(UH[:, n, 0:N], t1[:, 0:N], ACT.Square, a, ufree[n])
                    tmp_free[ti] = [g, a]
                    v = tt(UL[:, n, 0:N], t2[:, 0:N], UH[:, n, 0:N].bitcast(F32), ALU.subtract, a, g, ufree[n])
                    tmp_free[ti2] = [v]
                    um.append([a, v])

                if q == 0 and N == 512:
                    proj_feat_halves((HH, HL), hm, evac)
                    fz = fence()
                    proj_feat(2, (HH, HL), c0, c0 + N, shifted(evac, 4), hm)
                else:
                    hm.rest()
                    proj_feat(4, (HH, HL), c0, c0 + N, evac, hm)
                if q < 3:
                    proj_tok((UH, UL), 8, tiles, 2, y_evac_for(ym, fz, q == 0, False), lambda kt: um[kt], off=tiles[0])
                else:
                    pend = proj_last((UH, UL), tiles, y_evac_for(ym, fz, False, True), lambda kt: um[kt], off=tiles[0])
                ufree = [[PE.last()] for _ in range(8)]
            return pend, ym

        def hi_lo(oh, ol, src, *marks):
            a = act(oh, src, ACT.Copy, *marks)
            v = tt(ol, src, oh.bitcast(F32), ALU.subtract, a, *marks)
            return [a, v]

        def mla(li, hm, stack):
            fz = fence()
            with ExitStack() as s1:
                CQH = sb("CQH", [128, 3, 512], F32R, s1)
                CQL = sb("CQL", [128, 3, 512], F32R, s1)
                CKH = sb("CKH", [128, 2, 512], F32R, s1)
                CKL = sb("CKL", [128, 2, 512], F32R, s1)
                krT = sb("krT", [64, 512], F32, s1)
                cs = sb("cs", [64, 2, 256], F32, s1)
                rot = sb("rot", [64, 64], F32, s1)
                grow = sb("grow", [5, 128], F32, s1)
                gcol = sb("gcol", [128, 5], F32, s1)
                qn = [sb(f"qn{i}", [128, 512], F32, s1) for i in range(2)]
                kn = [sb(f"kn{i}", [128, 512], F32, s1) for i in range(2)]
                qr = [sb(f"qr{i}", [64, 512], F32, s1) for i in range(2)]
                Pl = [sb(f"Pl{i}", [128, 512], F32, s1) for i in range(4)]
                Pc = [sb(f"Pc{i}", [128, 256], F32, s1) for i in range(4)]
                PTl = sb("PTl", [128, 4, 256], F32, s1)
                PTc = sb("PTc", [128, 2, 256], F32, s1)
                CQ = Y[:, 0:2816].rearrange("p (t n) -> p t n", t=4)
                VV = [Y[:, o:o + 512].rearrange("p (t n) -> p t n", t=4) for o in (2816, 3328, 0)]
                mc1 = mload(cs[:, 0, :], cap("cos")[0:64, :])
                mc2 = mload(cs[:, 1, :], cap("sin")[0:64, :])
                mr = mload(rot[:], cap("rot")[0:64, :])
                mg1 = mload(grow[0:3, :], A["mla_g_q"][0].rearrange("(r p) -> r p", p=128))
                mg2 = mload(grow[3:5, :], A["mla_g_kv"][0].rearrange("(r p) -> r p", p=128))
                b, fr = bank()
                p = tr(b[:, 0:5], grow[:], ident[0:5, 0:5], fr, mg1, mg2)
                mg = cp(gcol[:], b[:, 0:5], p)
                release(b, mg)
                cm = {}

                def ev(off, w):
                    def f(nh, t, b, p):
                        m = copy_out(CQ[:, t, off:off + w], b[:, 0:w], p, fz)
                        cm[(t, off)] = m
                        release(b, m)
                    return f

                proj_tok((HH, HL), 8, [0, 1, 2, 3], 1, ev(0, 384), hm, width=384)

                def normed(c0, n):
                    s = stats()
                    for t in range(4):
                        m1 = sumsq(CQ[:, t, c0:c0 + n], s[:, 0, t:t + 1], cm[(t, c0)])
                    r, rm = rstd(s, 4, n, [m1])
                    return [ts(CQ[:, t, c0:c0 + n], CQ[:, t, c0:c0 + n], r[:, t:t + 1], None, ALU.mult, None, rm, m1,
                               cm[(t, c0)]) for t in range(4)]

                nq = normed(0, 384)
                proj_tok((HH, HL), 8, [0, 1, 2, 3], 1, ev(384, 320), hm, width=320)
                nk_ = normed(384, 256)
                for f in (5, 0, 1, 2, 3, 4):
                    w = 128 if f < 5 else 64
                    nm = (nq if f < 3 else nk_) if f < 5 else [cm[(t, 384)] for t in range(4)]
                    b, fr = bank()
                    PE.wait(fr)
                    for t in range(4):
                        p = tr(b[0:w, t * 128:t * 128 + 128], CQ[:, t, f * 128:f * 128 + w], ident[:], nm[t])
                    if f < 5:
                        oh, ol = (CQH[:, f, :], CQL[:, f, :]) if f < 3 else (CKH[:, f - 3, :], CKL[:, f - 3, :])
                        a = act(oh, b[:, :], ACT.Copy, p, mg, fz, scale=gcol[:, f:f + 1])
                        v = stt(ol, b[:, :], gcol[:, f:f + 1], oh.bitcast(F32), ALU.mult, ALU.subtract, a)
                        release(b, v)
                        if f < 3:
                            cqm = [a, v]
                        else:
                            ckm = [a, v]
                    else:
                        a = cp(krT[:], b[0:64, :], p, fz)
                        release(b, a)
                        krm = a

                def rope(x, xm):
                    b, fr = bank()
                    p = mm(b[0:64, 0:256], rot[:], x[:, 256:512], True, True, (fr, xm, mr), inc=True)
                    t1, tf, ti = tmp()
                    v1 = tt(t1[0:64, 0:256], b[0:64, 0:256], cs[:, 1, :], ALU.mult, p, mc2, tf)
                    release(b, v1)
                    v2 = tt(x[:, 256:512], x[:, 256:512], cs[:, 0, :], ALU.mult, p, mc1, xm)
                    v3 = tt(x[:, 256:512], x[:, 256:512], t1[0:64, 0:256], ALU.add, v1, v2)
                    tmp_free[ti] = [v3]
                    return v3

                krm = rope(krT, krm)
                SC = 192.0 ** -0.5
                sfree = [[fz], [fz]]
                vfree = [[fz, cqm, ckm, krm] for _ in range(3)]
                Plf = [[fz] for _ in range(4)]
                Pcf = [[fz] for _ in range(4)]
                PTfree = [fz]
                om = []

                def stage_a(h):
                    i = h % 2
                    k, wh, wl, wm = take()
                    b, fr = bank()
                    for q in range(3):
                        p = mm3(b[:, :], (wh[:, q, 0:128], wl[:, q, 0:128]), (CQH[:, q, :], CQL[:, q, :]),
                                q == 0, q == 2, (fr, wm, cqm), inc=(q == 2))
                    a1 = act(qn[i][:], b[:, :], ACT.Copy, p, sfree[i])
                    release(b, a1)
                    b, fr = bank()
                    for q in range(3):
                        p = mm3(b[0:64, :], (wh[:, q, 128:192], wl[:, q, 128:192]), (CQH[:, q, :], CQL[:, q, :]),
                                q == 0, q == 2, (fr,), inc=(q == 2))
                    gave(k, p)
                    v1 = cp(qr[i][:], b[0:64, :], p, sfree[i])
                    release(b, v1)
                    k, wh, wl, wm = take()
                    b, fr = bank()
                    for q in range(2):
                        p = mm3(b[:, :], (wh[:, q, 0:128], wl[:, q, 0:128]), (CKH[:, q, :], CKL[:, q, :]),
                                q == 0, q == 1, (fr, wm, ckm), inc=(q == 1))
                    a2 = act(kn[i][:], b[:, :], ACT.Copy, p, sfree[i])
                    release(b, a2)
                    b, fr = bank()
                    PE.wait(fr)
                    for t in range(4):
                        for q in range(2):
                            p = mm3(b[:, t * 128:t * 128 + 128],
                                    (CKH[:, q, t * 128:t * 128 + 128], CKL[:, q, t * 128:t * 128 + 128]),
                                    (wh[:, q, 128:256], wl[:, q, 128:256]), q == 0, q == 1, (),
                                    inc=(q == 1 and t == 3))
                    gave(k, p)
                    v2 = cp(VV[h % 3], b[:, :].rearrange("p (t n) -> p t n", t=4), p, vfree[h % 3])
                    release(b, v2)
                    v1 = rope(qr[i], v1)
                    return (i, a1, a2, v1, v2)

                def scores(h, S):
                    i, a1, a2, v1, v2 = S
                    marks = (a1, a2, v1, krm)
                    pm = []
                    raw = []
                    for half, nk, PB, PF in ((1, 512, Pl, Plf), (0, 256, Pc, Pcf)):
                        for t in range(2):
                            c = half * 256 + t * 128
                            b, fr = bank()
                            mm(b[:, 0:nk], qn[i][:, c:c + 128], kn[i][:, 0:nk], True, False, (fr, marks))
                            p = mm(b[:, 0:nk], qr[i][:, c:c + 128], krT[:, 0:nk], False, True, inc=True)
                            s = stats()
                            m = rmax(s[:, 0, 0:1], b[:, 0:nk], AX.X, p)
                            m = ts(s[:, 1, 0:1], s[:, 0, 0:1], -SC, None, ALU.mult, None, m)
                            a = act(PB[2 * i + t][:, 0:nk], b[:, 0:nk], ACT.Exp, m, PF[2 * i + t], bias=s[:, 1, 0:1], scale=SC,
                                    accum_out=s[:, 2, 0:1])
                            release(b, a)
                            raw.append((s, a, PB[2 * i + t], nk))
                    for s, a, P_, nk in raw:
                        m = rcp(s[:, 3, 0:1], s[:, 2, 0:1], a)
                        pm.append(ts(P_[:, 0:nk], P_[:, 0:nk], s[:, 3, 0:1], None, ALU.mult, None, m))
                    sfree[i] = [p]
                    return pm

                def values(h, S, pm):
                    i, a1, a2, v1, v2 = S
                    ptm = []
                    n = 0
                    for half, nk, PB, PF, PT in ((1, 4, Pl, Plf, PTl), (0, 2, Pc, Pcf, PTc)):
                        for t in range(2):
                            b, fr = bank()
                            PE.wait(fr, pm[n])
                            for kt in range(nk):
                                p = tr(
                                    b[:, kt * 128:kt * 128 + 128], PB[2 * i + t][:, kt * 128:kt * 128 + 128], ident[:])
                            PF[2 * i + t] = [p]
                            m = copy_out(PT[:, :, t * 128:t * 128 + 128],
                                         b[:, 0:nk * 128].rearrange("p (k n) -> p k n", k=nk), p, PTfree)
                            release(b, m)
                            ptm.append(m)
                            n += 1
                    b, fr = bank()
                    for kt in range(4):
                        mm(b[:, 256:512], VV[h % 3][:, kt, :], PTl[:, kt, :], kt == 0, kt == 3, (fr, ptm, v2))
                    for kt in range(2):
                        p = mm(b[:, 0:256], VV[h % 3][:, kt, :], PTc[:, kt, :], kt == 0, kt == 1, inc=(kt == 1))
                    PTfree[:] = [p]
                    vfree[h % 3] = [p]
                    m = hi_lo(HH[:, h, :], HL[:, h, :], b[:, :], p)
                    release(b, m)
                    om.append(m)

                SA = {0: stage_a(0)}
                prev = None
                for h in range(9):
                    if h < 7:
                        SA[h + 1] = stage_a(h + 1)
                    cur = (SA[h], scores(h, SA[h])) if h < 8 else None
                    if prev is not None:
                        values(h - 1, *prev)
                    prev = cur
                fz2 = fence()
            ym = {}
            return proj_last((HH, HL), [0, 1, 2, 3], y_evac_for(ym, fz2), lambda kt: om[kt]), ym

        def gla(li, hm, stack):
            fz = fence()
            S = Y[:, 0:2048].rearrange("p (r h n) -> p r h n", r=2, h=4)
            VL = Y[:, 2048:4096].rearrange("p (t n) -> p t n", t=2)
            with ExitStack() as s1:
                cst = sb("g_cst", [128, 9, 128], F32, s1)
                cum, end, endc = (lambda r: cst[:, r, :]), (lambda r: cst[:, 2 + r, :]), (lambda r: cst[:, 4 + r, :])
                tot, gmask = cst[:, 6, :], (lambda r: cst[:, 7 + r, :])
                z = sb("g_z", [65, 512], F32, s1)
                w2p = sb("g_w2p", [65, 2, 512], F32, s1)
                KLt = sb("g_klt", [128, 2, 512], F32, s1)
                gxa = sb("g_gx", [128, 2, 4, 512], F32, s1)
                qT = sb("g_qT", [128, 4, 256], F32, s1)
                go = sb("g_go", [128, 2], F32, s1)
                gor = sb("g_gor", [2, 128], F32, s1)
                gmarks = []

                def log_gate(r, t, dst, *marks):
                    b, fr = bank()
                    p = mm(b[:, :], z[:, t * 128:t * 128 + 128], w2p[:, r, :], True, True, (fr, gmarks), inc=True)
                    t1, tf, ti = tmp()
                    a = act(t1[:], b[:, :], ACT.Abs, p, tf)
                    a = act(t1[:], t1[:], ACT.Exp, a, scale=-1.0)
                    a = act(t1[:], t1[:], ACT.Ln, a, bias=ones[:, 0:1])
                    v = stt(dst, b[:, :], 0.0, t1[:], ALU.min, ALU.subtract, a, marks)
                    release(b, v)
                    tmp_free[ti] = [v]
                    return v

                with ExitStack() as s2:
                    KC = sb("g_kc", [128, 2, 512], F32, s2)
                    VC = sb("g_vc", [128, 2, 1024], F32, s2)
                    KE = sb("g_ke", [128, 2, 2, 512], F32, s2)
                    km, vm = {}, {}

                    def evk(nh, t, b, p):
                        dst = KC[:, t, :] if t < 2 else KLt[:, t - 2, :]
                        km[t] = copy_out(dst, b[:, :], p, fz)
                        release(b, km[t])

                    def evv(nh, t, b, p):
                        dst = (VC[:, t, :] if t < 2 else VL[:, t - 2, :])[:, nh * 512:nh * 512 + 512]
                        vm[(t, nh)] = copy_out(dst, b[:, :], p, fz)
                        release(b, vm[(t, nh)])

                    proj_tok_halves((HH, HL), [0, 1, 2, 3], hm, evk)
                    fz = fence()
                    mcs = mload(cst[:].rearrange("p a n -> p (a n)"), A["consts"][:, CONST_SLICES["cum"][0]:
                                CONST_SLICES["cum"][0] + 1152], fz)
                    v = mset(z[:], 1.0, fz)
                    v0 = mset(w2p[:], 0.0, fz)
                    zm0 = v
                    wm2 = []
                    for r in range(2):
                        wm2.append(mload(w2p[32 * r:32 * r + 16, r, :], A["gla_w_gate2"][0, r], v0))
                        wm2.append(mload(w2p[64:65, r, :], A["gla_b_gate"][0:1, r, :], v0))
                    mgo = mload(gor[:], A["gla_g_o"][0].rearrange("(r p) -> r p", p=128), fz)
                    gmarks.append(wm2)
                    zc = []
                    for r in range(2):
                        k, wh, wl, wm = take()
                        b, fr = bank()
                        for q in range(8):
                            p = mm3(b[0:16, :], (wh[:, q, :], wl[:, q, :]), (HH[:, q, :], HL[:, q, :]), q == 0, q == 7,
                                    (fr, wm, hm(q)), inc=(q == 7))
                        gave(k, p)
                        v = cp(z[32 * r:32 * r + 16, :], b[0:16, :], p, zm0)
                        release(b, v)
                        zc.append(v)
                    gmarks.append(zc)

                    proj_tok((HH, HL), 8, [0, 1, 2, 3], 1, evv, hm)
                    gm = {(r, t): log_gate(r, t, gxa[:, r, t, :], fz) for r in range(2) for t in range(2)}
                    proj_tok((HH, HL), 8, [0, 1, 2, 3], 1, evv, hm, first=1)
                    kem = []
                    for r in range(2):
                        for t in range(2):
                            b, fr = bank()
                            far = 1 if r == 0 else 0
                            p = mm(b[:, :], endc(r), gxa[:, r, t, :], True, t == far, (fr, gm[(r, 0)], gm[(r, 1)], mcs), inc=True)
                            if t != far:
                                p = mm(b[:, :], tot, gxa[:, r, far, :], False, True, inc=True)
                            a = act(KE[:, r, t, :], b[:, :], ACT.Exp, p, fz)
                            release(b, a)
                            kem.append(tt(KE[:, r, t, :], KE[:, r, t, :], KC[:, t, :], ALU.mult, a, km[t]))
                    qm = {}

                    def evq(n, b, p):
                        qm[n] = act(qT[:, n, :], b[:, 0:256], ACT.Copy, p, fz, scale=128.0 ** -0.5)
                        release(b, qm[n])

                    proj_feat(1, (HH, HL), 256, 512, evq, hm)
                    for r in range(2):
                        for t in range(2, 4):
                            gm[(r, t)] = log_gate(r, t, gxa[:, r, t, :], fz)
                    proj_feat(1, (HH, HL), 256, 512, shifted(evq, 2), hm)
                    Sm = {}
                    for r in range(2):
                        for hp in range(2):
                            b, fr = bank()
                            PE.wait(fr, kem)
                            for hh in range(2):
                                h = hp * 2 + hh
                                for t in range(2):
                                    p = mm(b[:, hh * 256:hh * 256 + 256], KE[:, r, t, h * 128:h * 128 + 128],
                                           VC[:, t, h * 256:h * 256 + 256], t == 0, t == 1,
                                           (vm[(t, h // 2)],), inc=True)
                            m = copy_out(S[:, r, hp * 2:hp * 2 + 2, :],
                                         b[:, :].rearrange("p (h n) -> p h n", h=2), p, fz)
                            release(b, m)
                            Sm[(r, hp * 2)] = Sm[(r, hp * 2 + 1)] = m
                    fz2 = fence()
                with ExitStack() as s2:
                    kT = sb("g_kT", [128, 4, 256], F32, s2)
                    EG = sb("g_eg", [128, 4, 128], F32, s2)
                    EN = sb("g_en", [128, 4, 128], F32, s2)
                    qt = sb("g_qt", [128, 4, 128], F32, s2)
                    kt_ = sb("g_ktt", [128, 4, 128], F32, s2)
                    KE = sb("g_kel", [128, 512], F32, s2)
                    AT = [sb(f"g_at{r}", [128, 4, 128], F32, s2) for r in range(2)]
                    az = [mset(AT[r][:], 0.0, fz2) for r in range(2)]
                    ktm = {}
                    for hp in range(2):
                        b, fr = bank()
                        PE.wait(fr, km[2], km[3])
                        for hh in range(2):
                            h = hp * 2 + hh
                            for t in range(2):
                                p = tr(
                                    b[:, hh * 256 + t * 128:hh * 256 + t * 128 + 128],
                                    KLt[:, t, h * 128:h * 128 + 128], ident[:])
                        m = copy_out(kT[:, hp * 2:hp * 2 + 2, :], b[:, :].rearrange("p (h n) -> p h n", h=2), p, fz2)
                        release(b, m)
                        ktm[hp] = m
                    OB = [[bank() for _ in range(2)] for _ in range(2)]
                    started = set()
                    use = [None]
                    atfree = [None, None]
                    kefree = [None]
                    for r in range(2):
                        for ti_, t in enumerate([0, 1] if r == 0 else [1, 0]):
                            b, fr = bank()
                            PE.wait(fr, gm[(r, 2)], gm[(r, 3)], mcs)
                            for h in range(4):
                                p = mm(b[:, h * 128:h * 128 + 128], gxa[:, r, 2 + t, h * 128:h * 128 + 128], cum(r), True, True,
                                       inc=True)
                            bv = b[:, :].rearrange("p (h n) -> p h n", h=4)
                            a1 = act(EG[:], bv, ACT.Exp, p, use[0], fz2)
                            a2 = act(EN[:], bv, ACT.Exp, p, use[0], fz2, scale=-1.0)
                            release(b, a2)
                            v1 = tt(qt[:], EG[:], qT[:, :, t * 128:t * 128 + 128], ALU.mult, a1, list(qm.values()),
                                    use[0], fz2)
                            v2 = tt(kt_[:], EN[:], kT[:, :, t * 128:t * 128 + 128], ALU.mult, a2, ktm[0], ktm[1],
                                    use[0], fz2)
                            b, fr = bank()
                            p = mm(b[:, :], end(r), gxa[:, r, 2 + t, :], True, True, (fr,), inc=True)
                            a3 = act(KE[:], b[:, :], ACT.Exp, p, kefree[0], fz2)
                            release(b, a3)
                            v3 = tt(KE[:], KE[:], KLt[:, t, :], ALU.mult, a3, km[2 + t])
                            b, fr = bank()
                            PE.wait(fr, v1, v2)
                            for h in range(4):
                                p = mm(b[:, h * 128:h * 128 + 128], kt_[:, h, :], qt[:, h, :], True, True, inc=True)
                            mk = gmask(r).bitcast(I32)
                            for h in range(4):
                                v4 = cpred(
                                    AT[r][:, h, :], mk, b[:, h * 128:h * 128 + 128], p, az, atfree[r], mcs)
                            release(b, v4)
                            for h in range(4):
                                ob, ofr = OB[t][h // 2]
                                first = (t, h // 2) not in started
                                started.add((t, h // 2))
                                p = mm(ob[:, (h % 2) * 256:(h % 2) * 256 + 256], AT[r][:, h, :],
                                       VL[:, t, h * 256:h * 256 + 256], first, False,
                                       (ofr, v4, vm[(2 + t, h // 2)]), inc=True)
                            atfree[r] = p
                            for ci, c in enumerate([0, 1] if r == 0 else [1, 0]):
                                last_chunk = ti_ == 1 and ci == 1
                                pr = {}
                                for h in range(4):
                                    ob = OB[t][h // 2][0]
                                    pr[h] = mm(ob[c * 64:c * 64 + 64, (h % 2) * 256:(h % 2) * 256 + 256],
                                               qt[:, h, c * 64:c * 64 + 64], S[:, r, h, :], False, False,
                                               (Sm[(r, h)],), inc=True)
                                use[0] = pr[3]
                                if last_chunk:
                                    continue
                                for hp in range(2):
                                    b, fr = bank()
                                    PE.wait(fr, v3)
                                    for hh in range(2):
                                        h = hp * 2 + hh
                                        p = mm(b[:, hh * 256:hh * 256 + 256],
                                               KE[c * 64:c * 64 + 64, h * 128:h * 128 + 128],
                                               VL[c * 64:c * 64 + 64, t, h * 256:h * 256 + 256], True, True, inc=True)
                                    for hh in range(2):
                                        h = hp * 2 + hh
                                        gi = c * 64 + (63 if r == 0 else 0)
                                        Sm[(r, h)] = stt(S[:, r, h, :], S[:, r, h, :], EG[:, h, gi:gi + 1],
                                                         b[:, hh * 256:hh * 256 + 256], ALU.mult, ALU.add, p, pr[h],
                                                         Sm[(r, h)])
                                    release(b, Sm[(r, h)])
                                kefree[0] = p
                                use[0] = [pr[3], Sm[(r, 3)], p]
                    of = PE.last()
                    fz3 = fence()
                with ExitStack() as s2:
                    OH = sb("g_oh", [128, 8, 256], F32R, s2)
                    OL = sb("g_ol", [128, 8, 256], F32R, s2)
                    sr = gxa[:, 0, :, :].rearrange("p t (a n) -> p (t a) n", a=2)
                    b, fr = bank()
                    p = tr(b[:, 0:2], gor[:], ident[0:2, 0:2], fr, mgo)
                    gom = cp(go[:], b[:, 0:2], p, fz3)
                    release(b, gom)
                    Z = Y4[:, 0:2, :]
                    zm = []
                    s = stats()
                    s_ = None
                    for t in range(2):
                        for h in range(4):
                            ob = OB[t][h // 2][0]
                            m = sumsq(ob[:, (h % 2) * 256:(h % 2) * 256 + 256], s[:, 0, t * 4 + h:t * 4 + h + 1], of)
                    rr, rm = rstd(s, 8, 256, [m])
                    for t in range(2):
                        for h in range(4):
                            ob = OB[t][h // 2][0]
                            m = act(Z[:, t, h * 256:h * 256 + 256], ob[:, (h % 2) * 256:(h % 2) * 256 + 256], ACT.Copy,
                                    rm, fz3, scale=rr[:, t * 4 + h:t * 4 + h + 1])
                            if h % 2 == 1:
                                release(ob, m)
                        zm.append(m)
                    srm = {}

                    def evr(n, b, p):
                        t1, tf, ti = tmp()
                        a = act(t1[:, 0:256], b[:, 0:256], ACT.Exp, p, tf, scale=-1.0)
                        a = act(t1[:, 0:256], t1[:, 0:256], ACT.Ln, a, bias=ones[:, 0:1])
                        a = act(t1[:, 0:256], t1[:, 0:256], ACT.Exp, a, scale=-1.0)
                        v = tt(sr[:, n, :], b[:, 0:256], t1[:, 0:256], ALU.mult, a, fz3)
                        release(b, v)
                        tmp_free[ti] = [v]
                        srm[n] = v

                    om = []

                    def part(fp):
                        b, fr = bank()
                        PE.wait(fr, zm)
                        for k in range(2):
                            f = fp * 2 + k
                            for t in range(2):
                                p = tr(b[:, k * 256 + t * 128:k * 256 + t * 128 + 128],
                                       Z[:, t, f * 128:f * 128 + 128], ident[:])
                        t1, tf, ti = tmp()
                        for k in range(2):
                            f = fp * 2 + k
                            v = stt(t1[:, k * 256:k * 256 + 256], b[:, k * 256:k * 256 + 256],
                                    go[:, f % 2:f % 2 + 1], sr[:, f, :], ALU.mult, ALU.mult, p, tf, gom, srm[f])
                        release(b, v)
                        m = hi_lo(OH[:, fp * 2:fp * 2 + 2, :], OL[:, fp * 2:fp * 2 + 2, :],
                                  t1[:, :].rearrange("p (k n) -> p k n", k=2), v, fz3)
                        tmp_free[ti] = m
                        om.append(m)

                    for nb in range(4):
                        proj_feat(1, (HH, HL), 256, 512, shifted(evr, nb * 2), hm)
                        if nb:
                            part(nb - 1)
                    part(3)
                    fz4 = fence()
            ym = {}
            return proj_last((OH, OL), [2, 3], y_evac_for(ym, fz4), lambda kt: om[kt // 2], off=2), ym

        def conv(li, hm, stack):
            fz = fence()
            BH = sb("c_bh", [128, 8, 512], F32R, stack)
            BL = sb("c_bl", [128, 8, 512], F32R, stack)
            cu = [sb(f"c_cu{i}", [128, 522], F32, stack) for i in range(2)]
            cv = [sb(f"c_cv{i}", [128, 512], F32, stack) for i in range(2)]
            cwr = sb("c_wr", [24, 128], F32, stack)
            cwc = sb("c_wc", [128, 24], F32, stack)
            cwm = cz = None

            def taps():
                nonlocal cwm, cz
                mw = mload(cwr[:], A["conv_w_2"][0].rearrange("a (r p) -> (a r) p", p=128), fz)
                b, fr = bank()
                p = tr(b[:, 0:24], cwr[:], ident[0:24, 0:24], fr, mw)
                cwm = cp(cwc[:], b[:, 0:24], p, fz)
                release(b, cwm)
                cz = [mset(cu[i][:], 0.0, fz) for i in range(2)]

            cufree = [None, None]
            cvfree = [None, None]
            om = []

            def view(i, sft, seg):
                if seg == 0:
                    return cu[i][:, 1 + sft:257 + sft]
                return cu[i][:, 258:522].rearrange("p (r n) -> p r n", r=4)[:, :, 1 + sft:65 + sft]

            for g in range(4):
                got = {}

                def ev(part, g=g, got=got):
                    def f(n, b, p):
                        d = g * 2 + n
                        i = n
                        if part == "c":
                            got[("c", i)] = act(cv[i][:], b[:, :], ACT.Copy, p, fz, cvfree[i])
                            release(b, got[("c", i)])
                        elif part == "u":
                            m = tt(view(i, 0, 0), b[:, 0:256], cv[i][:, 0:256], ALU.mult, p, got[("c", i)], cz,
                                   cufree[i])
                            m = tt(view(i, 0, 1), b[:, 256:512].rearrange("p (r n) -> p r n", r=4),
                                   cv[i][:, 256:512].rearrange("p (r n) -> p r n", r=4), ALU.mult)
                            release(b, m)
                            for seg in range(2):
                                o = cv[i][:, seg * 256:seg * 256 + 256]
                                if seg:
                                    o = o.rearrange("p (r n) -> p r n", r=4)
                                m = ts(o, view(i, -1, seg), cwc[:, d:d + 1], None, ALU.mult, None, m, cwm)
                                m = stt(o, view(i, 0, seg), cwc[:, 8 + d:9 + d], o, ALU.mult, ALU.add, m)
                                m = stt(o, view(i, 1, seg), cwc[:, 16 + d:17 + d], o, ALU.mult, ALU.add, m)
                            cufree[i] = m
                            got[("y", i)] = m
                        else:
                            m = tt(cv[i][:], cv[i][:], b[:, :], ALU.mult, p, got[("y", i)])
                            release(b, m)
                            m = hi_lo(BH[:, d, :], BL[:, d, :], cv[i][:], m, fz)
                            cvfree[i] = m
                            om.append(m)
                    return f

                if g == 0:
                    evc, evu = ev("c"), ev("u")
                    hm.later.append(taps)
                    proj_feat_halves((HH, HL), hm, lambda n, b, p: evc(n, b, p) if n < 2 else evu(n - 2, b, p))
                    fz = fence()
                else:
                    proj_feat(1, (HH, HL), 0, 512, ev("c"), hm)
                    proj_feat(1, (HH, HL), 0, 512, ev("u"), hm)
                proj_feat(1, (HH, HL), 0, 512, ev("b"), hm)
            ym = {}
            return proj_last((BH, BL), [0, 1, 2, 3], y_evac_for(ym, fz), lambda kt: om[kt]), ym

        def mlstm(li, hm, stack):
            fz = fence()
            ac_ = [Y[:, r * 2064:(r + 1) * 2064].rearrange("p (t h n) -> p t h n", t=2, h=8) for r in range(2)]
            with ExitStack() as s1:
                msk = sb("m_msk", [128, 2, 2, 256], F32, s1)
                sel = sb("m_sel", [8, 8, 128], F32, s1)
                qT = sb("m_qT", [128, 4, 256], F32, s1)
                kT = sb("m_kT", [128, 4, 256], F32, s1)
                VLe = sb("m_vl", [128, 2, 8, 129], F32, s1)
                C = sb("m_C", [128, 2, 4, 129], F32, s1)
                M = sb("m_M", [8, 2, 256], F32, s1)
                cols = sb("m_cols", [128, 2, 8, 8], F32, s1)
                nwc = sb("m_nwc", [128, 8], F32, s1)
                qm, ktm = {}, {}

                def evq(n, b, p):
                    qm[n] = act(qT[:, n, :], b[:, 0:256], ACT.Copy, p, fz, scale=0.125)
                    release(b, qm[n])

                def evkt(n, b, p):
                    ktm[n] = cp(kT[:, n, :], b[:, 0:256], p, fz)
                    release(b, ktm[n])

                with ExitStack() as s2:
                    KC = sb("m_kc", [128, 2, 512], F32, s2)
                    KW = sb("m_kw", [128, 2, 512], F32, s2)
                    VCe = sb("m_vc", [128, 2, 8, 129], F32, s2)
                    gt = sb("m_gt", [128, 4, 2, 16], F32, s2)
                    gbi = sb("m_gb", [128, 32], F32, s2)
                    f_a = sb("m_fa", [128, 4, 2, 8], F32, s2)
                    rw = sb("m_rw", [8, 5, 256], F32, s2)
                    o8 = sb("m_o8", [8, 256], F32, s2)
                    sm = sb("m_sm", [8, 2, 4], F32, s2)
                    gr = sb("m_gr", [16, 512], F32, s2)
                    km, vm = {}, {}

                    def evk(nh, t, b, p):
                        km[t] = copy_out(KC[:, t, :], b[:, :], p, fz)
                        release(b, km[t])

                    def evv(nh, t, b, p):
                        dst = (VCe[:, t, :, :] if t < 2 else VLe[:, t - 2, :, :])[:, nh * 4:nh * 4 + 4, 0:128]
                        vm[(t, nh)] = copy_out(dst, b[:, :].rearrange("p (h n) -> p h n", h=4), p, fz)
                        release(b, vm[(t, nh)])

                    proj_tok_halves((HH, HL), [0, 1], hm, evk)
                    fz = fence()
                    mmk = mload(msk[:].rearrange("p a b n -> p (a b n)"), cap("mmask"), fz)
                    msl = mload(sel[:].rearrange("p a n -> p (a n)"), cap("sel")[0:8, :], fz)
                    on = mset(VLe[:, :, :, 128:129], 1.0, fz)
                    mo8 = mset(o8[:], 1.0, fz)
                    on2 = mset(VCe[:, :, :, 128:129], 1.0, fz)
                    mgb = mload(gbi[:], A["ml_b_if_2"][0].rearrange("r g -> (r g)").partition_broadcast(128), fz)
                    b2, fr2 = bank()
                    grf = fz
                    for r in range(2):
                        k, wh, wl, wm = take()
                        b, fr = bank()
                        for q in range(8):
                            p = mm3(b[0:16, :], (wh[:, q, :], wl[:, q, :]), (HH[:, q, :], HL[:, q, :]), q == 0, q == 7,
                                    (fr, wm, hm(q)), inc=(q == 7))
                        gave(k, p)
                        v = cp(gr[:], b[0:16, :], p, grf)
                        release(b, v)
                        for t in range(4):
                            p = tr(b2[:, r * 64 + t * 16:r * 64 + t * 16 + 16], gr[:, t * 128:t * 128 + 128],
                                   ident[0:16, 0:16], fr2, v)
                        grf = p
                    bv = b2[:, 0:128].rearrange("p (r t g) -> p r t g", r=2, t=4)
                    for r in range(2):
                        v = tt(gt[:, :, r, :], bv[:, r, :, :],
                               gbi[:, r * 16:r * 16 + 16].unsqueeze(1).to_broadcast([128, 4, 16]), ALU.add, p, mgb, fz)
                    release(b2, v)
                    fv = gt[:, :, :, 8:16]
                    a = act(f_a[:], fv, ACT.Abs, v, fz)
                    a = act(f_a[:], f_a[:], ACT.Exp, a, scale=-1.0)
                    a = act(f_a[:], f_a[:], ACT.Ln, a, bias=ones[:, 0:1])
                    v5 = ts(fv, fv, 0.0, None, ALU.min, None, v, a)
                    gtm = tt(fv, fv, f_a[:], ALU.subtract, v5, a)
                    proj_tok((HH, HL), 8, [0, 1, 2, 3], 1, evv, hm)
                    rowm = {}
                    cm = []

                    def rows(r):
                        bi, fri = bank()
                        bf, frf = bank()
                        PE.wait(fri, frf, gtm)
                        for t in range(4):
                            tr(bi[0:8, t * 128:t * 128 + 128], gt[:, t, r, 0:8], ident[:])
                            p = tr(bf[0:8, t * 128:t * 128 + 128], gt[:, t, r, 8:16], ident[:])
                        rv = (lambda x: x) if r == 0 else (lambda x: x[:, ::-1])
                        B, AA, WK = rw[:, 0, :], rw[:, 1, :], rw[:, 2, :]
                        prevc = cm[-1] if cm else None
                        v = scan(
                            rv(B), o8[:], rv(bf[0:8, 0:256]), 0.0, ALU.mult, ALU.add, p, mo8, fz, prevc)
                        v = tt(AA, bi[0:8, 0:256], B, ALU.subtract, v, p, prevc)
                        v = rmax(sm[:, r, 0:1], AA, AX.X, v)
                        v = ts(sm[:, r, 1:2], sm[:, r, 0:1], 0.0, -1.0, ALU.max, ALU.mult, v)
                        a = act(WK, AA, ACT.Exp, v, prevc, bias=sm[:, r, 1:2])
                        last = 255 if r == 0 else 0
                        mi = tt(sm[:, r, 2:3], B[:, last:last + 1], sm[:, r, 1:2], ALU.subtract, v)
                        BL_, AL_, WI, EM = rw[:, 3, :], rw[:, 4, :], rw[:, 0, :], rw[:, 1, :]
                        v = scan(
                            rv(BL_), o8[:], rv(bf[0:8, 256:512]), 0.0, ALU.mult, ALU.add, p, prevc)
                        release(bf, v)
                        v = tt(AL_, bi[0:8, 256:512], BL_, ALU.subtract, v)
                        release(bi, v)
                        MR = M[:, r, :]
                        v = scan(
                            rv(MR), rv(AL_), rv(AL_), sm[:, r, 2:3], ALU.max, ALU.max, v, mi)
                        rowm[r] = v
                        a2 = act(WI, MR, ACT.Exp, v, mi, prevc, scale=-1.0, bias=sm[:, r, 2:3])
                        v = tt(EM, BL_, MR, ALU.add, v, a)
                        a3 = act(EM, EM, ACT.Exp, v, scale=-1.0)
                        return r, (WK, AL_, WI, EM), [a, a2, a3]

                    def rows_out(r, four, marks):
                        b, fr = bank()
                        PE.wait(fr, marks)
                        for n, row in enumerate(four):
                            for t in range(2):
                                p = tr(
                                    b[:, (n * 2 + t) * 8:(n * 2 + t) * 8 + 8], row[:, t * 128:t * 128 + 128],
                                    ident[0:8, 0:8])
                        v = cp(cols[:, r, :, :].rearrange("p a h -> p (a h)"),
                                                                    b[:, 0:64], p, fz)
                        release(b, v)
                        cm.append([v, p])
                    pend = rows(0)
                    nwr = gr[0:8, 0:128]
                    mnw = mload(nwr, A["ml_norm_w_2"][0].rearrange("(r p) -> r p", p=128), grf)
                    proj_tok((HH, HL), 8, [0, 1, 2, 3], 1, evv, hm, first=1)
                    rows_out(*pend)
                    b, fr = bank()
                    p = tr(b[:, 0:8], nwr, ident[0:8, 0:8], fr, mnw)
                    nwm = cp(nwc[:], b[:, 0:8], p, fz)
                    release(b, nwm)
                    pend = rows(1)
                    proj_feat(2, (HH, HL), 256, 512, evq, hm)
                    rows_out(*pend)
                    proj_feat(2, (HH, HL), 256, 512, evkt, hm)
                    Cm = {}
                    prev = None
                    for r in range(2):
                        kw = []
                        for t in range(2):
                            kw.append(tt(KW[:, t, :].rearrange("p (h n) -> p h n", h=8),
                                         KC[:, t, :].rearrange("p (h n) -> p h n", h=8),
                                         cols[:, r, t, :].unsqueeze(2).to_broadcast([128, 8, 64]), ALU.mult,
                                         km[t], cm[r], prev, fz))
                        for g2 in range(2):
                            b, fr = bank()
                            PE.wait(fr, kw, on2, list(vm.values()))
                            for pi in range(2):
                                for par in range(2):
                                    h = (g2 * 2 + pi) * 2 + par
                                    for t in range(2):
                                        p = mm(b[par * 64:par * 64 + 64, pi * 129:pi * 129 + 129],
                                               KW[:, t, h * 64:h * 64 + 64], VCe[:, t, h, :], t == 0, t == 1, inc=True)
                            Cm[(r, g2)] = copy_out(C[:, r, g2 * 2:g2 * 2 + 2, :],
                                                   b[:, 0:258].rearrange("p (h n) -> p h n", h=2), p, fz)
                            release(b, Cm[(r, g2)])
                        prev = p
                    fz2 = fence()
                with ExitStack() as s2:
                    DD = [sb(f"m_D{i}", [128, 2, 256], F32, s2) for i in range(2)]
                    SS = [sb(f"m_S{i}", [128, 2, 256], F32, s2) for i in range(2)]
                    s3 = s2.enter_context(ExitStack())
                    TI = [sb(f"m_T{i}", [128, 2, 129], F32, s3) for i in range(2)]
                    dfree, sfree2, tfree = [[fz2], [fz2]], [[fz2], [fz2]], [[fz2], [fz2]]
                    am = {}
                    steps = [(h, r) for h in range(8) for r in range(2)]
                    sbk = {}

                    def front(h, r):
                        base = (h % 2) * 64
                        pr = h // 2
                        i = (h * 2 + r) % 2
                        if r == 0:
                            b, fr = bank()
                            PE.wait(fr, qm[pr], ktm[pr])
                            for s_ in range(2):
                                p = mm(b[:, s_ * 256:s_ * 256 + 256], kT[base:base + 64, pr, s_ * 128:s_ * 128 + 128],
                                       qT[base:base + 64, pr, :], True, True, inc=True)
                            sbk[h] = (b, p)
                        b, fr = bank()
                        p = mm(b[:, 0:256], sel[:, h, :], M[:, r, :], True, True, (fr, rowm[r], msl), inc=True)
                        v = stt(DD[i][:], b[:, 0:256].unsqueeze(1).to_broadcast([128, 2, 256]), -1.0, msk[:, r, :, :],
                                ALU.mult, ALU.add, p, mmk, dfree[i])
                        release(b, v)
                        for s_ in range(2):
                            a = act(DD[i][:, s_, :], DD[i][:, s_, :], ACT.Exp, v, cm[r][0],
                                    bias=cols[:, r, 2 + s_, h:h + 1])
                        sb_, sp_ = sbk[h]
                        v = tt(SS[i][:], sb_[:, :].rearrange("p (s n) -> p s n", s=2), DD[i][:], ALU.mult, a, sp_,
                               sfree2[i])
                        dfree[i] = [v]
                        if r == 1:
                            release(sb_, v)
                        return v

                    def back(h, r, v):
                        base = (h % 2) * 64
                        pr = h // 2
                        i = (h * 2 + r) % 2
                        b1, fr1 = bank()
                        b2, fr2 = bank()
                        PE.wait(fr1, fr2, v, on, vm[(2, h // 4)], vm[(3, h // 4)], Cm[(r, pr // 2)])
                        for t in range(2):
                            p2 = mm(b2[:, t * 129:t * 129 + 129], qT[base:base + 64, pr, t * 128:t * 128 + 128],
                                    C[base:base + 64, r, pr, :], True, True, inc=True)
                        for t in range(2):
                            ss_ = [q for q in range(2) if (q <= t if r == 0 else q >= t)]
                            for n, q in enumerate(ss_):
                                p1 = mm(b1[:, t * 129:t * 129 + 129], SS[i][:, q, t * 128:t * 128 + 128],
                                        VLe[:, q, h, :], n == 0, n == len(ss_) - 1, inc=True)
                        for t in range(2):
                            a = act(TI[i][:, t, :], b2[:, t * 129:t * 129 + 129], ACT.Copy, p2, tfree[i], cm[r][0],
                                    scale=cols[:, r, 4 + t, h:h + 1])
                        release(b2, a)
                        sfree2[i] = [p1]
                        v = tt(ac_[r][:, :, h, :], b1[:, 0:258].rearrange("p (t n) -> p t n", t=2), TI[i][:], ALU.add,
                               p1, a, fz)
                        release(b1, v)
                        tfree[i] = [v]
                        am[(h, r)] = v

                    pend = None
                    for h, r in steps:
                        v = front(h, r)
                        if pend is not None:
                            back(*pend)
                        pend = (h, r, v)
                    back(*pend)
                    s3.close()
                    den = sb("m_den", [128, 2, 16], F32, s2)
                    fz2 = fence()
                    attn_done = [PE.last(), DV.last()]
                    OH = sb("m_oh", [128, 8, 256], F32R, s2)
                    so = [(DD + SS)[n // 2][:, n % 2, :] for n in range(8)]
                    OL = sb("m_ol", [128, 8, 256], F32R, s2)
                    som = {}

                    def evo(n, b, p):
                        t1, tf, ti = tmp()
                        a = act(t1[:, 0:256], b[:, 0:256], ACT.Exp, p, tf, scale=-1.0)
                        release(b, a)
                        a = act(t1[:, 0:256], t1[:, 0:256], ACT.Ln, a, bias=ones[:, 0:1])
                        a = act(so[n], t1[:, 0:256], ACT.Exp, a, attn_done, scale=-1.0)
                        tmp_free[ti] = [a]
                        som[n] = a

                    proj_feat(1, (HH, HL), 256, 512, evo, hm)
                    m2 = {}
                    for r in range(2):
                        dv = den[:, r, :].rearrange("p (t h) -> p t h", t=2)
                        m = stt(dv, ac_[r][:, :, :, 128], -1.0, ac_[r][:, :, :, 128], ALU.mult, ALU.max, am[(7, r)], fz2)
                        m = tt(dv, dv, cols[:, r, 6:8, :], ALU.max, m)
                        m = rcp(den[:, r, :], den[:, r, :], m)
                        for t in range(2):
                            o = ac_[r][:, t, :, 0:128]
                            m2[t] = tt(o, o, den[:, r, t * 8:t * 8 + 8].unsqueeze(2).to_broadcast([128, 8, 128]),
                                       ALU.mult, m, q=PO if t else DV)
                    proj_feat(1, (HH, HL), 256, 512, shifted(evo, 2), hm)
                    hsm = []
                    for t in range(2):
                        o = ac_[0][:, t, :, 0:128]
                        hsm.append(tt(o, o, ac_[1][:, t, :, 0:128], ALU.add, m2[t], q=PO if t else DV))
                    s = stats()
                    for t in range(2):
                        sq = ac_[1][:, t, :, 0:128]
                        o = ac_[0][:, t, :, 0:128]
                        m = tt(sq, o, o, ALU.mult, hsm[t], q=PO if t else DV)
                        m = rsum(s[:, 0, t * 8:t * 8 + 8], sq, AX.X, m)
                    proj_feat(1, (HH, HL), 256, 512, shifted(evo, 4), hm)
                    r_, rm = rstd(s, 16, 128, [m])
                    hz = []
                    for t in range(2):
                        o = ac_[0][:, t, :, 0:128]
                        hz.append(tt(o, o, r_[:, t * 8:t * 8 + 8].unsqueeze(2).to_broadcast([128, 8, 128]), ALU.mult,
                                     rm, hsm[t], q=PO if t else DV))
                    proj_feat(1, (HH, HL), 256, 512, shifted(evo, 6), hm)
                    om = []
                    for fp in range(4):
                        b, fr = bank()
                        PE.wait(fr, hz)
                        for k in range(2):
                            f = fp * 2 + k
                            for t in range(2):
                                p = tr(b[:, k * 256 + t * 128:k * 256 + t * 128 + 128], ac_[0][:, t, f, 0:128], ident[:])
                        t1, tf, ti = tmp()
                        for k in range(2):
                            f = fp * 2 + k
                            v = stt(t1[:, k * 256:k * 256 + 256], b[:, k * 256:k * 256 + 256], nwc[:, f:f + 1],
                                    so[f], ALU.mult, ALU.mult, p, tf, nwm, som[f])
                        release(b, v)
                        m = hi_lo(OH[:, fp * 2:fp * 2 + 2, :], OL[:, fp * 2:fp * 2 + 2, :],
                                  t1[:, :].rearrange("p (k n) -> p k n", k=2), v, attn_done)
                        tmp_free[ti] = m
                        om.append(m)
                    fz4 = fence()
            ym = {}
            return proj_last((OH, OL), [2, 3], y_evac_for(ym, fz4), lambda kt: om[kt // 2], off=2), ym

        mixers = [mla, gla, conv, mlstm]
        allow.update({(0, 0), (0, 1)})
        LAG[0] = 1 << 20
        while bg[0][0] in allow:
            step_bg()
        LAG[0] = 3
        for c in closing:
            c[0] = 3
        parts = [direct(0, 0), direct(1, 4)]
        xm = {t: d_x[t] for t in range(4)}
        dg = {}
        prep([0, 1], xm, dg, fence_mark)
        prep([2, 3], xm, dg)
        ensure((0, 0))
        direct_out(0, *parts[0])
        ensure((0, 1))
        direct_out(1, *parts[1])
        H = Hidden(0, 0, dg, xm)
        H.make(0)
        H.make(1)
        allow.update((0, part) for part in (3, 4, 2))
        for li in range(4):
            RATE[0] = 0.9 if li == 0 else 0.6
            both = LAYERS[li]["both"]
            tiles = [0, 1, 2, 3] if both else [2, 3]
            needed[:] = [(li, 2)]
            allow.update((li, part) for part in (3, 4))
            with ExitStack() as ls:
                pend, ym = mixers[li](li, H, ls)
                if li == 1:
                    fx = fence()
                    for t in range(2):
                        xm[t] = mload(X[:, t, :], A["ctx_2"][t * 128:t * 128 + 128, :], fx)
                H = transition(li, 2, tiles, pend, ym, xm, dg, (li, 1, both), [(li, 5)])
            RATE[0] = 0.6
            if li < 3:
                allow.update((li + 1, part) for part in (0, 1, 3, 4))
            if li == 1:
                H.rest()
                prep([0, 1], xm, dg, fence())
            needed[:] = [(li, 5)] + ([(li + 1, 0), (li + 1, 1)] if li < 3 else [])
            if li == 1:
                def ahead():
                    early_h.append(Hidden(2, 0, dg, xm))
                    early_h[0].make(0)

                early.append(ahead)
            with ExitStack() as ls:
                pend, ym = mlp(li, tiles, H, ls)
                H = transition(li, 5, tiles, pend, ym, xm, dg, (li + 1, 0, True) if li < 3 else None, [(li + 1, 2)])
        assert w_at[0] == len(WL) and not bg and not closing
        outs = []
        for t in range(2):
            outs.append(mload(out[t * 128:t * 128 + 128, :], X[:, 2 + t, :], xm[2 + t], q=SP))
        SP.wait(*outs)

        block = ctx.enter_context(nc.Block())

        @block.sync
        def _(e):
            SP.play(e)

        @block.gpsimd
        def _(e):
            PO.play(e)

        @block.scalar
        def _(e):
            AC.play(e)

        @block.vector
        def _(e):
            DV.play(e)

        @block.tensor
        def _(e):
            PE.play(e)


_INS = ['x', 'c', 'ctx', 'c_ctx', 'ada_w', 'ada_b', 'norm_g', 'mlp_w1', 'mlp_w2', 'mla_w_dq', 'mla_g_q', 'mla_w_uq',
        'mla_w_dkv', 'mla_g_kv', 'mla_w_ukv', 'mla_w_o', 'gla_w_q', 'gla_w_k', 'gla_w_v', 'gla_w_r', 'gla_w_gate1',
        'gla_w_gate2', 'gla_b_gate', 'gla_g_o', 'gla_w_o', 'c_2', 'ctx_2', 'c_ctx_2', 'norm_w_2', 'mod_w_2', 'mod_b_2',
        'mlp_w1_2', 'mlp_w2_2', 'conv_w_in_2', 'conv_w_2', 'conv_w_out_2', 'ml_w_qkvo_2', 'ml_w_if_2', 'ml_b_if_2',
        'ml_norm_w_2', 'ml_w_out_2']


def kernel(**inputs):
    import numpy as _np
    import concourse.bacc as _bacc
    from concourse import mybir as _mybir
    from concourse.bass_utils import run_bass_kernel_spmd as _run

    nc = _bacc.Bacc("TRN2", target_bir_lowering=False, num_devices=1)
    arrays, aps = {}, {}
    for name in _INS:
        a = _np.ascontiguousarray(inputs[name])
        if name in ("x", "ctx", "ctx_2"):
            a = a.reshape(256, 1024)
        if name in ("c", "c_ctx", "c_2", "c_ctx_2"):
            a = a.reshape(8, 128)
        arrays[f"in_{name}"] = a
        aps[name] = nc.dram_tensor(f"in_{name}", a.shape, _mybir.dt.from_np(a.dtype), kind="ExternalInput").ap()
    arrays["in_consts"] = CONSTS
    aps["consts"] = nc.dram_tensor("in_consts", CONSTS.shape, _mybir.dt.float32, kind="ExternalInput").ap()
    o = nc.dram_tensor("out_0", (256, 1024), _mybir.dt.float32, kind="ExternalOutput").ap()
    build(nc, aps, o)
    r = _run(nc, [arrays], core_ids=[0])
    return r.results[0]["out_0"].reshape(1, 256, 1024)
```
